# Optimizing a Trainium2 kernel written in Bass

```python
import math
import jax, jax.numpy as jnp
from jax import lax
import numpy as np

D_MODEL = 1024
BATCH = 1
SEQ = 256
DEPTH = 1

NSA_WIDTH = D_MODEL // 2
POOL_WIDTH = D_MODEL // 4
SGU_WIDTH = D_MODEL // 4
MIX_WIDTH = NSA_WIDTH + POOL_WIDTH + SGU_WIDTH

NSA_HEADS = 8
NSA_KV_GROUPS = 2
HEADS_PER_GROUP = NSA_HEADS // NSA_KV_GROUPS
HEAD_DIM = NSA_WIDTH // NSA_HEADS
KV_WIDTH = NSA_KV_GROUPS * HEAD_DIM
GATE_WIDTH = NSA_HEADS * 3
CMP_STRIDE = 16
CMP_LEN = 2 * CMP_STRIDE
CMP_HIDDEN = 2 * HEAD_DIM
SEL_BLOCK = 64
SEL_TOPK = 16
N_LOCAL_SEL = 2
SEL_RATIO = SEL_BLOCK // CMP_STRIDE
SEL_AGG = (1.0, 2.0, 2.0, 2.0, 1.0)
FORCE_SCORE = 1e9
WINDOW = 512
Q_BLOCK = 128

REL_BUCKETS = 32
REL_MAX_DIST = 1024

POOL_WINDOWS = (2, 4, 8, 16)
POOL_GROUPS = len(POOL_WINDOWS)
POOL_CH = POOL_WIDTH // POOL_GROUPS

SGU_GROUPS = 4
SGU_CH = SGU_WIDTH // SGU_GROUPS
SGU_CHUNK = 128

IN_WIDTHS = (NSA_WIDTH, KV_WIDTH, KV_WIDTH, KV_WIDTH, KV_WIDTH, KV_WIDTH, KV_WIDTH,
             GATE_WIDTH, POOL_WIDTH, SGU_WIDTH, SGU_WIDTH)
IN_WIDTH = sum(IN_WIDTHS)
IN_SPLITS = tuple(int(s) for s in np.cumsum(IN_WIDTHS)[:-1])

MEM_LEN = 256
MEM_HEADS = 4
MEM_HEAD_DIM = D_MODEL // MEM_HEADS

FFN_HIDDEN = ((11 * D_MODEL // 4) // 128) * 128
CONV_WIDTH = 3

EPS = 1e-6
F32 = jnp.float32


def rms_norm(x, g):
    xf = x.astype(F32)
    y = xf * lax.rsqrt(jnp.mean(xf * xf, axis=-1, keepdims=True) + EPS)
    return (y * g.astype(F32)).astype(x.dtype)

def layer_norm(x, g, b):
    xf = x.astype(F32)
    mu = jnp.mean(xf, axis=-1, keepdims=True)
    var = jnp.mean(jnp.square(xf - mu), axis=-1, keepdims=True)
    return ((xf - mu) * lax.rsqrt(var + EPS) * g.astype(F32) + b.astype(F32)).astype(x.dtype)

def t5_bucket(dist):
    n = jnp.maximum(dist, 0)
    max_exact = REL_BUCKETS // 2
    nf = jnp.maximum(n, 1).astype(F32)
    large = max_exact + (jnp.log(nf / max_exact) / math.log(REL_MAX_DIST / max_exact)
                         * (REL_BUCKETS - max_exact)).astype(jnp.int32)
    large = jnp.minimum(large, REL_BUCKETS - 1)
    return jnp.where(n < max_exact, n, large)

def masked_softmax(s, mask):
    s = jnp.where(mask, s.astype(F32), -jnp.inf)
    m = jnp.max(s, axis=-1, keepdims=True)
    m = jnp.where(jnp.isfinite(m), m, 0.0)
    e = jnp.where(mask, jnp.exp(s - m), 0.0)
    return e / jnp.maximum(jnp.sum(e, axis=-1, keepdims=True), 1.0)

def compress(kv, pos, w1, b1, w2, b2):
    B, S, G, dk = kv.shape
    r = kv.reshape(B, S // CMP_STRIDE, CMP_STRIDE, G, dk)
    blocks = jnp.concatenate([r[:, :-1], r[:, 1:]], axis=2) + pos[None, None, :, None, :]
    h = jax.nn.gelu(jnp.einsum('bclgd,ldh->bcgh', blocks, w1) + b1)
    return jnp.einsum('bcgh,hd->bcgd', h, w2) + b2

def nsa_mixer(q, k_cmp, v_cmp, k_sel, v_sel, k_win, v_win, gates, rel_bias,
              cmp_pos, cmp_w1, cmp_b1, cmp_w2, cmp_b2):
    B, S, G, Hg, dk = q.shape
    scale = dk ** -0.5
    kc = compress(k_cmp, cmp_pos[0], cmp_w1[0], cmp_b1[0], cmp_w2[0], cmp_b2[0])
    vc = compress(v_cmp, cmp_pos[1], cmp_w1[1], cmp_b1[1], cmp_w2[1], cmp_b2[1])
    NC = kc.shape[1]
    NS = S // SEL_BLOCK
    topk = min(SEL_TOPK, NS)
    ksb = jnp.transpose(k_sel.reshape(B, NS, SEL_BLOCK, G, dk), (0, 3, 1, 2, 4))
    vsb = jnp.transpose(v_sel.reshape(B, NS, SEL_BLOCK, G, dk), (0, 3, 1, 2, 4))
    kwp = jnp.pad(k_win, ((0, 0), (WINDOW, 0), (0, 0), (0, 0)))
    vwp = jnp.pad(v_win, ((0, 0), (WINDOW, 0), (0, 0), (0, 0)))
    cmp_end = jnp.arange(NC) * CMP_STRIDE + CMP_LEN - 1
    sel_start = jnp.arange(NS) * SEL_BLOCK
    jj = jnp.arange(NS)
    bias_g = jnp.transpose(rel_bias.reshape(REL_BUCKETS, G, Hg), (1, 0, 2))
    gidx = jnp.arange(G)
    bidx = jnp.arange(B)
    ti = jnp.arange(Q_BLOCK)
    wj = jnp.arange(Q_BLOCK + WINDOW)
    wdist = ti[:, None] + WINDOW - wj[None, :]
    win_band = (wdist >= 0) & (wdist < WINDOW)
    win_bias = jnp.transpose(rel_bias[t5_bucket(wdist)].reshape(Q_BLOCK, Q_BLOCK + WINDOW, G, Hg), (2, 3, 0, 1))
    nblk = S // Q_BLOCK
    qb = jnp.moveaxis(q.reshape(B, nblk, Q_BLOCK, G, Hg, dk), 1, 0)
    gb = jnp.moveaxis(gates.reshape(B, nblk, Q_BLOCK, G, Hg, 3), 1, 0)

    def block(args):
        qi, gi, i = args
        s0 = i * Q_BLOCK
        t = s0 + ti
        qs = qi * scale
        sc = jnp.einsum('btghd,bcgd->bghtc', qs, kc)
        cdist = t[:, None] - cmp_end[None, :]
        cbias = jnp.transpose(rel_bias[t5_bucket(cdist)].reshape(Q_BLOCK, NC, G, Hg), (2, 3, 0, 1))
        pc = masked_softmax(sc + cbias, cdist >= 0)
        o_cmp = jnp.einsum('bghtc,bcgd->btghd', pc.astype(vc.dtype), vc)
        imp = jnp.pad(jnp.sum(pc, axis=2), ((0, 0), (0, 0), (0, 0), (1, 1)))
        p_sel = sum(w * imp[..., m:m + SEL_RATIO * NS:SEL_RATIO] for m, w in enumerate(SEL_AGG))
        blk_q = t // SEL_BLOCK
        rel_blk = blk_q[:, None] - jj[None, :]
        svalid = sel_start[None, :] <= t[:, None]
        forced = (jj[None, :] == 0) | ((rel_blk >= 0) & (rel_blk < N_LOCAL_SEL))
        score = jnp.where(forced, FORCE_SCORE, jnp.where(svalid, p_sel, -1.0))
        _, sidx = lax.top_k(score, topk)
        ks = ksb[bidx[:, None, None, None], gidx[None, :, None, None], sidx]
        vs = vsb[bidx[:, None, None, None], gidx[None, :, None, None], sidx]
        spos = sidx[..., None] * SEL_BLOCK + jnp.arange(SEL_BLOCK)
        sdist = t[None, None, :, None, None] - spos
        sbias = bias_g[gidx[None, :, None, None, None], t5_bucket(sdist)]
        ss = jnp.einsum('btghd,bgtkld->bghtkl', qs, ks) + jnp.transpose(sbias, (0, 1, 5, 2, 3, 4))
        nsel = topk * SEL_BLOCK
        ps = masked_softmax(ss.reshape(B, G, Hg, Q_BLOCK, nsel), (sdist >= 0).reshape(B, G, 1, Q_BLOCK, nsel))
        o_sel = jnp.einsum('bghtn,bgtnd->btghd', ps.astype(vs.dtype), vs.reshape(B, G, Q_BLOCK, nsel, dk))
        kw = lax.dynamic_slice_in_dim(kwp, s0, Q_BLOCK + WINDOW, axis=1)
        vw = lax.dynamic_slice_in_dim(vwp, s0, Q_BLOCK + WINDOW, axis=1)
        wpos = s0 - WINDOW + wj
        sw = jnp.einsum('btghd,bsgd->bghts', qs, kw) + win_bias
        pw = masked_softmax(sw, win_band & (wpos >= 0)[None, :])
        o_win = jnp.einsum('bghts,bsgd->btghd', pw.astype(vw.dtype), vw)
        return gi[..., 0:1] * o_cmp + gi[..., 1:2] * o_sel + gi[..., 2:3] * o_win

    out = lax.map(block, (qb, gb, jnp.arange(nblk)))
    return jnp.moveaxis(out, 0, 1).reshape(B, S, G * Hg * dk)

def pool_mixer(p, w, scale):
    B, S, C = p.shape
    pf = p.astype(F32)
    cs = jnp.pad(jnp.cumsum(pf, axis=1), ((0, 0), (1, 0), (0, 0)))
    t = jnp.arange(S)
    outs = []
    for gi, win in enumerate(POOL_WINDOWS):
        seg = cs[:, :, gi * POOL_CH:(gi + 1) * POOL_CH]
        lo = jnp.maximum(t + 1 - win, 0)
        cnt = jnp.minimum(t + 1, win).astype(F32)
        outs.append((seg[:, 1:] - seg[:, lo]) / cnt[None, :, None] - pf[:, :, gi * POOL_CH:(gi + 1) * POOL_CH])
    d = jnp.stack(outs, axis=2).astype(p.dtype)
    return jnp.einsum('bsgc,gcd->bsgd', d, w).reshape(B, S, C) * scale

def sgu_mixer(u, v, norm_g, norm_b, w_s, b_s):
    B, S, C = u.shape
    u = jax.nn.gelu(u)
    v = layer_norm(jax.nn.gelu(v), norm_g, norm_b)
    vc = v.reshape(B, S // SGU_CHUNK, SGU_CHUNK, SGU_GROUPS, SGU_CH)
    causal = jnp.tril(jnp.ones((SGU_CHUNK, SGU_CHUNK), dtype=bool))
    ws = jnp.where(causal, w_s, 0.0)
    mixed = jnp.einsum('hts,bnshc->bnthc', ws, vc) + jnp.transpose(b_s)[:, :, None]
    return u * mixed.reshape(B, S, C)

def memory_attention(h, mem_n, wq, wk, wv, wo):
    B, S, D = h.shape
    M = mem_n.shape[1]
    q = (h @ wq).reshape(B, S, MEM_HEADS, MEM_HEAD_DIM)
    k = (mem_n @ wk).reshape(B, M, MEM_HEADS, MEM_HEAD_DIM)
    v = (mem_n @ wv).reshape(B, M, MEM_HEADS, MEM_HEAD_DIM)
    s = jnp.einsum('bshd,bmhd->bhsm', q, k).astype(F32) * (MEM_HEAD_DIM ** -0.5)
    p = jax.nn.softmax(s, axis=-1).astype(v.dtype)
    return jnp.einsum('bhsm,bmhd->bshd', p, v).reshape(B, S, D) @ wo

def conv_ffn(h, w_up, conv_w, conv_b, w_down):
    a = h @ w_up
    a = lax.conv_general_dilated(a, conv_w[:, None, :], window_strides=(1,),
                                 padding=[(CONV_WIDTH - 1, 0)],
                                 dimension_numbers=('NWC', 'WIO', 'NWC'),
                                 feature_group_count=a.shape[-1]) + conv_b
    gate, val = jnp.split(a, 2, axis=-1)
    return (jax.nn.gelu(gate) * val) @ w_down

def first_inputs(seed: int = 0) -> dict:
    key = jax.random.key(seed)
    ks = iter(jax.random.split(key, 40))

    def nrm(shape, scale):
        return jax.random.normal(next(ks), shape, F32) * scale

    def gain(shape):
        return 1.0 + 0.1 * jax.random.normal(next(ks), shape, F32)

    L, D, H2 = DEPTH, D_MODEL, 2 * FFN_HIDDEN
    return {
        'x': nrm((BATCH, SEQ, D), 1.0),
        'mem': nrm((BATCH, MEM_LEN, D), 1.0),
        'rel_bias': nrm((REL_BUCKETS, NSA_HEADS), 0.2),
        'mix_norm_pre': gain((L, D)),
        'mix_norm_post': gain((L, D)),
        'w_in': nrm((L, D, IN_WIDTH), D ** -0.5),
        'cmp_pos': nrm((L, 2, CMP_LEN, HEAD_DIM), 0.1),
        'cmp_w1': nrm((L, 2, CMP_LEN, HEAD_DIM, CMP_HIDDEN), (CMP_LEN * HEAD_DIM) ** -0.5),
        'cmp_b1': nrm((L, 2, CMP_HIDDEN), 0.01),
        'cmp_w2': nrm((L, 2, CMP_HIDDEN, HEAD_DIM), CMP_HIDDEN ** -0.5),
        'cmp_b2': nrm((L, 2, HEAD_DIM), 0.01),
        'pool_w': nrm((L, POOL_GROUPS, POOL_CH, POOL_CH), POOL_CH ** -0.5),
        'pool_scale': gain((L, POOL_WIDTH)),
        'sgu_norm_g': gain((L, SGU_WIDTH)),
        'sgu_norm_b': nrm((L, SGU_WIDTH), 0.01),
        'sgu_w': nrm((L, SGU_GROUPS, SGU_CHUNK, SGU_CHUNK), SGU_CHUNK ** -0.5),
        'sgu_b': gain((L, SGU_GROUPS, SGU_CHUNK)),
        'w_out': nrm((L, MIX_WIDTH, D), MIX_WIDTH ** -0.5),
        'mem_norm_pre': gain((L, D)),
        'mem_norm_kv': gain((L, D)),
        'mem_norm_post': gain((L, D)),
        'w_mq': nrm((L, D, D), D ** -0.5),
        'w_mk': nrm((L, D, D), D ** -0.5),
        'w_mv': nrm((L, D, D), D ** -0.5),
        'w_mo': nrm((L, D, D), D ** -0.5),
        'ffn_norm_pre': gain((L, D)),
        'ffn_norm_post': gain((L, D)),
        'w_up': nrm((L, D, H2), D ** -0.5),
        'conv_w': nrm((L, CONV_WIDTH, H2), CONV_WIDTH ** -0.5),
        'conv_b': nrm((L, H2), 0.01),
        'w_down': nrm((L, FFN_HIDDEN, D), FFN_HIDDEN ** -0.5),
    }

def first_block(x, mem, rel_bias, mix_norm_pre, mix_norm_post, w_in, cmp_pos, cmp_w1, cmp_b1,
              cmp_w2, cmp_b2, pool_w, pool_scale, sgu_norm_g, sgu_norm_b, sgu_w, sgu_b, w_out,
              mem_norm_pre, mem_norm_kv, mem_norm_post, w_mq, w_mk, w_mv, w_mo,
              ffn_norm_pre, ffn_norm_post, w_up, conv_w, conv_b, w_down):
    B, S, D = x.shape
    G, Hg, dk = NSA_KV_GROUPS, HEADS_PER_GROUP, HEAD_DIM
    for l in range(DEPTH):
        h = rms_norm(x, mix_norm_pre[l])
        proj = h @ w_in[l]
        q, kc, vc, ksl, vsl, kw, vw, gt, pin, u, v = jnp.split(proj, IN_SPLITS, axis=-1)
        gates = jax.nn.sigmoid(gt.astype(F32)).astype(x.dtype).reshape(B, S, G, Hg, 3)
        kv = lambda a: a.reshape(B, S, G, dk)
        out_a = nsa_mixer(q.reshape(B, S, G, Hg, dk), kv(kc), kv(vc), kv(ksl), kv(vsl), kv(kw), kv(vw),
                          gates, rel_bias, cmp_pos[l], cmp_w1[l], cmp_b1[l], cmp_w2[l], cmp_b2[l])
        out_b = pool_mixer(pin, pool_w[l], pool_scale[l])
        out_c = sgu_mixer(u, v, sgu_norm_g[l], sgu_norm_b[l], sgu_w[l], sgu_b[l])
        mix = jnp.concatenate([out_a, out_b, out_c], axis=-1) @ w_out[l]
        x = x + rms_norm(mix, mix_norm_post[l])
        h = rms_norm(x, mem_norm_pre[l])
        m = rms_norm(mem, mem_norm_kv[l])
        x = x + rms_norm(memory_attention(h, m, w_mq[l], w_mk[l], w_mv[l], w_mo[l]), mem_norm_post[l])
        h = rms_norm(x, ffn_norm_pre[l])
        x = x + rms_norm(conv_ffn(h, w_up[l], conv_w[l], conv_b[l], w_down[l]), ffn_norm_post[l])
    return x


DEPTH_2 = 2

N_MIXERS = 2
N_A = (DEPTH_2 + 1) // 2
N_B = DEPTH_2 // 2
N_META = 16
EXPAND = 2
E_CONV = EXPAND * D_MODEL
E_MLSTM = EXPAND * D_MODEL
N_HEADS = 4
DV = E_MLSTM // N_HEADS
DK = DV // 2
QK = N_HEADS * DK
CHUNK = 64
RMS_EPS = 1e-6


def _rmsnorm(x, w):
    xf = x.astype(jnp.float32)
    y = xf * lax.rsqrt(jnp.mean(xf * xf, axis=-1, keepdims=True) + RMS_EPS)
    return (y * w.astype(jnp.float32)).astype(x.dtype)

def _short_conv_mixer(u, w_in, w_conv, w_out):
    proj = u @ w_in
    b_gate, c_gate, xin, z = jnp.split(proj, 4, axis=-1)
    y = lax.conv_general_dilated(
        c_gate * xin, w_conv[:, None, :].astype(u.dtype),
        window_strides=(1,), padding=[(CONV_WIDTH - 1, 0)],
        dimension_numbers=("NWC", "WIO", "NWC"), feature_group_count=E_CONV)
    return (jax.nn.silu(z) * b_gate * y) @ w_out

def _mlstm_chunk(carry, inp):
    c_state, n_state, m_state = carry
    q, k, v, logi, logf = inp
    L = q.shape[-2]
    b = jnp.cumsum(logf, axis=-1)
    causal = jnp.tril(jnp.ones((L, L), dtype=bool))
    log_d = jnp.where(causal, b[..., :, None] - b[..., None, :] + logi[..., None, :], -jnp.inf)
    log_inter = b + m_state[..., None]
    m_row = jnp.maximum(log_inter, jnp.max(log_d, axis=-1))
    d = jnp.exp(log_d - m_row[..., None])
    inter = jnp.exp(log_inter - m_row)
    s = jnp.einsum("bhtd,bhsd->bhts", q, k) * d
    num = jnp.einsum("bhts,bhsv->bhtv", s, v) + inter[..., None] * jnp.einsum("bhtd,bhdv->bhtv", q, c_state)
    den = jnp.sum(s, axis=-1) + inter * jnp.einsum("bhtd,bhd->bht", q, n_state)
    h = num / jnp.maximum(jnp.abs(den), jnp.exp(-m_row))[..., None]
    log_w = b[..., -1:] - b + logi
    m_new = jnp.maximum(b[..., -1] + m_state, jnp.max(log_w, axis=-1))
    decay = jnp.exp(b[..., -1] + m_state - m_new)
    w = jnp.exp(log_w - m_new[..., None])
    c_new = decay[..., None, None] * c_state + jnp.einsum("bhs,bhsd,bhsv->bhdv", w, k, v)
    n_new = decay[..., None] * n_state + jnp.einsum("bhs,bhsd->bhd", w, k)
    return (c_new, n_new, m_new), h

def _mlstm_mixer(u, w_in, gate_b, head_norm_w, w_out):
    bsz, T, _ = u.shape
    proj = u @ w_in
    q, k, v, o, z, g = jnp.split(
        proj, [QK, 2 * QK, 2 * QK + E_MLSTM, 2 * QK + 2 * E_MLSTM, 2 * QK + 3 * E_MLSTM], axis=-1)
    g = g.astype(jnp.float32) + gate_b.astype(jnp.float32)
    logi = jnp.transpose(g[..., :N_HEADS], (0, 2, 1))
    logf = jnp.transpose(jax.nn.log_sigmoid(g[..., N_HEADS:]), (0, 2, 1))

    def heads(a, dh):
        return a.astype(jnp.float32).reshape(bsz, T, N_HEADS, dh).transpose(0, 2, 1, 3)

    q = heads(q, DK) * (DK ** -0.5)
    k = heads(k, DK)
    v = heads(v, DV)
    seqs = (q, k, v, logi, logf)

    def chunks(a):
        real = a[:, :, N_META:]
        nc = real.shape[2] // CHUNK
        return jnp.moveaxis(real.reshape(bsz, N_HEADS, nc, CHUNK, *real.shape[3:]), 2, 0)

    carry0 = (jnp.zeros((bsz, N_HEADS, DK, DV), jnp.float32),
              jnp.zeros((bsz, N_HEADS, DK), jnp.float32),
              jnp.zeros((bsz, N_HEADS), jnp.float32))
    carry, h_meta = _mlstm_chunk(carry0, tuple(a[:, :, :N_META] for a in seqs))
    _, h_real = lax.scan(_mlstm_chunk, carry, tuple(chunks(a) for a in seqs))
    h_real = jnp.moveaxis(h_real, 0, 2).reshape(bsz, N_HEADS, T - N_META, DV)
    h = jnp.concatenate([h_meta, h_real], axis=2).transpose(0, 2, 1, 3)
    h = h * lax.rsqrt(jnp.mean(h * h, axis=-1, keepdims=True) + RMS_EPS)
    h = h * head_norm_w.astype(jnp.float32).reshape(N_HEADS, DV)
    h = h.reshape(bsz, T, E_MLSTM).astype(u.dtype) * jax.nn.sigmoid(o) * jax.nn.silu(z)
    return h @ w_out

def second_inputs(seed: int = 0) -> dict:
    key = jax.random.key(seed)
    ks = jax.random.split(key, 12)
    f32 = jnp.float32
    x = jax.random.normal(ks[0], (BATCH, SEQ, D_MODEL), f32)
    meta_tokens = jax.random.normal(ks[1], (N_META, D_MODEL), f32)
    norm_w = 1.0 + 0.05 * jax.random.normal(ks[2], (DEPTH_2, D_MODEL), f32)
    conv_in_w = jax.random.normal(ks[3], (N_A, D_MODEL, 4 * E_CONV), f32) * D_MODEL ** -0.5
    conv_w = jax.random.normal(ks[4], (N_A, CONV_WIDTH, E_CONV), f32) * CONV_WIDTH ** -0.5
    conv_out_w = jax.random.normal(ks[5], (N_A, E_CONV, D_MODEL), f32) * E_CONV ** -0.5
    n_in = 2 * QK + 3 * E_MLSTM + 2 * N_HEADS
    mlstm_in_w = jax.random.normal(ks[6], (N_B, D_MODEL, n_in), f32) * D_MODEL ** -0.5
    i_bias = 0.1 * jax.random.normal(ks[7], (N_B, N_HEADS), f32)
    f_bias = jnp.linspace(3.0, 6.0, N_HEADS, dtype=f32)[None, :] + 0.1 * jax.random.normal(ks[8], (N_B, N_HEADS), f32)
    mlstm_gate_b = jnp.concatenate([i_bias, f_bias], axis=-1)
    mlstm_head_norm_w = 1.0 + 0.05 * jax.random.normal(ks[9], (N_B, E_MLSTM), f32)
    mlstm_out_w = jax.random.normal(ks[10], (N_B, E_MLSTM, D_MODEL), f32) * E_MLSTM ** -0.5
    final_norm_w = 1.0 + 0.05 * jax.random.normal(ks[11], (D_MODEL,), f32)
    return {"x": x, "meta_tokens": meta_tokens, "norm_w": norm_w, "conv_in_w": conv_in_w,
            "conv_w": conv_w, "conv_out_w": conv_out_w, "mlstm_in_w": mlstm_in_w,
            "mlstm_gate_b": mlstm_gate_b, "mlstm_head_norm_w": mlstm_head_norm_w,
            "mlstm_out_w": mlstm_out_w, "final_norm_w": final_norm_w}

def second_block(x, meta_tokens, norm_w, conv_in_w, conv_w, conv_out_w, mlstm_in_w,
              mlstm_gate_b, mlstm_head_norm_w, mlstm_out_w, final_norm_w):
    bsz = x.shape[0]
    meta = jnp.broadcast_to(meta_tokens.astype(x.dtype)[None], (bsz, N_META, D_MODEL))
    h = jnp.concatenate([meta, x], axis=1)
    for i in range(DEPTH_2):
        u = _rmsnorm(h, norm_w[i])
        j = i // N_MIXERS
        if i % N_MIXERS == 0:
            h = h + _short_conv_mixer(u, conv_in_w[j], conv_w[j], conv_out_w[j])
        else:
            h = h + _mlstm_mixer(u, mlstm_in_w[j], mlstm_gate_b[j], mlstm_head_norm_w[j], mlstm_out_w[j])
    h = _rmsnorm(h, final_norm_w)
    return h[:, N_META:]


def setup_inputs(seed=0):
    out = dict(first_inputs(seed))
    for name, value in second_inputs(seed + 1).items():
        if name != "x":
            out[name + "_2"] = value
    return out


def reference(
    x, mem, rel_bias, mix_norm_pre, mix_norm_post, w_in, cmp_pos, cmp_w1, cmp_b1, cmp_w2,
    cmp_b2, pool_w, pool_scale, sgu_norm_g, sgu_norm_b, sgu_w, sgu_b, w_out, mem_norm_pre,
    mem_norm_kv, mem_norm_post, w_mq, w_mk, w_mv, w_mo, ffn_norm_pre, ffn_norm_post, w_up,
    conv_w, conv_b, w_down, meta_tokens_2, norm_w_2, conv_in_w_2, conv_w_2, conv_out_w_2,
    mlstm_in_w_2, mlstm_gate_b_2, mlstm_head_norm_w_2, mlstm_out_w_2, final_norm_w_2,
):
    x = first_block(
        x, mem, rel_bias, mix_norm_pre, mix_norm_post, w_in, cmp_pos, cmp_w1, cmp_b1, cmp_w2,
        cmp_b2, pool_w, pool_scale, sgu_norm_g, sgu_norm_b, sgu_w, sgu_b, w_out, mem_norm_pre,
        mem_norm_kv, mem_norm_post, w_mq, w_mk, w_mv, w_mo, ffn_norm_pre, ffn_norm_post, w_up,
        conv_w, conv_b, w_down,
    )
    return second_block(
        x, meta_tokens_2, norm_w_2, conv_in_w_2, conv_w_2, conv_out_w_2, mlstm_in_w_2,
        mlstm_gate_b_2, mlstm_head_norm_w_2, mlstm_out_w_2, final_norm_w_2,
    )


_drawn_inputs = setup_inputs


def setup_inputs(seed=0):
    import zlib

    import numpy as np

    out = dict(_drawn_inputs(seed))
    spreads = {}
    factors = {'cmp_b1': 8.0,
     'cmp_b2': 8.0,
     'sgu_norm_b': 8.0,
     'conv_b': 6.864,
     'mlstm_head_norm_w_2': 7.432}
    for name, (base, spread) in spreads.items():
        noise = np.random.default_rng([zlib.crc32(name.encode()), seed]).standard_normal(out[name].shape)
        drawn = base * np.exp(spread * noise) if base else spread * noise
        out[name] = __import__('jax').numpy.asarray(drawn.astype(out[name].dtype))
    for name, factor in factors.items():
        out[name] = (out[name] * factor).astype(out[name].dtype)
    return out
```

```python
from contextlib import ExitStack

import concourse.bass as bass
from concourse import mybir

F32 = mybir.dt.float32
F32R = mybir.dt.float32r
ALU = mybir.AluOpType
ACT = mybir.ActivationFunctionType
AX = mybir.AxisListType

P = 128
S = 256
META = 16
T = META + S
D = 1024
KT = D // P
HEADS, GROUPS, HD = 8, 2, 64
NCMP = 15
CSTRIDE = 16
FFN_TILES = 22
E_TILES = 16
MEM_HEADS = 4
LHEADS = 4
EPS = 1e-6
MASKED = -1.0e30

SLOTS = 4
AHEAD = SLOTS - 1
_LAYOUT = [("kc", 1), ("vc", 1), ("sgu_v", 2), ("sgu_u", 2), ("pool", 2), ("cmp", 4), ("vs", 1), ("vw", 1),
           ("ks", 1), ("kw", 1), ("q", 4), ("gates", 1), ("mk", 8), ("mv", 8), ("w_out", 8), ("mq", 8),
           ("mo", 8), ("up", 44), ("down", 24), ("conv_in", 64), ("conv_out", 16), ("lgates", 1), ("lk", 8),
           ("lq", 8), ("lv", 16), ("oz", 32), ("lout", 16)]
CHUNK = {}
NCHUNKS = 0
for _name, _n in _LAYOUT:
    CHUNK[_name] = NCHUNKS
    NCHUNKS += _n
_TILES = dict(cmp=2, down=8, conv_out=8, lout=8)
TILE = {}
_t = 0
for _name, _n in _LAYOUT:
    TILE[_name] = _t
    _t += _TILES.get(_name, _n)

_COLS = [("g_mix_pre", 8), ("g_mix_post", 8), ("g_mem_pre", 8), ("g_mem_kv", 8), ("g_mem_post", 8),
         ("g_ffn_pre", 8), ("g_ffn_post", 8), ("g_conv", 8), ("g_mlstm", 8), ("g_final", 8),
         ("pool_scale", 2), ("cmp_b1", 2), ("cmp_b2k", 1), ("cmp_b2v", 64), ("cmp_pos", 32), ("cmp_w2", 128),
         ("sgu_g", 256), ("sgu_b", 256), ("sgu_bias", 256), ("sgu_w", 512), ("pool_w", 128), ("pool_inv", 512),
         ("ffn_conv", 176), ("conv_taps", 48), ("head_norm", 16), ("gate_b", 1)]
COL = {}
NCOLS = 0
for _name, _n in _COLS:
    COL[_name] = NCOLS
    NCOLS += _n

NORM_X, NORM_MEM, NORM_MIX, NORM_X1, NORM_MEMOUT, NORM_X2, NORM_FFN, NORM_H0, NORM_H1, NORM_FINAL = range(10)
PRE_X, PRE_X1, PRE_X2, PRE_H0, PRE_H1 = range(5)
ACT_MIX, ACT_MEM, ACT_FFN, ACT_CONV, ACT_LSTM = 0, 8, 16, 38, 54


class Chain:

    def __init__(self, eng, sem):
        self.eng, self.sem, self.count = eng, sem, 0

    def note(self, ins):
        ins.then_inc(self.sem, 1)
        self.count += 1
        return ins

    def wait(self):
        self.eng.wait_ge(self.sem, self.count)

    def link(self, ins):
        self.note(ins)
        self.wait()


def build(nc, weights, x_in, mem_in, meta_in, params, rel_bias, onehot, out, bias_rows):
    with ExitStack() as ctx:
        def sb(name, shape, dt=F32):
            return ctx.enter_context(nc.sbuf_tensor(name, shape, dt))

        def sem(name):
            return ctx.enter_context(nc.semaphore(name))

        def psum(name, cols):
            return ctx.enter_context(nc.psum_tensor(name, [P, cols], F32))

        raw = sb("raw", [P, SLOTS, D])
        w_hi = sb("w_hi", [P, SLOTS, D], F32R)
        w_lo = sb("w_lo", [P, SLOTS, D], F32R)
        XR = sb("XR", [P, KT, T])
        XH = sb("XH", [P, KT, T], F32R)
        XL = sb("XL", [P, KT, T], F32R)
        MH = sb("MH", [P, KT, S], F32R)
        ML = sb("ML", [P, KT, S], F32R)
        AH = sb("AH", [P, E_TILES * T], F32R)
        AL = sb("AL", [P, E_TILES * T], F32R)
        cst = sb("cst", [P, NCOLS])
        ident = sb("ident", [P, P])
        ones_d = sb("ones_d", [P, P])
        ones_h = sb("ones_h", [P, P])
        ones_1 = sb("ones_1", [P, P])
        Y = sb("Y", [P, KT, T])
        SQ = sb("SQ", [P, KT, T])
        root = sb("root", [P, T])
        rstd = sb("rstd", [P, T])
        root_m = sb("root_m", [P, T])
        rstd_m = sb("rstd_m", [P, T])
        rb = sb("rb", [33, HEADS])
        sel = sb("sel", [LHEADS, LHEADS, P])
        small = sb("small", [P, 160])
        AR = sb("AR", [P, 12200])

        def col(name, i=0, w=1):
            return cst[:, COL[name] + i:COL[name] + i + w]

        def ar(off, *dims):
            n = 1
            for d in dims:
                n *= d
            v = AR[:, off:off + n]
            if len(dims) == 1:
                return v
            if len(dims) == 2:
                return v.rearrange("p (a b) -> p a b", a=dims[0])
            if len(dims) == 3:
                return v.rearrange("p (a b c) -> p a b c", a=dims[0], b=dims[1])
            return v.rearrange("p (a b c d) -> p a b c d", a=dims[0], b=dims[1], c=dims[2])

        bias = ar(0, HEADS, S)
        Sx = ar(2048, 768)
        PTx = ar(2816, 2, 384)
        RF = ar(2048, 2, 16, 2, NCMP)
        KC2 = ar(3584, 2, GROUPS, S)
        Pc = ar(3584, 2, 2, 4, 32)
        PcT = ar(4096, GROUPS, S)
        qT = ar(4608, 4, S)
        kT = ar(5632, 2, S)
        Vtok = ar(6144, 2, 2, P)
        VX = ar(6656, GROUPS, 4, HD)
        hc = ar(7168, GROUPS, 4, 32)
        hk = ar(7424, 2 * NCMP)
        kcmp = ar(7454, 16)
        vcmp = ar(7470, GROUPS, HD)
        cb = ar(7600, 2, NCMP, HEADS)
        Sc = ar(7840, 2, HEADS, NCMP)
        gT = ar(8080, S)
        gtok = ar(8336, 2, 24)
        m16 = ar(8384, 16)
        s16 = ar(8400, 16)
        KTm = ar(8448, KT, S)
        VM = ar(0, KT, 2, P)
        hot = ar(10496, 512)
        vec = ar(11008, 512)
        stats = ar(11520, 2, 6)
        mv = ar(11532, 2, 2)
        rs2 = ar(11536, 2)
        mx4 = ar(11540, 4)
        sm4 = ar(11544, 4)
        rc4 = ar(11548, 4)
        t512 = ar(11552, 512)
        sqv = SQ[:, :, :].rearrange("p a b -> p (a b)")
        uT = sqv[:, 0:512].rearrange("p (a b) -> p a b", a=2)
        vg = sqv[:, 512:1024].rearrange("p (a b) -> p a b", a=2)
        vn = sqv[:, 1024:1536].rearrange("p (a b) -> p a b", a=2)
        yv = Y[:, :, :].rearrange("p a b -> p (a b)")
        pT = yv[:, 0:544].rearrange("p (a b) -> p a b", a=2)
        wA = yv[:, 544:1088].rearrange("p (a b) -> p a b", a=2)
        wB = yv[:, 1088:1632].rearrange("p (a b) -> p a b", a=2)
        pd = yv[:, 1632:2144].rearrange("p (a b) -> p a b", a=2)
        mem_raw = yv[:, 0:2048].rearrange("p (a b) -> p a b", a=KT)
        qM = ar(4608, KT, S)
        Em = ar(2048, 2, 2, S)
        PTm = ar(3072, 2, 2, S)
        Gt = ar(0, 2, S)
        Vt = ar(512, 2, S)
        Ft = ar(1024, 2, S)
        cT = ar(0, T)
        CX = ar(512, T + 2)
        SZ = ar(1024, T)
        ZZ = ar(1536, T)
        Yc = ar(2048, T)
        Fc = ar(2560, T)
        lk = yv.rearrange("p (a b) -> p a b", a=KT)
        lq = sqv[:, 0:2048].rearrange("p (a b) -> p a b", a=KT)
        lv = ar(0, 3, 2048)
        so = ar(6144, 4, S)
        hn = ar(7168, 4, S)
        sqh = ar(8192, 4, S)
        Pl = ar(9216, 640)
        Dl = ar(9856, 640)
        em = ar(10496, S)
        rden = ar(10752, S)
        rhead = ar(11008, S)
        lroot = ar(11264, S)
        lvT = ar(11520, 2, T)
        tz = ar(9216, S)
        gx = ar(6144, T)
        ge = ar(6416, T)
        gl = ar(6688, T)
        gF = ar(6960, T)
        gA = ar(7232, T)
        gM = ar(7504, T)
        gone = ar(7776, T)
        lf = ar(8048, T)
        negM = root_m[0:LHEADS, :]
        negFM = rstd_m[0:LHEADS, :]
        acol = small[:, 0:12].rearrange("p (a b) -> p a b", a=3)

        ACC = [psum("acc0", 512), psum("acc1", 512)]
        SC = psum("scores", 1024)
        PTB = psum("turned", 1024)
        OB = [psum("outs0", 512), psum("outs1", 512)]

        x_loaded, meta_loaded, mem_loaded, params_loaded = sem("x_loaded"), sem("meta_loaded"), sem("mem_loaded"), sem("params_loaded")
        rel_loaded = sem("rel_loaded")
        bias_stored, bias_loaded, out_stored = sem("bias_stored"), sem("bias_loaded"), sem("out_stored")
        weights_loaded = [sem(f"weights_loaded{s}") for s in range(SLOTS)]
        hi_ready, lo_ready, chunk_done = sem("hi_ready"), sem("lo_ready"), sem("chunk_done")
        evacuated = [sem("evacuated0"), sem("evacuated1")]
        consts_ready = sem("consts_ready")
        sgu_masked = sem("sgu_masked")
        sq_ready, stat_ready, root_ready = sem("sq_ready"), sem("stat_ready"), sem("root_ready")
        mem_sq = sem("mem_sq")
        normed, normed_hi, normed_lo = sem("normed"), sem("normed_hi"), sem("normed_lo")
        mem_normed, mem_hi, mem_lo = sem("mem_normed"), sem("mem_hi"), sem("mem_lo")
        y_ready, x_updated = sem("y_ready"), sem("x_updated")
        act_ready, act_hi, act_lo = sem("act_ready"), sem("act_hi"), sem("act_lo")
        bias_vec, bias_copied = sem("bias_vec"), sem("bias_copied")
        cmp_bias = sem("cmp_bias")
        cmp_in = sem("cmp_in")
        cmp_out, cmp_kv = sem("cmp_out"), sem("cmp_kv")
        cb_copied, pc_zero, hc_zero, vx_zero = sem("cb_copied"), sem("pc_zero"), sem("hc_zero"), sem("vx_zero")
        sgu_var, sgu_root, sgu_normed, sgu_mixed = sem("sgu_var"), sem("sgu_root"), sem("sgu_normed"), sem("sgu_mixed")
        pool_padded, pool_diff, pool_mixed = sem("pool_padded"), sem("pool_diff"), sem("pool_mixed")
        gate_turned, gate_ready = sem("gate_turned"), sem("gate_ready")
        cs_ready, cs_shifted, cs_exp, cp_ready, cp_turned, cp_copied = (
            sem("cs_ready"), sem("cs_shifted"), sem("cs_exp"), sem("cp_ready"), sem("cp_turned"), sem("cp_copied"))
        scores, max_ready, exped, probs, turned, copied, outs = (
            sem("scores"), sem("max_ready"), sem("exped"), sem("probs"), sem("turned"), sem("copied"), sem("outs"))
        m_scores, m_max, m_exped, m_probs, m_turned, m_copied, m_outs = (
            sem("m_scores"), sem("m_max"), sem("m_exped"), sem("m_probs"), sem("m_turned"), sem("m_copied"), sem("m_outs"))
        f_init, f_gelu = sem("f_init"), sem("f_gelu")
        c_sig, cx_zero = sem("c_sig"), sem("cx_zero")
        g_raw, g_abs, g_ln, g_rows, g_turned, g_cols = (
            sem("g_raw"), sem("g_abs"), sem("g_ln"), sem("g_rows"), sem("g_turned"), sem("g_cols"))
        l_vturned, l_vcopied = sem("l_vturned"), sem("l_vcopied")
        l_scores, l_rows, l_decay, l_masked, l_probs, l_num, l_hn, l_sq, l_stat, l_root, l_rhead = (
            sem("l_scores"), sem("l_rows"), sem("l_decay"), sem("l_masked"), sem("l_probs"), sem("l_num"),
            sem("l_hn"), sem("l_sq"), sem("l_stat"), sem("l_root"), sem("l_rhead"))
        o_sig, z_sig = sem("o_sig"), sem("z_sig")
        vec_steps, act_steps, pool_steps = sem("vec_steps"), sem("act_steps"), sem("pool_steps")

        def acc(t):
            return ACC[t % 2]

        def wait_evacuated(eng, t, i=0):
            eng.wait_ge(evacuated[t % 2], t // 2 + 1 + 2 * i)

        def wait_chunk(eng, n, i=0):
            eng.wait_ge(chunk_done, n + 1 + 4 * i)

        def freed(ins, t):
            ins.then_inc(evacuated[t % 2], 1)

        def a_hi(k, w=S):
            return AH[:, k * w:(k + 1) * w]

        def a_lo(k, w=S):
            return AL[:, k * w:(k + 1) * w]

        def ffn_hi(k):
            return a_hi(k) if k < 16 else MH[:, k - 16, :]

        def ffn_lo(k):
            return a_lo(k) if k < 16 else ML[:, k - 16, :]

        block = ctx.enter_context(nc.Block())

        @block.sync
        def _(sp):
            sp.dma_start(XR[:, :, META:T], x_in).then_inc(x_loaded, 16)
            sp.dma_start(cst[:, :], params).then_inc(params_loaded, 16)
            sp.dma_start(rb[0:32, :], rel_bias).then_inc(rel_loaded, 16)
            sp.dma_start(hot[0:33, :], onehot).then_inc(rel_loaded, 16)
            sp.dma_start(XR[:, :, 0:META], meta_in).then_inc(meta_loaded, 16)

            def load(n, i=0):
                if n >= SLOTS:
                    sp.wait_ge(lo_ready, n - SLOTS + 1 + 4 * i)
                sp.dma_start(raw[:, n % SLOTS, :], weights[n + 4 * i]).then_inc(weights_loaded[n % SLOTS], 16)

            load(0)
            load(1)
            sp.dma_start(mem_raw, mem_in).then_inc(mem_loaded, 16)
            load(2)
            load(3)
            rounds = (NCHUNKS - SLOTS) // SLOTS
            with sp.Fori(0, rounds) as i:
                for s in range(SLOTS):
                    load(SLOTS + s, i)
            for n in range(SLOTS * (rounds + 1), NCHUNKS):
                load(n)
            for k in range(KT):
                sp.wait_ge(normed, 8 * 5 + k + 1)
                sp.dma_start(out[k * P:(k + 1) * P, :], SQ[:, k, META:T]).then_inc(out_stored, 16)
            sp.wait_ge(out_stored, 16 * KT)

        @block.gpsimd
        def _(pool):
            chain = Chain(pool, pool_steps)
            nc.gpsimd.memset(ones_d[:, :], 1.0 / D).then_inc(consts_ready, 1)
            nc.gpsimd.memset(ones_h[:, :], 1.0 / 512).then_inc(consts_ready, 1)
            nc.gpsimd.memset(ones_1[:, :], 1.0).then_inc(consts_ready, 1)
            chain.link(nc.gpsimd.memset(ident[:, :], 0.0))
            chain.link(nc.gpsimd.memset(sel[:, :, :], 0.0))
            nc.gpsimd.affine_select(out=ident[:, :], in_=ident[:, :], compare_op=ALU.not_equal, fill=1.0, base=0,
                                    pattern=[[-1, P]], channel_multiplier=1).then_inc(consts_ready, 1)
            nc.gpsimd.affine_select(out=sel[:, :, :], in_=sel[:, :, :], compare_op=ALU.not_equal, fill=1.0, base=0,
                                    pattern=[[-1, LHEADS], [0, P]], channel_multiplier=1).then_inc(consts_ready, 1)
            pool.wait_ge(consts_ready, 7)
            nc.gpsimd.memset(hc[:, :, :, :], 0.0).then_inc(hc_zero, 1)
            nc.gpsimd.memset(VX[:, :, :, :], 0.0).then_inc(vx_zero, 1)
            pool.wait_ge(params_loaded, 16)
            sw = col("sgu_w", 0, 512).rearrange("p (h t) -> p h t", h=4)
            nc.gpsimd.affine_select(out=sw, in_=sw, compare_op=ALU.is_ge, fill=0.0, base=0,
                                    pattern=[[0, 4], [1, P]], channel_multiplier=-1).then_inc(sgu_masked, 1)
            pool.wait_ge(mem_lo, 1)
            nc.gpsimd.memset(pT[:, :, 0:META], 0.0).then_inc(pool_padded, 1)
            pool.wait_ge(cmp_in, 1)
            nc.gpsimd.memset(AR[:, 3584:4096], 0.0).then_inc(pc_zero, 1)
            pool.wait_ge(pool_padded, 1)
            for t in (TILE["pool"], TILE["pool"] + 1):
                wait_evacuated(pool, t)
            chain.link(nc.gpsimd.tensor_tensor(wA[:, :, 1:T], pT[:, :, 1:T], pT[:, :, 0:T - 1], ALU.add))
            chain.link(nc.gpsimd.tensor_tensor(wB[:, :, 3:T], wA[:, :, 3:T], wA[:, :, 1:T - 2], ALU.add))
            inv = col("pool_inv", 0, 512).rearrange("p (a b) -> p a b", a=2)
            chain.link(nc.gpsimd.tensor_tensor(pd[0:64, 0, :], wA[0:64, 0, META:T], inv[0:64, 0, :], ALU.mult))
            chain.link(nc.gpsimd.tensor_tensor(pd[64:128, 0, :], wB[64:128, 0, META:T], inv[64:128, 0, :], ALU.mult))
            chain.link(nc.gpsimd.tensor_tensor(wA[:, 1, 7:T], wB[:, 1, 7:T], wB[:, 1, 3:T - 4], ALU.add))
            chain.link(nc.gpsimd.tensor_tensor(pd[0:64, 1, :], wA[0:64, 1, META:T], inv[0:64, 1, :], ALU.mult))
            chain.link(nc.gpsimd.tensor_tensor(wB[64:128, 1, 15:T], wA[64:128, 1, 15:T], wA[64:128, 1, 7:T - 8], ALU.add))
            chain.link(nc.gpsimd.tensor_tensor(pd[64:128, 1, :], wB[64:128, 1, META:T], inv[64:128, 1, :], ALU.mult))
            nc.gpsimd.tensor_tensor(pd, pd, pT[:, :, META:T], ALU.subtract).then_inc(pool_diff, 1)
            for h in range(LHEADS):
                pool.wait_ge(l_decay, 2 * h + 2)
                nc.gpsimd.affine_select(out=Dl[:, 0:S], in_=Dl[:, 0:S], compare_op=ALU.is_ge, fill=0.0, base=0,
                                        pattern=[[1, S]], channel_multiplier=-1).then_inc(l_masked, 1)
                nc.gpsimd.affine_select(out=Dl[:, S:S + P], in_=Dl[:, S:S + P], compare_op=ALU.is_ge, fill=0.0,
                                        base=0, pattern=[[1, P]], channel_multiplier=-1).then_inc(l_masked, 1)

        @block.scalar
        def _(act):
            chain = Chain(act, act_steps)

            def hi(n, i=0):
                act.wait_ge(weights_loaded[n % SLOTS], 16 * (n // SLOTS + 1) + 16 * i)
                if n >= SLOTS:
                    act.wait_ge(chunk_done, n - SLOTS + 1 + 4 * i)
                nc.scalar.activation(w_hi[:, n % SLOTS, :], raw[:, n % SLOTS, :], ACT.Copy).then_inc(hi_ready, 1)

            def ahead(n, i=0):
                if n + AHEAD < NCHUNKS:
                    hi(n + AHEAD, i)

            def take_root(e, w, lo, dst=root):
                act.wait_ge(stat_ready, e + 1)
                nc.scalar.activation(dst[:, lo:T], OB[1][:, 0:w], ACT.Sqrt, bias=eps_col).then_inc(root_ready, 1)

            def normed_to_hi(pre, lo):
                for k in range(KT):
                    act.wait_ge(normed, 8 * pre + k + 1)
                    nc.scalar.activation(XH[:, k, lo:T], SQ[:, k, lo:T], ACT.Copy).then_inc(normed_hi, 1)

            def square_x(lo, update):
                for k in range(KT):
                    act.wait_ge(x_updated, 8 * update + k + 1)
                    nc.scalar.activation(SQ[:, k, lo:T], XR[:, k, lo:T], ACT.Square).then_inc(sq_ready, 1)

            def to_y(t, m):
                nc.scalar.activation(Y[:, m, META:T], acc(t)[:, 0:S], ACT.Copy).then_inc(y_ready, 1)
                freed(nc.scalar.activation(SQ[:, m, META:T], acc(t)[:, 0:S], ACT.Square), t)

            eps_col = small[:, 158:159]
            act.wait_ge(consts_ready, 7)
            act.wait_ge(x_loaded, 16)
            for k in range(KT):
                nc.scalar.activation(SQ[:, k, META:T], XR[:, k, META:T], ACT.Square).then_inc(sq_ready, 1)
            act.wait_ge(bias_vec, 1)
            nc.scalar.activation(vec[0:HEADS, :], OB[0][0:HEADS, :], ACT.Copy).then_inc(bias_copied, 1)
            act.wait_ge(bias_copied, 1)
            act.dma_start(bias_rows, vec[0:HEADS, :]).then_inc(bias_stored, 16)
            for n in range(AHEAD):
                hi(n)
            take_root(NORM_X, S, META)
            normed_to_hi(PRE_X, META)
            act.wait_ge(bias_stored, 16)
            act.dma_start(bias, bass.AP(tensor=bias_rows.tensor, offset=bias_rows.offset + S - 127,
                                        ap=[[1, P], [512, HEADS], [1, S]])).then_inc(bias_loaded, 16)
            act.wait_ge(stat_ready, NORM_MEM + 1)
            nc.scalar.activation(root_m[:, 0:S], PTB[:, 0:S], ACT.Sqrt, bias=eps_col).then_inc(root_ready, 1)
            n, t = CHUNK["kc"], TILE["kc"]
            ahead(n)
            wait_chunk(act, n)
            for g in range(GROUPS):
                src = acc(t)[g * HD:(g + 1) * HD, 0:S]
                chain.note(nc.scalar.activation(KC2[0:HD, 0, g, :], src, ACT.Copy))
                last = nc.scalar.activation(KC2[HD:P, 0, g, 0:S - 1], src[:, 1:S], ACT.Copy)
                if g == 0:
                    chain.note(last)
            chain.wait()
            freed(last, t)
            ahead(CHUNK["vc"])
            act.wait_ge(mem_normed, 1)
            nc.scalar.activation(MH[:, :, :], mem_raw, ACT.Copy).then_inc(mem_hi, 1)
            for j in range(2):
                n, t = CHUNK["sgu_v"] + j, TILE["sgu_v"] + j
                ahead(n)
                wait_chunk(act, n)
                freed(nc.scalar.activation(vg[:, :, j * P:(j + 1) * P], acc(t)[:, 0:S].rearrange("p (a b) -> p a b", a=2),
                                           ACT.Gelu_apprx_tanh), t)
            for j in range(2):
                n, t = CHUNK["sgu_u"] + j, TILE["sgu_u"] + j
                ahead(n)
                wait_chunk(act, n)
                freed(nc.scalar.activation(uT[:, j, :], acc(t)[:, 0:S], ACT.Gelu_apprx_tanh), t)
            act.wait_ge(mem_lo, 1)
            for j in range(2):
                n, t = CHUNK["pool"] + j, TILE["pool"] + j
                ahead(n)
                wait_chunk(act, n)
                freed(nc.scalar.activation(pT[:, j, META:T], acc(t)[:, 0:S], ACT.Copy), t)
            n, t = CHUNK["cmp"], TILE["cmp"]
            ahead(n)
            ahead(n + 1)
            wait_chunk(act, n + 1)
            freed(nc.scalar.activation(hk, acc(t)[:, 0:30], ACT.Gelu_apprx_tanh, bias=col("cmp_b1", 0)), t)
            ahead(n + 2)
            ahead(n + 3)
            wait_chunk(act, n + 3)
            act.wait_ge(hc_zero, 1)
            for r in range(4):
                last = nc.scalar.activation(hc[:, :, r, 0:NCMP], acc(t + 1)[:, 0:30].rearrange("p (g c) -> p g c", g=2),
                                            ACT.Gelu_apprx_tanh, bias=col("cmp_b1", 1))
                if r < 3:
                    chain.note(last)
            freed(last, t + 1)
            act.wait_ge(sgu_var, 1)
            nc.scalar.activation(rs2, mv[:, :, 1], ACT.Sqrt, bias=eps_col).then_inc(sgu_root, 1)
            for name in ("vs", "vw", "ks", "kw"):
                ahead(CHUNK[name])
            for j in range(4):
                n, t = CHUNK["q"] + j, TILE["q"] + j
                ahead(n)
                wait_chunk(act, n)
                freed(nc.scalar.mul(qT[:, j, :], acc(t)[:, 0:S], HD ** -0.5), t)
            n, t = CHUNK["gates"], TILE["gates"]
            ahead(n)
            wait_chunk(act, n)
            freed(nc.scalar.activation(gT[0:24, :], acc(t)[0:24, 0:S], ACT.Exp, scale=-1.0), t)
            act.wait_ge(cs_shifted, 1)
            nc.scalar.activation(Sc[:, :, :, :], Sc[:, :, :, :], ACT.Exp).then_inc(cs_exp, 1)

            def out_hi(j):
                act.wait_ge(outs, j + 1)
                nc.scalar.activation(a_hi(j), OB[j % 2][:, 0:S], ACT.Copy).then_inc(act_hi, 1)

            for h in range(HEADS):
                n = CHUNK["mk"] + 2 * h
                ahead(n)
                act.wait_ge(max_ready, h + 1)
                for b in range(4):
                    lo, w = (P * b, P) if b < 2 else (S * (b - 1), S)
                    last = nc.scalar.activation(Sx[:, lo:lo + w], Sx[:, lo:lo + w], ACT.Exp, bias=mx4[:, b:b + 1],
                                                accum_out=sm4[:, b:b + 1])
                    if b < 3:
                        chain.note(last)
                chain.wait()
                last.then_inc(exped, 1)
                ahead(n + 1)
                if h >= 2 and h % 2 == 0:
                    out_hi(h // 2 - 1)
                if h == 0:
                    act.wait_ge(cp_turned, 1)
                    nc.scalar.activation(PcT[:, :, :], OB[0][:, 0:512].rearrange("p (g t) -> p g t", g=2),
                                         ACT.Copy).then_inc(cp_copied, 1)
                act.wait_ge(turned, h + 1)
                nc.scalar.activation(PTx[:, :, :], PTB[:, :].rearrange("p (b t) -> p b t", b=2)[:, :, 0:384],
                                     ACT.Copy).then_inc(copied, 1)
            out_hi(3)
            for j in range(2):
                act.wait_ge(act_ready, j + 1)
                nc.scalar.activation(a_hi(4 + j), t512[:, j * S:(j + 1) * S], ACT.Copy).then_inc(act_hi, 1)
            for j in range(2):
                act.wait_ge(act_ready, 3 + j)
                nc.scalar.activation(a_hi(6 + j), vg[:, j, :], ACT.Copy).then_inc(act_hi, 1)
            for m in range(KT):
                n, t = CHUNK["w_out"] + m, TILE["w_out"] + m
                ahead(n)
                wait_chunk(act, n)
                to_y(t, m)
            take_root(NORM_MIX, S, META)
            square_x(META, 0)
            take_root(NORM_X1, S, META)
            normed_to_hi(PRE_X1, META)
            def m_exp(h):
                act.wait_ge(m_max, h + 1)
                if h >= 2:
                    act.wait_ge(m_turned, h - 1)
                for b in range(2):
                    last = nc.scalar.activation(Em[:, h % 2, b, :], SC[:, (h % 2) * 512 + b * S:(h % 2) * 512 + (b + 1) * S],
                                                ACT.Exp, bias=small[:, 16 + 2 * h + b:17 + 2 * h + b],
                                                accum_out=small[:, 24 + 2 * h + b:25 + 2 * h + b])
                    if b < 1:
                        chain.link(last)
                last.then_inc(m_exped, 1)

            def m_copy(h):
                act.wait_ge(m_turned, h + 1)
                if h >= 2:
                    act.wait_ge(m_outs, h - 1)
                nc.scalar.activation(PTm[:, h % 2, :, :], PTB[:, (h % 2) * 512:(h % 2) * 512 + 512].rearrange("p (m t) -> p m t", m=2),
                                     ACT.Copy).then_inc(m_copied, 1)

            def m_hi(h):
                act.wait_ge(m_outs, h + 1)
                nc.scalar.activation(AH[:, 2 * h * S:(2 * h + 2) * S], OB[h % 2][:, :], ACT.Copy).then_inc(act_hi, 1)

            for m in range(KT):
                n, t = CHUNK["mq"] + m, TILE["mq"] + m
                ahead(n)
                wait_chunk(act, n)
                freed(nc.scalar.mul(qM[:, m, :], acc(t)[:, 0:S], (D // MEM_HEADS) ** -0.5), t)
                if m >= 3 and m % 2 == 1:
                    m_exp((m - 3) // 2)
                if m >= 5 and m % 2 == 1:
                    m_copy((m - 5) // 2)
                if m == 7:
                    m_hi(0)
            m_exp(3)
            m_copy(2)
            m_hi(1)
            m_copy(3)
            m_hi(2)
            m_hi(3)
            for m in range(KT):
                n, t = CHUNK["mo"] + m, TILE["mo"] + m
                ahead(n)
                wait_chunk(act, n)
                to_y(t, m)
            take_root(NORM_MEMOUT, S, META)
            square_x(META, 1)
            take_root(NORM_X2, S, META)
            normed_to_hi(PRE_X2, META)
            taps = col("ffn_conv", 0, 176).rearrange("p (a b) -> p a b", b=8)

            def ffn_act(i, hid):
                for r in range(2):
                    for v in range(2):
                        n, t = CHUNK["up"] + 2 * r + v, TILE["up"] + 2 * r + v
                        ahead(n, i)
                        wait_chunk(act, n, i)
                        dst = (Gt, Vt)[v][:, r, :]
                        nc.scalar.activation(dst, acc(t)[:, 0:S], ACT.Identity, bias=taps[:, 2 * i + r, 4 * v + 3:4 * v + 4],
                                             scale=taps[:, 2 * i + r, 4 * v + 2:4 * v + 3]).then_inc(f_init, 1)
                    wait_evacuated(act, TILE["up"] + 2 * r, i)
                    nc.scalar.activation(Gt[:, r, :], Gt[:, r, :], ACT.Gelu_apprx_tanh).then_inc(f_gelu, 1)
                    act.wait_ge(act_ready, 4 + 1 + r + 2 * i)
                    nc.scalar.activation(hid(i, r), Ft[:, r, :], ACT.Copy).then_inc(act_hi, 1)

            for i in range(FFN_TILES // 2):
                ffn_act(i, lambda i, r: ffn_hi(2 * i + r))
            for m in range(KT):
                n, t = CHUNK["down"] + 3 * m, TILE["down"] + m
                for c in range(3):
                    ahead(n + c)
                wait_chunk(act, n + 2)
                to_y(t, m)
            take_root(NORM_FFN, S, META)
            act.wait_ge(meta_loaded, 16)
            square_x(0, 2)
            take_root(NORM_H0, T, 0)
            normed_to_hi(PRE_H0, 0)
            def conv_act(i):
                n, t = CHUNK["conv_in"], TILE["conv_in"]
                ahead(n, i)
                wait_chunk(act, n, i)
                freed(nc.scalar.activation(cT, acc(t)[:, 0:T], ACT.Copy), t)
                ahead(n + 1, i)
                ahead(n + 2, i)
                wait_chunk(act, n + 2, i)
                nc.scalar.activation(SZ, acc(t + 2)[:, 0:T], ACT.Sigmoid).then_inc(c_sig, 1)
                ahead(n + 3, i)
                act.wait_ge(act_ready, 4 + FFN_TILES + 1 + i)
                nc.scalar.activation(AH[:, bass.ds(i * T, T)] if not isinstance(i, int) else a_hi(i, T), Fc,
                                     ACT.Copy).then_inc(act_hi, 1)

            for i in range(E_TILES):
                conv_act(i)
            for m in range(KT):
                n, t = CHUNK["conv_out"] + 2 * m, TILE["conv_out"] + m
                ahead(n)
                ahead(n + 1)
                wait_evacuated(act, t)
                nc.scalar.activation(SQ[:, m, :], XR[:, m, :], ACT.Square).then_inc(sq_ready, 1)
            take_root(NORM_H1, T, 0)
            normed_to_hi(PRE_H1, 0)
            n, t = CHUNK["lgates"], TILE["lgates"]
            ahead(n)
            wait_chunk(act, n)
            freed(nc.scalar.activation(gx[0:36, :], acc(t)[0:36, 0:T], ACT.Identity, bias=col("gate_b")[0:36]), t)
            wait_evacuated(act, t)
            chain.link(nc.scalar.activation(ge[32:36, :], gx[32:36, :], ACT.Abs))
            chain.link(nc.scalar.activation(ge[32:36, :], ge[32:36, :], ACT.Exp, scale=-1.0))
            nc.scalar.activation(gl[32:36, :], ge[32:36, :], ACT.Ln, bias=ones_1[32:36, 0:1]).then_inc(g_ln, 1)
            for m in range(KT):
                n, t = CHUNK["lk"] + m, TILE["lk"] + m
                ahead(n)
                wait_chunk(act, n)
                freed(nc.scalar.activation(lk[:, m, :], acc(t)[:, 0:T], ACT.Copy), t)
            for m in range(KT):
                n, t = CHUNK["lq"] + m, TILE["lq"] + m
                ahead(n)
                wait_chunk(act, n)
                freed(nc.scalar.mul(lq[:, m, :], acc(t)[:, 0:S], S ** -0.5), t)

            def decay(h):
                act.wait_ge(l_rows, h + 1)
                if h == 0:
                    act.wait_ge(g_cols, 1)
                else:
                    act.wait_ge(l_probs, 3 * h)
                chain.note(nc.scalar.activation(Dl[:, 0:S], PTB[:, 0:S], ACT.Exp, bias=acol[:, 1, h:h + 1]))
                chain.note(nc.scalar.activation(Dl[:, S:S + P], PTB[:, P:S], ACT.Exp, bias=acol[:, 2, h:h + 1]))
                nc.scalar.activation(Dl[0:META, 384:640], PTB[0:META, 0:S], ACT.Exp,
                                     bias=acol[0:META, 0, h:h + 1]).then_inc(l_decay, 1)
                chain.wait()
                if h:
                    act.wait_ge(l_hn, h)
                nc.scalar.activation(em, PTB[:, S:2 * S], ACT.Exp).then_inc(l_decay, 1)

            for m in range(E_TILES):
                n, t = CHUNK["lv"] + m, TILE["lv"] + m
                ahead(n)
                wait_chunk(act, n)
                if m >= 2:
                    act.wait_ge(l_vturned, m - 1)
                freed(nc.scalar.activation(lvT[:, m % 2, :], acc(t)[:, 0:T], ACT.Copy), t)
                if m == 4:
                    decay(0)
            for h in range(LHEADS):
                act.wait_ge(l_hn, h + 1)
                nc.scalar.activation(sqh[:, :, :], hn[:, :, :], ACT.Square).then_inc(l_sq, 1)
                if h + 1 < LHEADS:
                    decay(h + 1)
                act.wait_ge(l_stat, h + 1)
                nc.scalar.activation(lroot, PTB[:, 512:512 + S], ACT.Sqrt, bias=eps_col).then_inc(l_root, 1)
                for m in range(4):
                    n, t = CHUNK["oz"] + 8 * h + m, TILE["oz"] + 8 * h + m
                    ahead(n)
                    wait_chunk(act, n)
                    if h:
                        act.wait_ge(act_ready, 42 + 4 * h)
                    freed(nc.scalar.activation(so[:, m, :], acc(t)[:, 0:S], ACT.Sigmoid), t)
                for m in range(4):
                    n, t = CHUNK["oz"] + 8 * h + 4 + m, TILE["oz"] + 8 * h + 4 + m
                    ahead(n)
                    wait_chunk(act, n)
                    act.wait_ge(l_num, h + 1)
                    nc.scalar.activation(tz, acc(t)[:, 0:S], ACT.Sigmoid).then_inc(z_sig, 1)
                    act.wait_ge(act_ready, 42 + 4 * h + m + 1)
                    nc.scalar.activation(a_hi(4 * h + m), hn[:, m, :], ACT.Copy).then_inc(act_hi, 1)
            for m in range(KT):
                n, t = CHUNK["lout"] + 2 * m, TILE["lout"] + m
                ahead(n)
                ahead(n + 1)
                wait_evacuated(act, t)
                nc.scalar.activation(SQ[:, m, META:T], XR[:, m, META:T], ACT.Square).then_inc(sq_ready, 1)
            take_root(NORM_FINAL, S, META)

        @block.tensor
        def _(pe):
            def stat(e, src, w, dst):
                for k in range(KT):
                    src(k)
                    last = nc.tensor.matmul(dst, ones_d[:, :], (SQ[:, k, T - w:T] if e != NORM_MEM else KTm[:, k, :]),
                                            start=(k == 0), stop=(k == KT - 1))
                last.then_inc(stat_ready, 1)

            def stat_x(e, count, w):
                stat(e, lambda k: pe.wait_ge(sq_ready, 8 * count + k + 1), w, OB[1][:, 0:w])

            def stat_y(e, name):
                stat(e, lambda k: wait_evacuated(pe, TILE[name] + k), S, OB[1][:, 0:S])

            def begin(n, t, first, i=0):
                pe.wait_ge(lo_ready, n + 1 + 4 * i)
                if first and t >= 2:
                    pe.wait_ge(evacuated[t % 2], t // 2 + 2 * i)

            def chunk(n, t, xh, xl, w, i=0, k0=0, nk=KT, total=KT, ready=None):
                begin(n, t, k0 == 0, i)
                s = n % SLOTS
                for j in range(nk):
                    k = k0 + j
                    if ready:
                        ready(k)
                    wh, wl = w_hi[:, s, j * P:(j + 1) * P], w_lo[:, s, j * P:(j + 1) * P]
                    nc.tensor.matmul(acc(t)[:, 0:w], wh, xh(k), start=(k == 0), stop=False)
                    nc.tensor.matmul(acc(t)[:, 0:w], wh, xl(k), start=False, stop=False)
                    last = nc.tensor.matmul(acc(t)[:, 0:w], wl, xh(k), start=False, stop=(k == total - 1))
                last.then_inc(chunk_done, 1)

            def chunk_tokens(n, t, xh, xl):
                begin(n, t, True)
                s = n % SLOTS
                for b in range(2):
                    o = acc(t)[:, b * P:(b + 1) * P]
                    for k in range(KT):
                        wh, wl = w_hi[:, s, k * P:(k + 1) * P], w_lo[:, s, k * P:(k + 1) * P]
                        nc.tensor.matmul(o, xh(k)[:, b * P:(b + 1) * P], wh, start=(k == 0), stop=False)
                        nc.tensor.matmul(o, xl(k)[:, b * P:(b + 1) * P], wh, start=False, stop=False)
                        last = nc.tensor.matmul(o, xh(k)[:, b * P:(b + 1) * P], wl, start=False, stop=(k == KT - 1))
                last.then_inc(chunk_done, 1)

            def xh(k):
                return XH[:, k, META:T]

            def xl(k):
                return XL[:, k, META:T]

            def xha(k):
                return XH[:, k, :]

            def xla(k):
                return XL[:, k, :]

            def pre_ready(pre):
                return lambda k: pe.wait_ge(normed_lo, 8 * pre + k + 1)

            pe.wait_ge(consts_ready, 7)
            pe.wait_ge(rel_loaded, 32)
            nc.tensor.matmul(OB[0][0:HEADS, :], rb[:, :], hot[0:33, :], start=True, stop=True).then_inc(bias_vec, 1)
            for b in range(2):
                for c in range(NCMP):
                    lo = S + P * b - CSTRIDE * c - 31
                    o = (b * NCMP + c) * HEADS
                    last = nc.tensor.matmul(SC[:, o:o + HEADS], hot[0:33, lo:lo + P], rb[:, :], start=True, stop=True)
            last.then_inc(cmp_bias, 1)
            stat_x(NORM_X, 0, S)
            stat(NORM_MEM, lambda k: pe.wait_ge(mem_sq, 1), S, PTB[:, 0:S])
            chunk(CHUNK["kc"], TILE["kc"], xh, xl, S, ready=pre_ready(PRE_X))
            chunk(CHUNK["vc"], TILE["vc"], xh, xl, S)
            for j in range(2):
                chunk_tokens(CHUNK["sgu_v"] + j, TILE["sgu_v"] + j, xh, xl)
            for name in ("sgu_u", "pool"):
                for j in range(2):
                    chunk(CHUNK[name] + j, TILE[name] + j, xh, xl, S)
            for v in range(2):
                def rhs(part):
                    return lambda k: part[:, 2048 + (v * 16 + k) * 30:2048 + (v * 16 + k + 1) * 30]
                if v == 0:
                    pe.wait_ge(cmp_in, 2)
                for c in range(2):
                    chunk(CHUNK["cmp"] + 2 * v + c, TILE["cmp"] + v, rhs(AH), rhs(AL), 30, k0=8 * c, total=16)
            chunk_tokens(CHUNK["vs"], TILE["vs"], xh, xl)
            w2 = col("cmp_w2", 0, 128)
            wait_evacuated(pe, TILE["cmp"])
            wait_evacuated(pe, TILE["cmp"] + 1)
            pe.wait_ge(bias_copied, 1)
            for g in range(GROUPS):
                nc.tensor.matmul(OB[0][g * HD:(g + 1) * HD, 0:NCMP], w2[:, 0:HD], hk[:, g * NCMP:(g + 1) * NCMP],
                                 start=True, stop=True)
            for g in range(GROUPS):
                last = nc.tensor.matmul(OB[0][:, 64 + g * HD:64 + (g + 1) * HD], hc[:, g, :, :].rearrange("p a b -> p (a b)"),
                                        w2[:, HD:2 * HD], start=True, stop=True)
            last.then_inc(cmp_out, 1)
            chunk_tokens(CHUNK["vw"], TILE["vw"], xh, xl)
            chunk(CHUNK["ks"], TILE["ks"], xh, xl, S)
            chunk(CHUNK["kw"], TILE["kw"], xh, xl, S)
            pe.wait_ge(sgu_normed, 1)
            pe.wait_ge(sgu_masked, 1)
            pe.wait_ge(root_ready, 1)
            sw = col("sgu_w", 0, 512).rearrange("p (h t) -> p h t", h=4)
            for h in range(4):
                for b in range(2):
                    o = OB[1][(h % 2) * HD:(h % 2 + 1) * HD, (h // 2) * S + b * P:(h // 2) * S + (b + 1) * P]
                    last = nc.tensor.matmul(o, vn[:, b, h * HD:(h + 1) * HD], sw[:, h, :], start=True, stop=True)
            last.then_inc(sgu_mixed, 1)
            for j in range(4):
                chunk(CHUNK["q"] + j, TILE["q"] + j, xh, xl, S)
            chunk(CHUNK["gates"], TILE["gates"], xh, xl, S)
            pe.wait_ge(pool_diff, 1)
            pe.wait_ge(root_ready, 2)
            pw = col("pool_w", 0, 128).rearrange("p (a b) -> p a b", a=2)
            for j in range(2):
                for r in range(2):
                    o = PTB[r * HD:(r + 1) * HD, r * 512 + j * S:r * 512 + (j + 1) * S]
                    last = nc.tensor.matmul(o, pw[r * HD:(r + 1) * HD, j, :], pd[r * HD:(r + 1) * HD, j, :],
                                            start=True, stop=True)
            last.then_inc(pool_mixed, 1)
            wait_evacuated(pe, TILE["gates"])
            pe.wait_ge(sgu_mixed, 2)
            for b in range(2):
                last = nc.tensor.transpose(OB[1][:, b * 24:(b + 1) * 24], gT[0:24, b * P:(b + 1) * P], ident[0:24, 0:24])
            last.then_inc(gate_turned, 1)
            pe.wait_ge(cmp_kv, 2)
            pe.wait_ge(cb_copied, 1)
            for g in range(GROUPS):
                for j in range(4):
                    for b in range(2):
                        o = g * 512 + (b * 4 + j) * NCMP
                        last = nc.tensor.matmul(SC[:, o:o + NCMP], qT[g * HD:(g + 1) * HD, j, b * P:(b + 1) * P],
                                                kcmp[g * HD:(g + 1) * HD, 0:NCMP], start=True, stop=True)
            last.then_inc(cs_ready, 1)

            def qk(h):
                j, g = h // 2, h % 2
                if h == 0:
                    pe.wait_ge(cs_shifted, 1)
                    wait_evacuated(pe, TILE["kw"])
                    wait_evacuated(pe, TILE["q"] + 3)
                else:
                    pe.wait_ge(max_ready, h)
                q = qT[g * HD:(g + 1) * HD, j, :]
                for r in range(2):
                    k = kT[g * HD:(g + 1) * HD, r, :]
                    nc.tensor.matmul(SC[:, r * P:(r + 1) * P], q[:, 0:P], k[:, 0:P], start=True, stop=True)
                for r in range(2):
                    k = kT[g * HD:(g + 1) * HD, r, :]
                    last = nc.tensor.matmul(SC[:, 512 + r * S:512 + (r + 1) * S], q[:, P:S], k, start=True, stop=True)
                last.then_inc(scores, 1)

            def turn(h):
                pe.wait_ge(probs, h + 1)
                if h == 0:
                    pe.wait_ge(pool_mixed, 2)
                else:
                    pe.wait_ge(copied, h)
                for r in range(2):
                    o = r * 512
                    nc.tensor.transpose(PTB[:, o:o + P], Sx[:, r * P:(r + 1) * P], ident[:, :])
                    nc.tensor.transpose(PTB[:, o + P:o + S], Sx[:, S + r * S:S + r * S + P], ident[:, :])
                    last = nc.tensor.transpose(PTB[:, o + S:o + S + P], Sx[:, S + r * S + P:S + (r + 1) * S], ident[:, :])
                last.then_inc(turned, 1)

            def pv(h):
                j, g = h // 2, h % 2
                pe.wait_ge(copied, h + 1)
                if h == 0:
                    pe.wait_ge(cp_copied, 1)
                if g == 0 and j >= 2:
                    pe.wait_ge(act_lo, j - 1)
                o = OB[j % 2][g * HD:(g + 1) * HD, 0:S]
                for r in range(2):
                    nc.tensor.matmul(o, Vtok[:, r, 0, g * HD:(g + 1) * HD], PTx[:, r, 0:S], start=(r == 0), stop=False)
                    nc.tensor.matmul(o[:, P:S], Vtok[:, r, 1, g * HD:(g + 1) * HD], PTx[:, r, S:384], start=False, stop=False)
                last = nc.tensor.matmul(o, VX[:, g, j, :], PcT[:, g, :], start=False, stop=True)
                if g:
                    last.then_inc(outs, 1)

            for h in range(HEADS):
                qk(h)
                n, t = CHUNK["mk"] + 2 * h, TILE["mk"] + 2 * h
                if h == 0:
                    pe.wait_ge(mem_lo, 1)
                for c in range(2):
                    if c == 1 and h:
                        pv(h - 1)
                    if h < 4:
                        chunk(n + c, t + c, lambda k: MH[:, k, :], lambda k: ML[:, k, :], S)
                    else:
                        chunk_tokens(n + c, t + c, lambda k: MH[:, k, :], lambda k: ML[:, k, :])
                if h == 0:
                    pe.wait_ge(cp_ready, 1)
                    pe.wait_ge(cmp_kv, 2)
                    for g in range(GROUPS):
                        for b in range(2):
                            last = nc.tensor.transpose(OB[0][:, g * S + b * P:g * S + (b + 1) * P],
                                                       Pc[:, b, g, :, :].rearrange("p a b -> p (a b)"), ident[:, :])
                    last.then_inc(cp_turned, 1)
                turn(h)
            pv(HEADS - 1)
            pe.wait_ge(act_lo, 8)
            for m in range(KT):
                chunk(CHUNK["w_out"] + m, TILE["w_out"] + m, a_hi, a_lo, S)
            stat_y(NORM_MIX, "w_out")
            stat_x(NORM_X1, 1, S)

            def m_qk(h):
                for j in (2 * h, 2 * h + 1):
                    wait_evacuated(pe, TILE["mq"] + j)
                if h >= 2:
                    pe.wait_ge(m_exped, h - 1)
                for b in range(2):
                    for j in range(2):
                        last = nc.tensor.matmul(SC[:, (h % 2) * 512 + b * S:(h % 2) * 512 + (b + 1) * S],
                                                qM[:, 2 * h + j, b * P:(b + 1) * P], KTm[:, 2 * h + j, :],
                                                start=(j == 0), stop=(j == 1))
                last.then_inc(m_scores, 1)

            def m_turn(h):
                pe.wait_ge(m_probs, h + 1)
                if h >= 2:
                    pe.wait_ge(m_copied, h - 1)
                for m in range(2):
                    for b in range(2):
                        last = nc.tensor.transpose(PTB[:, (h % 2) * 512 + m * S + b * P:(h % 2) * 512 + m * S + (b + 1) * P],
                                                   Em[:, h % 2, b, m * P:(m + 1) * P], ident[:, :])
                last.then_inc(m_turned, 1)

            def m_pv(h):
                pe.wait_ge(m_copied, h + 1)
                if h >= 2:
                    pe.wait_ge(act_lo, ACT_MEM + h - 1)
                for v in range(2):
                    for m in range(2):
                        last = nc.tensor.matmul(OB[h % 2][:, v * S:(v + 1) * S], VM[:, 2 * h + v, m, :], PTm[:, h % 2, m, :],
                                                start=(m == 0), stop=(m == 1))
                last.then_inc(m_outs, 1)

            for m in range(KT):
                chunk(CHUNK["mq"] + m, TILE["mq"] + m, xh, xl, S, ready=pre_ready(PRE_X1) if m == 0 else None)
                if m == 2:
                    m_qk(0)
                if m == 4:
                    m_turn(0)
                    m_qk(1)
                if m == 5:
                    m_pv(0)
                if m == 6:
                    m_turn(1)
                    m_qk(2)
                if m == 7:
                    m_pv(1)
            m_qk(3)
            m_turn(2)
            m_pv(2)
            m_turn(3)
            m_pv(3)
            pe.wait_ge(act_lo, 12)
            for m in range(KT):
                chunk(CHUNK["mo"] + m, TILE["mo"] + m, a_hi, a_lo, S)
            stat_y(NORM_MEMOUT, "mo")
            stat_x(NORM_X2, 2, S)
            def ffn_pe(i, ready=None):
                for r in range(4):
                    chunk(CHUNK["up"] + r, TILE["up"] + r, xh, xl, S, i=i, ready=ready if r == 0 else None)

            for i in range(FFN_TILES // 2):
                ffn_pe(i, pre_ready(PRE_X2) if i == 0 else None)
            for m in range(KT):
                for c in range(3):
                    chunk(CHUNK["down"] + 3 * m + c, TILE["down"] + m, ffn_hi, ffn_lo, S, k0=8 * c,
                          nk=min(8, FFN_TILES - 8 * c), total=FFN_TILES,
                          ready=(lambda k: pe.wait_ge(act_lo, 12 + k + 1)) if m == 0 else None)
            stat_y(NORM_FFN, "down")
            stat_x(NORM_H0, 3, T)
            def conv_pe(i, ready=None):
                for r in range(4):
                    chunk(CHUNK["conv_in"] + r, TILE["conv_in"] + r, xha, xla, T, i=i, ready=ready if r == 0 else None)

            for i in range(E_TILES):
                conv_pe(i, pre_ready(PRE_H0) if i == 0 else None)
            for m in range(KT):
                for c in range(2):
                    chunk(CHUNK["conv_out"] + 2 * m + c, TILE["conv_out"] + m, lambda k: a_hi(k, T), lambda k: a_lo(k, T), T,
                          k0=8 * c, total=E_TILES, ready=(lambda k: pe.wait_ge(act_lo, 12 + FFN_TILES + k + 1)) if m == 0 else None)
            stat_x(NORM_H1, 4, T)
            chunk(CHUNK["lgates"], TILE["lgates"], xha, xla, T, ready=pre_ready(PRE_H1))
            for m in range(KT):
                chunk(CHUNK["lk"] + m, TILE["lk"] + m, xha, xla, T)
            pe.wait_ge(g_rows, 3)
            for s, (lo, w) in enumerate(((0, META), (META, P), (META + P, P))):
                last = nc.tensor.transpose(OB[0][0:w, 4 * s:4 * s + 4], gA[0:LHEADS, lo:lo + w], ident[0:LHEADS, 0:LHEADS])
            last.then_inc(g_turned, 1)
            for m in range(KT):
                chunk(CHUNK["lq"] + m, TILE["lq"] + m, xh, xl, S)

            def l_qk(h):
                if h == 0:
                    wait_evacuated(pe, TILE["lk"] + 7)
                    wait_evacuated(pe, TILE["lq"] + 7)
                else:
                    pe.wait_ge(l_probs, 3 * h)
                for j in range(2):
                    nc.tensor.matmul(SC[:, 0:S], lk[:, 2 * h + j, META:META + P], lq[:, 2 * h + j, :],
                                     start=(j == 0), stop=(j == 1))
                for j in range(2):
                    nc.tensor.matmul(SC[:, S:S + P], lk[:, 2 * h + j, META + P:T], lq[:, 2 * h + j, P:S],
                                     start=(j == 0), stop=(j == 1))
                for j in range(2):
                    last = nc.tensor.matmul(SC[0:META, 512:512 + S], lk[:, 2 * h + j, 0:META], lq[:, 2 * h + j, :],
                                            start=(j == 0), stop=(j == 1))
                last.then_inc(l_scores, 1)

            def l_bcast(h):
                if h:
                    pe.wait_ge(l_decay, 2 * h)
                nc.tensor.matmul(PTB[:, 0:S], sel[:, h, :], negM[:, META:T], start=True, stop=True)
                nc.tensor.matmul(PTB[:, S:2 * S], sel[:, h, :], negFM[:, META:T], start=True, stop=True).then_inc(l_rows, 1)

            def l_pv(h):
                pe.wait_ge(l_probs, 3 * h + 3)
                if h:
                    pe.wait_ge(l_root, h)
                parts = ((0, P, Pl[:, 0:S], 0), (1, P, Pl[:, S:S + P], P), (2, META, Pl[0:META, 384:640], 0))
                for s, w, p, lo in parts:
                    nc.tensor.matmul(PTB[:, 512 + lo:512 + S], ones_1[0:w, :], p, start=(s == 0), stop=(s == 2))
                for v in range(4):
                    o = OB[v // 2][:, (v % 2) * S:(v % 2 + 1) * S]
                    for s, w, p, lo in parts:
                        c = 512 * h + v * P
                        last = nc.tensor.matmul(o[:, lo:S], lv[0:w, s, c:c + P], p, start=(s == 0), stop=(s == 2))
                last.then_inc(l_num, 1)

            def v_turn(m):
                wait_evacuated(pe, TILE["lv"] + m)
                if m >= 2:
                    pe.wait_ge(l_vcopied, m - 1)
                if m == 0:
                    pe.wait_ge(g_cols, 1)
                o = OB[m % 2]
                nc.tensor.transpose(o[:, 0:P], lvT[:, m % 2, META:META + P], ident[:, :])
                nc.tensor.transpose(o[:, P:2 * P], lvT[:, m % 2, META + P:T], ident[:, :])
                nc.tensor.transpose(o[0:META, 2 * P:3 * P], lvT[:, m % 2, 0:META], ident[:, :]).then_inc(l_vturned, 1)

            for m in range(E_TILES):
                chunk(CHUNK["lv"] + m, TILE["lv"] + m, xha, xla, T)
                if m >= 1:
                    v_turn(m - 1)
                if m == 2:
                    pe.wait_ge(g_rows, 3)
                    l_bcast(0)
                if m == 4:
                    l_qk(0)
            v_turn(E_TILES - 1)
            pe.wait_ge(l_vcopied, E_TILES)
            for h in range(LHEADS):
                l_pv(h)
                if h + 1 < LHEADS:
                    l_bcast(h + 1)
                    l_qk(h + 1)
                n, t = CHUNK["oz"] + 8 * h, TILE["oz"] + 8 * h
                chunk(n, t, xh, xl, S)
                pe.wait_ge(l_sq, h + 1)
                for v in range(4):
                    last = nc.tensor.matmul(PTB[:, 512:512 + S], ones_h[:, :], sqh[:, v, :], start=(v == 0), stop=(v == 3))
                last.then_inc(l_stat, 1)
                for m in range(1, 8):
                    chunk(n + m, t + m, xh, xl, S)
            for m in range(KT):
                for c in range(2):
                    chunk(CHUNK["lout"] + 2 * m + c, TILE["lout"] + m, a_hi, a_lo, S, k0=8 * c, total=E_TILES,
                          ready=(lambda k: pe.wait_ge(act_lo, 12 + FFN_TILES + E_TILES + k + 1)) if m == 0 else None)
            stat_x(NORM_FINAL, 5, S)

        @block.vector
        def _(dve):
            chain = Chain(dve, vec_steps)
            V = nc.vector

            def lo(n, i=0):
                dve.wait_ge(hi_ready, n + 1 + 4 * i)
                s = n % SLOTS
                V.tensor_tensor(w_lo[:, s, :], raw[:, s, :], w_hi[:, s, :].bitcast(F32), ALU.subtract).then_inc(lo_ready, 1)

            def ahead(n, i=0):
                if n + AHEAD < NCHUNKS:
                    lo(n + AHEAD, i)

            def reciprocal_root(e, a, src=root, dst=rstd):
                dve.wait_ge(root_ready, e + 1)
                chain.link(V.reciprocal(dst[:, a:T], src[:, a:T]))

            def apply_norm(pre, gain, a):
                def rest(k):
                    dve.wait_ge(normed_hi, 8 * pre + k + 1)
                    V.tensor_tensor(XL[:, k, a:T], SQ[:, k, a:T], XH[:, k, a:T].bitcast(F32), ALU.subtract).then_inc(normed_lo, 1)
                for k in range(KT):
                    V.scalar_tensor_tensor(out=SQ[:, k, a:T], in0=XR[:, k, a:T], scalar=col(gain, k), in1=rstd[:, a:T],
                                           op0=ALU.mult, op1=ALU.mult).then_inc(normed, 1)
                    if k:
                        rest(k - 1)
                rest(KT - 1)

            def add_post_norm(gain, update):
                dve.wait_ge(y_ready, 8 * update + 8)
                for k in range(KT):
                    chain.link(V.scalar_tensor_tensor(out=Y[:, k, META:T], in0=Y[:, k, META:T], scalar=col(gain, k),
                                                      in1=rstd[:, META:T], op0=ALU.mult, op1=ALU.mult))
                    V.tensor_tensor(XR[:, k, META:T], XR[:, k, META:T], Y[:, k, META:T], ALU.add).then_inc(x_updated, 1)

            V.memset(rb[32:33, :], MASKED).then_inc(consts_ready, 1)
            V.memset(small[:, 158:159], EPS).then_inc(consts_ready, 1)
            dve.wait_ge(mem_loaded, 16)
            V.tensor_tensor(KTm[:, :, :], mem_raw, mem_raw, ALU.mult).then_inc(mem_sq, 1)
            for n in range(AHEAD):
                lo(n)
            dve.wait_ge(params_loaded, 16)
            reciprocal_root(NORM_X, META)
            apply_norm(PRE_X, "g_mix_pre", META)
            dve.wait_ge(root_ready, 2)
            chain.link(V.reciprocal(rstd_m[:, 0:S], root_m[:, 0:S]))
            for k in range(KT):
                last = V.scalar_tensor_tensor(out=mem_raw[:, k, :], in0=mem_raw[:, k, :], scalar=col("g_mem_kv", k),
                                              in1=rstd_m[:, 0:S], op0=ALU.mult, op1=ALU.mult)
                if k < KT - 1:
                    chain.note(last)
            chain.wait()
            last.then_inc(mem_normed, 1)
            ahead(CHUNK["kc"])
            n, t = CHUNK["vc"], TILE["vc"]
            ahead(n)
            wait_chunk(dve, n)
            for g in range(GROUPS):
                src = acc(t)[g * HD:(g + 1) * HD, 0:S]
                chain.note(V.tensor_copy(KC2[0:HD, 1, g, :], src))
                last = V.tensor_copy(KC2[HD:P, 1, g, 0:S - 1], src[:, 1:S])
                if g == 0:
                    chain.note(last)
            freed(last, t)
            ahead(CHUNK["sgu_v"])
            dve.wait_ge(mem_hi, 1)
            V.tensor_tensor(ML[:, :, :], mem_raw, MH[:, :, :].bitcast(F32), ALU.subtract).then_inc(mem_lo, 1)
            ahead(CHUNK["sgu_v"] + 1)
            wait_evacuated(dve, TILE["kc"])
            wait_evacuated(dve, TILE["vc"])
            chain.wait()
            pos = col("cmp_pos", 0, 32).rearrange("p (a b) -> p a b", a=2)
            for v in range(2):
                for g in range(GROUPS):
                    src = KC2[:, v, g, :].rearrange("p (c l) -> p l c", l=CSTRIDE)
                    for half in range(2):
                        ks = slice(8 * half, 8 * half + 8)
                        chain.note(V.tensor_tensor(RF[:, v, ks, g, :], src[:, 0:CSTRIDE:2, half:half + NCMP],
                                                   pos[:, v, ks].unsqueeze(2).to_broadcast([P, 8, NCMP]), ALU.add))
            chain.wait()
            rf = RF[:, :, :, :, :].rearrange("p a b c d -> p (a b c d)")
            V.tensor_copy(AH[:, 2048:3008], rf).then_inc(cmp_in, 1)
            dve.wait_ge(cmp_in, 1)
            V.tensor_tensor(AL[:, 2048:3008], rf, AH[:, 2048:3008].bitcast(F32), ALU.subtract).then_inc(cmp_in, 1)
            ahead(CHUNK["sgu_u"])
            dve.wait_ge(cmp_bias, 1)
            V.tensor_copy(cb[:, :, :, :].rearrange("p a b c -> p (a b c)"), SC[:, 0:240]).then_inc(cb_copied, 1)
            for j in range(2):
                wait_evacuated(dve, TILE["sgu_v"] + j)
            for b in range(2):
                chain.note(V.bn_stats(stats[:, b, :], vg[:, b, :]))
            chain.wait()
            for b in range(2):
                last = V.bn_aggr(mv[:, b, :], stats[:, b, :])
                if b == 0:
                    chain.link(last)
            last.then_inc(sgu_var, 1)
            for c in range(CHUNK["sgu_u"] + 1, CHUNK["cmp"] + 4):
                ahead(c)
            n, t = CHUNK["vs"], TILE["vs"]
            ahead(n)
            wait_chunk(dve, n)
            freed(V.tensor_copy(Vtok[:, 0, :, :], acc(t)[:, 0:S].rearrange("p (a b) -> p a b", a=2)), t)
            dve.wait_ge(sgu_root, 1)
            chain.link(V.reciprocal(rs2, rs2))
            for b in range(2):
                chain.link(V.tensor_scalar(vn[:, b, :], vg[:, b, :], mv[:, b, 0:1], rs2[:, b:b + 1], ALU.subtract, ALU.mult))
                chain.link(V.tensor_tensor(vn[:, b, :], vn[:, b, :], col("sgu_g", 0, 256), ALU.mult))
                last = V.tensor_tensor(vn[:, b, :], vn[:, b, :], col("sgu_b", 0, 256), ALU.add)
                if b == 0:
                    chain.link(last)
            last.then_inc(sgu_normed, 1)
            n, t = CHUNK["vw"], TILE["vw"]
            ahead(n)
            wait_chunk(dve, n)
            freed(V.tensor_copy(Vtok[:, 1, :, :], acc(t)[:, 0:S].rearrange("p (a b) -> p a b", a=2)), t)
            dve.wait_ge(cmp_out, 1)
            V.tensor_scalar(kcmp[:, 0:NCMP], OB[0][:, 0:NCMP], col("cmp_b2k"), None, ALU.add).then_inc(cmp_kv, 1)
            for g in range(GROUPS):
                chain.note(V.tensor_tensor(vcmp[:, g, :], OB[0][:, 64 + g * HD:64 + (g + 1) * HD], col("cmp_b2v", 0, 64), ALU.add))
            chain.wait()
            dve.wait_ge(vx_zero, 1)
            for j in range(4):
                last = V.tensor_copy(VX[32 * j:32 * j + 32, :, j, :], vcmp[32 * j:32 * j + 32, :, :])
                if j < 3:
                    chain.note(last)
            chain.wait()
            last.then_inc(cmp_kv, 1)
            for j, name in enumerate(("ks", "kw")):
                n, t = CHUNK[name], TILE[name]
                ahead(n)
                wait_chunk(dve, n)
                freed(V.tensor_copy(kT[:, j, :], acc(t)[:, 0:S]), t)
            ahead(CHUNK["q"])
            ahead(CHUNK["q"] + 1)
            dve.wait_ge(sgu_mixed, 1)
            dve.wait_ge(sgu_normed, 1)
            sbias = col("sgu_bias", 0, 256).rearrange("p (a b) -> p a b", a=2)
            for j in range(2):
                last = V.tensor_tensor(vg[:, j, :].rearrange("p (n t) -> p n t", n=2), OB[1][:, j * S:(j + 1) * S].rearrange("p (n t) -> p n t", n=2),
                                       sbias[:, j, :].unsqueeze(1).to_broadcast([P, 2, P]), ALU.add)
                if j == 0:
                    chain.note(last)
            last.then_inc(sgu_mixed, 1)
            chain.wait()
            dve.wait_ge(sgu_mixed, 2)
            ahead(CHUNK["q"] + 2)
            ahead(CHUNK["q"] + 3)
            for j in range(2):
                wait_evacuated(dve, TILE["sgu_u"] + j)
            chain.link(V.tensor_tensor(vg[:, :, :], vg[:, :, :], uT[:, :, :], ALU.mult))
            ahead(CHUNK["gates"])
            dve.wait_ge(gate_turned, 1)
            chain.link(V.tensor_scalar(gtok[:, :, :], OB[1][:, 0:48].rearrange("p (a b) -> p a b", a=2), 1.0, None, ALU.add))
            chain.link(V.reciprocal(gtok[:, :, :], gtok[:, :, :]))
            V.sem_inc(gate_ready, 1) if False else None
            dve.wait_ge(pool_mixed, 1)
            for j in range(2):
                for r in range(2):
                    chain.note(V.tensor_scalar(t512[r * HD:(r + 1) * HD, j * S:(j + 1) * S],
                                               PTB[r * HD:(r + 1) * HD, r * 512 + j * S:r * 512 + (j + 1) * S],
                                               col("pool_scale", j)[r * HD:(r + 1) * HD], None, ALU.mult))
            chain.wait()
            V.memset(small[:, 156:157], 0.0).then_inc(pool_mixed, 1)
            dve.wait_ge(cs_ready, 1)
            for b in range(2):
                for g in range(GROUPS):
                    chain.note(V.tensor_tensor(Sc[:, b, 4 * g:4 * g + 4, :],
                                               SC[:, g * 512 + b * 60:g * 512 + (b + 1) * 60].rearrange("p (j c) -> p j c", j=4),
                                               cb[:, b, :, g:HEADS:2].rearrange("p c h -> p h c"), ALU.add))
            chain.wait()
            sc = Sc[:, :, :, :].rearrange("p b h c -> p (b h) c")
            chain.link(V.tensor_reduce(m16, sc, AX.X, ALU.max))
            chain.link(V.tensor_scalar(m16, m16, MASKED * 1e-10, None, ALU.max))
            V.tensor_tensor(sc, sc, m16.unsqueeze(2).to_broadcast([P, 16, NCMP]), ALU.subtract).then_inc(cs_shifted, 1)
            dve.wait_ge(cs_exp, 1)
            chain.link(V.tensor_reduce(s16, sc, AX.X, ALU.add))
            chain.link(V.tensor_scalar(s16, s16, 1.0, None, ALU.max))
            chain.link(V.reciprocal(s16, s16))
            gate = gtok[:, :, :].rearrange("p b (h r) -> p b h r", r=3)
            chain.link(V.tensor_tensor(s16.rearrange("p (b h) -> p b h", b=2), s16.rearrange("p (b h) -> p b h", b=2),
                                       gate[:, :, :, 0], ALU.mult))
            dve.wait_ge(pc_zero, 1)
            for b in range(2):
                last = V.tensor_tensor(Pc[:, b, :, :, 0:NCMP].rearrange("p g j c -> p (g j) c"), Sc[:, b, :, :],
                                       s16[:, 8 * b:8 * b + 8].unsqueeze(2).to_broadcast([P, 8, NCMP]), ALU.mult)
                if b == 0:
                    chain.link(last)
            last.then_inc(cp_ready, 1)

            def out_lo(j):
                dve.wait_ge(act_hi, j + 1)
                V.tensor_tensor(a_lo(j), OB[j % 2][:, 0:S], a_hi(j).bitcast(F32), ALU.subtract).then_inc(act_lo, 1)

            dve.wait_ge(bias_loaded, 16)
            for h in range(HEADS):
                n, t = CHUNK["mk"] + 2 * h, TILE["mk"] + 2 * h
                ahead(n)
                dve.wait_ge(scores, h + 1)
                if h:
                    dve.wait_ge(turned, h)
                chain.note(V.tensor_tensor(Sx[:, 0:S].rearrange("p (r s) -> p r s", r=2), SC[:, 0:S].rearrange("p (r s) -> p r s", r=2),
                                           bias[:, h, 127::-1].unsqueeze(1).to_broadcast([P, 2, P]), ALU.add))
                chain.link(V.tensor_tensor(Sx[:, S:768].rearrange("p (r s) -> p r s", r=2), SC[:, 512:1024].rearrange("p (r s) -> p r s", r=2),
                                           bias[:, h, 255::-1].unsqueeze(1).to_broadcast([P, 2, S]), ALU.add))
                chain.note(V.tensor_reduce(mx4[:, 0:2], Sx[:, 0:S].rearrange("p (r s) -> p r s", r=2), AX.X, ALU.max, negate=True))
                last = V.tensor_reduce(mx4[:, 2:4], Sx[:, S:768].rearrange("p (r s) -> p r s", r=2), AX.X, ALU.max, negate=True)
                chain.wait()
                last.then_inc(max_ready, 1)

                def evac(c):
                    wait_chunk(dve, n + c)
                    m = 2 * h + c
                    if m < KT:
                        freed(V.tensor_copy(KTm[:, m, :], acc(t + c)[:, 0:S]), t + c)
                    else:
                        freed(V.tensor_copy(VM[:, m - KT, :, :], acc(t + c)[:, 0:S].rearrange("p (a b) -> p a b", a=2)), t + c)

                evac(0)
                dve.wait_ge(exped, h + 1)
                chain.link(V.reciprocal(rc4, sm4))
                hh = 4 * (h % 2) + h // 2
                chain.link(V.tensor_tensor(rc4.rearrange("p (b r) -> p b r", b=2), rc4.rearrange("p (b r) -> p b r", b=2),
                                           gtok[:, :, 3 * hh + 1:3 * hh + 3], ALU.mult))
                for b in range(4):
                    a, w = (P * b, P) if b < 2 else (S * (b - 1), S)
                    last = V.tensor_scalar(Sx[:, a:a + w], Sx[:, a:a + w], rc4[:, b:b + 1], None, ALU.mult)
                    if b < 3:
                        chain.note(last)
                chain.wait()
                last.then_inc(probs, 1)
                ahead(n + 1)
                evac(1)
                if h >= 2 and h % 2 == 0:
                    out_lo(h // 2 - 1)
            out_lo(3)
            V.memset(small[:, 156:157], 0.0).then_inc(act_ready, 2)
            for j in range(2):
                dve.wait_ge(act_hi, 5 + j)
                V.tensor_tensor(a_lo(4 + j), t512[:, j * S:(j + 1) * S], a_hi(4 + j).bitcast(F32), ALU.subtract).then_inc(act_lo, 1)
            V.memset(small[:, 156:157], 0.0).then_inc(act_ready, 2)
            for j in range(2):
                dve.wait_ge(act_hi, 7 + j)
                V.tensor_tensor(a_lo(6 + j), vg[:, j, :], a_hi(6 + j).bitcast(F32), ALU.subtract).then_inc(act_lo, 1)
            for m in range(KT):
                ahead(CHUNK["w_out"] + m)
            reciprocal_root(NORM_MIX, META)
            add_post_norm("g_mix_post", 0)
            reciprocal_root(NORM_X1, META)
            apply_norm(PRE_X1, "g_mem_pre", META)

            def m_maximum(h):
                dve.wait_ge(m_scores, h + 1)
                V.tensor_reduce(small[:, 16 + 2 * h:18 + 2 * h], SC[:, (h % 2) * 512:(h % 2) * 512 + 512].rearrange("p (b m) -> p b m", b=2),
                                AX.X, ALU.max, negate=True).then_inc(m_max, 1)

            def m_normalise(h):
                dve.wait_ge(m_exped, h + 1)
                chain.link(V.reciprocal(small[:, 32 + 2 * h:34 + 2 * h], small[:, 24 + 2 * h:26 + 2 * h]))
                for b in range(2):
                    last = V.tensor_scalar(Em[:, h % 2, b, :], Em[:, h % 2, b, :], small[:, 32 + 2 * h + b:33 + 2 * h + b], None, ALU.mult)
                    if b == 0:
                        chain.link(last)
                last.then_inc(m_probs, 1)

            def m_lo(h):
                dve.wait_ge(act_hi, 8 + h + 1)
                V.tensor_tensor(AL[:, 2 * h * S:(2 * h + 2) * S], OB[h % 2][:, :], AH[:, 2 * h * S:(2 * h + 2) * S].bitcast(F32),
                                ALU.subtract).then_inc(act_lo, 1)

            for m in range(KT):
                ahead(CHUNK["mq"] + m)
                if m >= 3 and m % 2 == 1:
                    m_maximum((m - 3) // 2)
                    m_normalise((m - 3) // 2)
                if m == 7:
                    m_lo(0)
            m_maximum(3)
            m_normalise(3)
            for h in range(1, 4):
                m_lo(h)
            for m in range(KT):
                ahead(CHUNK["mo"] + m)
            reciprocal_root(NORM_MEMOUT, META)
            add_post_norm("g_mem_post", 1)
            reciprocal_root(NORM_X2, META)
            apply_norm(PRE_X2, "g_ffn_pre", META)
            taps = col("ffn_conv", 0, 176).rearrange("p (a b) -> p a b", b=8)

            def ffn_dve(i, hid, rest):
                for r in range(2):
                    for v in range(2):
                        n, t = CHUNK["up"] + 2 * r + v, TILE["up"] + 2 * r + v
                        ahead(n, i)
                        dst = (Gt, Vt)[v][:, r, :]
                        dve.wait_ge(f_init, 2 * r + v + 1 + 4 * i)
                        chain.link(V.scalar_tensor_tensor(out=dst[:, 1:S], in0=acc(t)[:, 0:S - 1], scalar=taps[:, 2 * i + r, 4 * v + 1:4 * v + 2],
                                                          in1=dst[:, 1:S], op0=ALU.mult, op1=ALU.add))
                        freed(V.scalar_tensor_tensor(out=dst[:, 2:S], in0=acc(t)[:, 0:S - 2], scalar=taps[:, 2 * i + r, 4 * v:4 * v + 1],
                                                     in1=dst[:, 2:S], op0=ALU.mult, op1=ALU.add), t)
                    dve.wait_ge(f_gelu, r + 1 + 2 * i)
                    wait_evacuated(dve, TILE["up"] + 2 * r + 1, i)
                    V.tensor_tensor(Ft[:, r, :], Gt[:, r, :], Vt[:, r, :], ALU.mult).then_inc(act_ready, 1)
                    dve.wait_ge(act_hi, 12 + r + 1 + 2 * i)
                    V.tensor_tensor(rest(i, r), Ft[:, r, :], hid(i, r).bitcast(F32), ALU.subtract).then_inc(act_lo, 1)

            for i in range(FFN_TILES // 2):
                ffn_dve(i, lambda i, r: ffn_hi(2 * i + r), lambda i, r: ffn_lo(2 * i + r))
            for c in range(24):
                ahead(CHUNK["down"] + c)
            reciprocal_root(NORM_FFN, META)
            add_post_norm("g_ffn_post", 2)
            reciprocal_root(NORM_H0, 0)
            apply_norm(PRE_H0, "g_conv", 0)
            ctaps = col("conv_taps", 0, 48).rearrange("p (a b) -> p a b", b=3)
            chain.link(V.memset(CX[:, 0:2], 0.0))
            base_ready, base_hi = 4 + FFN_TILES, 12 + FFN_TILES

            def conv_dve(i):
                n, t = CHUNK["conv_in"], TILE["conv_in"]
                ahead(n, i)
                ahead(n + 1, i)
                wait_chunk(dve, n + 1, i)
                wait_evacuated(dve, t, i)
                freed(V.tensor_tensor(CX[:, 2:T + 2], acc(t + 1)[:, 0:T], cT, ALU.mult), t + 1)
                wait_evacuated(dve, t + 1, i)
                chain.link(V.tensor_scalar(Yc, CX[:, 2:T + 2], ctaps[:, i, 2:3], None, ALU.mult))
                chain.link(V.scalar_tensor_tensor(out=Yc, in0=CX[:, 1:T + 1], scalar=ctaps[:, i, 1:2], in1=Yc, op0=ALU.mult, op1=ALU.add))
                chain.link(V.scalar_tensor_tensor(out=Yc, in0=CX[:, 0:T], scalar=ctaps[:, i, 0:1], in1=Yc, op0=ALU.mult, op1=ALU.add))
                ahead(n + 2, i)
                dve.wait_ge(c_sig, 1 + i)
                freed(V.tensor_tensor(ZZ, acc(t + 2)[:, 0:T], SZ, ALU.mult), t + 2)
                wait_evacuated(dve, t + 2, i)
                chain.link(V.tensor_tensor(Yc, Yc, ZZ, ALU.mult))
                ahead(n + 3, i)
                wait_chunk(dve, n + 3, i)
                freed(V.tensor_tensor(Fc, acc(t + 3)[:, 0:T], Yc, ALU.mult), t + 3)
                wait_evacuated(dve, t + 3, i)
                V.memset(small[:, 156:157], 0.0).then_inc(act_ready, 1)
                dve.wait_ge(act_hi, base_hi + 1 + i)
                V.tensor_tensor(a_lo(i, T), Fc, a_hi(i, T).bitcast(F32), ALU.subtract).then_inc(act_lo, 1)

            for i in range(E_TILES):
                conv_dve(i)
            for m in range(KT):
                n, t = CHUNK["conv_out"] + 2 * m, TILE["conv_out"] + m
                ahead(n)
                ahead(n + 1)
                wait_chunk(dve, n + 1)
                freed(V.tensor_tensor(XR[:, m, :], acc(t)[:, 0:T], XR[:, m, :], ALU.add), t)
            reciprocal_root(NORM_H1, 0)
            apply_norm(PRE_H1, "g_mlstm", 0)
            ahead(CHUNK["lgates"])
            chain.note(V.memset(gone[0:LHEADS, :], 1.0))
            wait_evacuated(dve, TILE["lgates"])
            chain.note(V.tensor_scalar(lf[32:36, :], gx[32:36, :], 0.0, None, ALU.min))
            chain.wait()
            dve.wait_ge(g_ln, 1)
            chain.link(V.tensor_tensor(lf[0:LHEADS, :], lf[32:36, :], gl[32:36, :], ALU.subtract))
            chain.link(V.tensor_tensor_scan(gF[0:LHEADS, :], gone[0:LHEADS, :], lf[0:LHEADS, :], 0.0, ALU.mult, ALU.add))
            V.tensor_tensor(gA[0:LHEADS, :], gx[0:LHEADS, :], gF[0:LHEADS, :], ALU.subtract).then_inc(g_rows, 1)
            dve.wait_ge(g_rows, 1)
            chain.link(V.tensor_tensor_scan(gM[0:LHEADS, :], gone[0:LHEADS, :], gA[0:LHEADS, :], 0.0, ALU.mult, ALU.max))
            V.tensor_scalar(negM, gM[0:LHEADS, :], -1.0, None, ALU.mult).then_inc(g_rows, 1)
            dve.wait_ge(g_rows, 2)
            V.tensor_tensor(negFM, negM, gF[0:LHEADS, :], ALU.subtract).then_inc(g_rows, 1)
            for m in range(KT):
                ahead(CHUNK["lk"] + m)
            dve.wait_ge(g_turned, 1)
            chain.note(V.tensor_copy(acol[0:META, 0, :], OB[0][0:META, 0:4]))
            last = V.tensor_copy(acol[:, 1:3, :], OB[0][:, 4:12].rearrange("p (a b) -> p a b", a=2))
            chain.wait()
            last.then_inc(g_cols, 1)
            for m in range(KT):
                ahead(CHUNK["lq"] + m)

            def l_weights(h):
                dve.wait_ge(l_scores, h + 1)
                dve.wait_ge(l_masked, 2 * h + 2)
                if h:
                    dve.wait_ge(z_sig, 4 * h)
                V.tensor_tensor(Pl[:, 0:S], SC[:, 0:S], Dl[:, 0:S], ALU.mult).then_inc(l_probs, 1)
                V.tensor_tensor(Pl[:, S:S + P], SC[:, S:S + P], Dl[:, S:S + P], ALU.mult).then_inc(l_probs, 1)
                V.tensor_tensor(Pl[0:META, 384:640], SC[0:META, 512:512 + S], Dl[0:META, 384:640], ALU.mult).then_inc(l_probs, 1)

            def v_copy(m):
                dve.wait_ge(l_vturned, m + 1)
                o = OB[m % 2]
                c = slice(m * P, (m + 1) * P)
                chain.note(V.tensor_copy(lv[0:META, 2, c], o[0:META, 2 * P:3 * P]))
                last = V.tensor_copy(lv[:, 0:2, c], o[:, 0:2 * P].rearrange("p (a b) -> p a b", a=2))
                chain.wait()
                last.then_inc(l_vcopied, 1)

            for m in range(E_TILES):
                ahead(CHUNK["lv"] + m)
                if m >= 2:
                    v_copy(m - 2)
                if m == 6:
                    l_weights(0)
            v_copy(E_TILES - 2)
            v_copy(E_TILES - 1)
            base_ready, base_hi = 4 + FFN_TILES + E_TILES, 12 + FFN_TILES + E_TILES
            for h in range(LHEADS):
                n, t = CHUNK["oz"] + 8 * h, TILE["oz"] + 8 * h
                dve.wait_ge(l_num, h + 1)
                dve.wait_ge(l_decay, 2 * h + 2)
                if h:
                    dve.wait_ge(act_hi, base_hi + 4 * h)
                chain.link(V.scalar_tensor_tensor(out=rden, in0=PTB[:, 512:512 + S], scalar=-1.0, in1=em, op0=ALU.mult, op1=ALU.max))
                chain.link(V.tensor_tensor(rden, PTB[:, 512:512 + S], rden, ALU.max))
                chain.link(V.reciprocal(rden, rden))
                for v in range(2):
                    last = V.tensor_tensor(hn[:, 2 * v:2 * v + 2, :], OB[v][:, :].rearrange("p (a b) -> p a b", a=2),
                                           rden.unsqueeze(1).to_broadcast([P, 2, S]), ALU.mult)
                    if v == 0:
                        chain.link(last)
                last.then_inc(l_hn, 1)
                ahead(n)
                dve.wait_ge(l_root, h + 1)
                chain.link(V.reciprocal(rhead, lroot))
                chain.link(V.tensor_tensor(hn[:, :, :], hn[:, :, :], rhead.unsqueeze(1).to_broadcast([P, 4, S]), ALU.mult))
                for m in range(1, 4):
                    ahead(n + m)
                for m in range(4):
                    e = 4 * h + m
                    ahead(n + 4 + m)
                    wait_evacuated(dve, t + m)
                    chain.link(V.scalar_tensor_tensor(out=hn[:, m, :], in0=hn[:, m, :], scalar=col("head_norm", e), in1=so[:, m, :],
                                                      op0=ALU.mult, op1=ALU.mult))
                    dve.wait_ge(z_sig, e + 1)
                    chain.link(V.tensor_tensor(hn[:, m, :], hn[:, m, :], tz, ALU.mult))
                    freed(V.tensor_tensor(hn[:, m, :], acc(t + 4 + m)[:, 0:S], hn[:, m, :], ALU.mult), t + 4 + m)
                    wait_evacuated(dve, t + 4 + m)
                    V.memset(small[:, 156:157], 0.0).then_inc(act_ready, 1)
                    dve.wait_ge(act_hi, base_hi + e + 1)
                    V.tensor_tensor(a_lo(e), hn[:, m, :], a_hi(e).bitcast(F32), ALU.subtract).then_inc(act_lo, 1)
                if h + 1 < LHEADS:
                    l_weights(h + 1)
            for m in range(KT):
                n, t = CHUNK["lout"] + 2 * m, TILE["lout"] + m
                ahead(n)
                ahead(n + 1)
                wait_chunk(dve, n + 1)
                freed(V.tensor_tensor(XR[:, m, META:T], acc(t)[:, 0:S], XR[:, m, META:T], ALU.add), t)
            reciprocal_root(NORM_FINAL, META)
            for k in range(KT):
                V.scalar_tensor_tensor(out=SQ[:, k, META:T], in0=XR[:, k, META:T], scalar=col("g_final", k), in1=rstd[:, META:T],
                                       op0=ALU.mult, op1=ALU.mult).then_inc(normed, 1)


def _tiles(np, w, cols):
    k = w.shape[0] // P
    return w[:, cols].reshape(k, P, len(cols)).transpose(1, 0, 2).reshape(P, -1)


def _pack_weights(np, a):
    ar = np.arange

    def lin(w):
        return [_tiles(np, w, ar(m * P, (m + 1) * P)) for m in range(w.shape[1] // P)]

    def pad(c):
        return np.concatenate([c, np.zeros((P, D - c.shape[1]), c.dtype)], axis=1)

    def narrow(w, at):
        out = np.zeros((D, P), w.dtype)
        out[:, at] = w
        return _tiles(np, out, ar(P))

    def deep(w):
        rows = [w[r:r + D] for r in range(0, w.shape[0], D)]
        return [pad(_tiles(np, r, ar(m * P, (m + 1) * P))) for m in range(KT) for r in rows]

    w = a["w_in"][0]
    q, kc, vc, ks, vs, kw, vw, gt, pin, u, v = np.split(w, np.cumsum([512] + [128] * 6 + [24, 256, 256]), axis=1)
    pairs = [np.concatenate([ar(j * HD, (j + 1) * HD), ar((j + 4) * HD, (j + 5) * HD)]) for j in range(4)]
    parts = lin(kc) + lin(vc) + lin(v) + lin(u) + lin(pin)
    for kv in range(2):
        parts += [_tiles(np, a["cmp_w1"][0, kv].reshape(2048, P)[r:r + D], ar(P)) for r in (0, D)]
    parts += lin(vs) + lin(vw) + lin(ks) + lin(kw) + [_tiles(np, q, p) for p in pairs] + [narrow(gt, ar(24))]
    parts += lin(a["w_mk"][0]) + lin(a["w_mv"][0])
    rows = np.concatenate(pairs + [ar(512, 1024)])
    parts += lin(a["w_out"][0][rows]) + lin(a["w_mq"][0]) + lin(a["w_mo"][0])
    up = a["w_up"][0]
    for j in range(FFN_TILES):
        parts += [_tiles(np, up, ar(c, c + P)) for c in (j * P, (FFN_TILES + j) * P)]
    parts += deep(a["w_down"][0])
    cin = a["conv_in_w_2"][0]
    for e in range(E_TILES):
        for part in (1, 2, 3, 0):
            parts.append(_tiles(np, cin, ar(part * 2048 + e * P, part * 2048 + (e + 1) * P)))
    parts += deep(a["conv_out_w_2"][0])
    lq, lk, lv, lo, lz, lg = np.split(a["mlstm_in_w_2"][0], [1024, 2048, 4096, 6144, 8192], axis=1)
    parts += [narrow(lg, np.concatenate([ar(4), ar(32, 36)]))] + lin(lk) + lin(lq) + lin(lv)
    o, z = lin(lo), lin(lz)
    for h in range(LHEADS):
        parts += o[4 * h:4 * h + 4] + z[4 * h:4 * h + 4]
    parts += deep(a["mlstm_out_w_2"][0])
    out = np.stack(parts)
    assert out.shape == (NCHUNKS, P, D)
    return out


def _pack_params(np, a):
    def cols(v):
        return v.reshape(-1, P).T

    def rows(v):
        return np.broadcast_to(v[None, :], (P, v.shape[0]))

    f = {}
    for name, key in (("g_mix_pre", "mix_norm_pre"), ("g_mix_post", "mix_norm_post"), ("g_mem_pre", "mem_norm_pre"),
                      ("g_mem_kv", "mem_norm_kv"), ("g_mem_post", "mem_norm_post"), ("g_ffn_pre", "ffn_norm_pre"),
                      ("g_ffn_post", "ffn_norm_post"), ("pool_scale", "pool_scale"), ("cmp_b1", "cmp_b1")):
        f[name] = cols(a[key][0])
    f["g_conv"], f["g_mlstm"] = cols(a["norm_w_2"][0]), cols(a["norm_w_2"][1])
    f["g_final"] = cols(a["final_norm_w_2"])
    f["cmp_b2k"] = np.concatenate([a["cmp_b2"][0, 0]] * 2)[:, None]
    f["cmp_b2v"] = rows(a["cmp_b2"][0, 1])
    f["cmp_pos"] = a["cmp_pos"][0].reshape(2, 16, P).transpose(2, 0, 1).reshape(P, 32)
    f["cmp_w2"] = a["cmp_w2"][0].transpose(1, 0, 2).reshape(P, 128)
    f["sgu_g"], f["sgu_b"] = rows(a["sgu_norm_g"][0]), rows(a["sgu_norm_b"][0])
    sb = a["sgu_b"][0]
    f["sgu_bias"] = np.concatenate([np.repeat(sb[2 * j:2 * j + 2], HD, axis=0) for j in range(2)], axis=1)
    f["sgu_w"] = a["sgu_w"][0].transpose(2, 0, 1).reshape(P, 512)
    pw = a["pool_w"][0]
    f["pool_w"] = np.concatenate([pw[0:2].reshape(P, HD), pw[2:4].reshape(P, HD)], axis=1)
    tokens = np.arange(S)
    inv = [1.0 / np.minimum(tokens + 1, w) for w in (2, 4, 8, 16)]
    f["pool_inv"] = np.concatenate([np.repeat(np.stack(inv[2 * j:2 * j + 2]), HD, axis=0) for j in range(2)], axis=1).astype(np.float32)
    cw, cbias = a["conv_w"][0], a["conv_b"][0]
    four = np.concatenate([cw, cbias[None]], axis=0).reshape(4, 2, FFN_TILES, P)
    f["ffn_conv"] = four.transpose(3, 2, 1, 0).reshape(P, 176)
    f["conv_taps"] = a["conv_w_2"][0].reshape(3, E_TILES, P).transpose(2, 1, 0).reshape(P, 48)
    f["head_norm"] = cols(a["mlstm_head_norm_w_2"][0])
    gb = np.zeros((P, 1), np.float32)
    gb[0:4, 0], gb[32:36, 0] = a["mlstm_gate_b_2"][0][0:4], a["mlstm_gate_b_2"][0][4:8]
    f["gate_b"] = gb
    return np.concatenate([f[name] for name, _ in _COLS], axis=1)


def _onehot(np):
    import math
    d = np.arange(512) - 256
    n = np.maximum(d, 1).astype(np.float32)
    large = 16 + (np.log(n / np.float32(16)) / np.float32(math.log(64.0)) * np.float32(16)).astype(np.int32)
    bucket = np.where(d < 16, d, np.minimum(large, 31))
    bucket = np.where(d < 0, 32, bucket)
    return (np.arange(33)[:, None] == bucket[None, :]).astype(np.float32)


def kernel(**inputs):
    import numpy as np
    import concourse.bacc as bacc
    from concourse.bass_utils import run_bass_kernel_spmd as run

    a = {k: np.asarray(v) for k, v in inputs.items()}
    order = [j + 4 * g for j in range(4) for g in range(2)]

    def feature_major(v):
        return v.T.reshape(KT, P, -1).transpose(1, 0, 2)

    arrays = {
        "weights": _pack_weights(np, a),
        "x_t": feature_major(a["x"][0]),
        "mem_t": feature_major(a["mem"][0]),
        "meta_t": feature_major(a["meta_tokens_2"]),
        "params": _pack_params(np, a),
        "rel_bias": a["rel_bias"][:, order],
        "onehot": _onehot(np),
    }
    arrays = {k: np.ascontiguousarray(v) for k, v in arrays.items()}
    nc = bacc.Bacc("TRN2", target_bir_lowering=False, num_devices=1)
    args = [nc.dram_tensor(k, v.shape, F32, kind="ExternalInput").ap() for k, v in arrays.items()]
    out = nc.dram_tensor("out_t", (D, S), F32, kind="ExternalOutput").ap()
    bias_rows = nc.dram_tensor("bias_rows", (HEADS, 512), F32, kind="Internal").ap()
    build(nc, *args, out, bias_rows)
    r = run(nc, [arrays], core_ids=[0])
    return np.ascontiguousarray(r.results[0]["out_t"].T)[None]
```

```python
from contextlib import ExitStack

import concourse.bass as bass
from concourse import mybir

F32 = mybir.dt.float32
F32R = mybir.dt.float32r
ALU = mybir.AluOpType
ACT = mybir.ActivationFunctionType
AX = mybir.AxisListType

P = 128
S = 256
META = 16
T = META + S
D = 1024
KT = D // P
HEADS, GROUPS, HD = 8, 2, 64
NCMP = 15
CSTRIDE = 16
CMP_BIASES = NCMP + P // CSTRIDE
FFN_TILES = 22
E_TILES = 16
MEM_HEADS = 4
LHEADS = 4
EPS = 1e-6
MASKED = -1.0e30

SLOTS = 4
AHEAD = SLOTS - 1
_LAYOUT = [("kc", 1), ("vc", 1), ("sgu_v", 2), ("sgu_u", 2), ("cmp", 4), ("vsw", 2), ("pool", 2),
           ("ks", 1), ("kw", 1), ("q", 4), ("gates", 1), ("mk", 8), ("mv", 8), ("w_out", 8), ("mq", 8),
           ("mo", 8), ("up", 44), ("down", 24), ("conv_in", 64), ("conv_out", 16), ("lgates", 1), ("lk", 8),
           ("lq", 8), ("lv", 16), ("oz", 32), ("lout", 16)]
CHUNK = {}
NCHUNKS = 0
for _name, _n in _LAYOUT:
    CHUNK[_name] = NCHUNKS
    NCHUNKS += _n
_TILES = dict(sgu_v=1, cmp=1, vsw=1, mv=4, down=8, conv_out=8, lout=8)
TILE = {}
_t = 0
for _name, _n in _LAYOUT:
    TILE[_name] = _t
    _t += _TILES.get(_name, _n)

_COLS = [("g_mix_pre", 8), ("g_mix_post", 8), ("g_mem_pre", 8), ("g_mem_kv", 8), ("g_mem_post", 8),
         ("g_ffn_pre", 8), ("g_ffn_post", 8), ("g_conv", 8), ("g_mlstm", 8), ("g_final", 8),
         ("pool_scale", 2), ("cmp_b1", 2), ("cmp_b2k", 1), ("cmp_b2v", 64), ("cmp_pos", 32), ("cmp_w2", 128),
         ("sgu_g", 256), ("sgu_b", 256), ("sgu_bias", 256), ("sgu_w", 512), ("pool_w", 128), ("pool_inv", 512),
         ("ffn_conv", 176), ("conv_taps", 48), ("head_norm", 16), ("gate_b", 1)]
COL = {}
NCOLS = 0
for _name, _n in _COLS:
    COL[_name] = NCOLS
    NCOLS += _n
GAINS = COL["pool_scale"]

NORM_X, NORM_MEM, NORM_MIX, NORM_X1, NORM_MEMOUT, NORM_X2, NORM_FFN, NORM_H0, NORM_H1, NORM_FINAL = range(10)
PRE_X, PRE_H1 = range(2)
RAW_X1, RAW_X2, RAW_H0, RAW_H1 = range(4)
ACT_MEM = 8
SQ_H1, SQ_FINAL = 32, 40
WARM = 28
POOL_FROM = 6


class Chain:

    def __init__(self, eng, sem):
        self.eng, self.sem, self.count = eng, sem, 0

    def note(self, ins):
        ins.then_inc(self.sem, 1)
        self.count += 1
        return ins

    def wait(self):
        self.eng.wait_ge(self.sem, self.count)

    def link(self, ins):
        self.note(ins)
        self.wait()


def build(nc, weights, x_in, mem_in, meta_in, params, rel_bias, onehot, out, bias_rows):
    with ExitStack() as ctx:
        def sb(name, shape, dt=F32):
            return ctx.enter_context(nc.sbuf_tensor(name, shape, dt))

        def sem(name):
            return ctx.enter_context(nc.semaphore(name))

        def psum(name, cols):
            return ctx.enter_context(nc.psum_tensor(name, [P, cols], F32))

        raw = sb("raw", [P, SLOTS, D])
        w_hi = sb("w_hi", [P, SLOTS, D], F32R)
        w_lo = sb("w_lo", [P, SLOTS, D], F32R)
        XR = sb("XR", [P, KT, T])
        XH = sb("XH", [P, KT, T], F32R)
        XL = sb("XL", [P, KT, T], F32R)
        MH = sb("MH", [P, KT, S], F32R)
        ML = sb("ML", [P, KT, S], F32R)
        AH = sb("AH", [P, E_TILES * T], F32R)
        AL = sb("AL", [P, E_TILES * T], F32R)
        cst = sb("cst", [P, NCOLS])
        ident = sb("ident", [P, P])
        ones_d = sb("ones_d", [P, P])
        ones_h = sb("ones_h", [P, P])
        ones_1 = sb("ones_1", [P, P])
        Y = sb("Y", [P, KT, T])
        SQ = sb("SQ", [P, KT, T])
        root = sb("root", [P, T])
        rstd = sb("rstd", [P, T])
        root_m = sb("root_m", [P, T])
        rstd_m = sb("rstd_m", [P, T])
        rb = sb("rb", [33, HEADS])
        sel = sb("sel", [LHEADS, LHEADS, P])
        small = sb("small", [P, 160])
        AR = sb("AR", [P, 12200])

        def col(name, i=0, w=1):
            return cst[:, COL[name] + i:COL[name] + i + w]

        def ar(off, *dims):
            n = 1
            for d in dims:
                n *= d
            v = AR[:, off:off + n]
            if len(dims) == 1:
                return v
            if len(dims) == 2:
                return v.rearrange("p (a b) -> p a b", a=dims[0])
            if len(dims) == 3:
                return v.rearrange("p (a b c) -> p a b c", a=dims[0], b=dims[1])
            return v.rearrange("p (a b c d) -> p a b c d", a=dims[0], b=dims[1], c=dims[2])

        bias = ar(0, HEADS, S)
        Sx = ar(2048, 768)
        PTx = ar(2816, 2, 384)
        RF = ar(2048, 16, 2, 2, 16)
        KC2 = ar(3584, 2, GROUPS, S)
        Pc = ar(3584, 2, 2, 4, 32)
        PcT = ar(4096, GROUPS, S)
        qT = ar(4608, 4, S)
        kT = ar(5632, 2, S)
        Vtok = ar(6144, 2, 2, P)
        VX = ar(6656, GROUPS, 4, HD)
        hc = ar(7168, GROUPS, 4, 32)
        hk = ar(7424, 32)
        kcmp = ar(7456, 16)
        vcmp = ar(7472, GROUPS, HD)
        cb = ar(7600, CMP_BIASES, HEADS)
        Sc = ar(7840, 2, HEADS, NCMP)
        gT = ar(8080, S)
        gtok = ar(8336, 2, 24)
        m16 = ar(8384, 16)
        s16 = ar(8400, 16)
        KTm = ar(8448, KT, S)
        VM = ar(0, KT, 2, P)
        hot = ar(10496, 512)
        vec = ar(11008, 512)
        stats = ar(11520, 2, 6)
        mv = ar(11532, 2, 2)
        rs2 = ar(11536, 2)
        mx4 = ar(11540, 4)
        sm4 = ar(11544, 4)
        rc4 = ar(11548, 4)
        t512 = ar(11552, 512)
        ch = ar(4096, S)
        SS = sb("SS", [P, T])
        sqv = SQ[:, :, :].rearrange("p a b -> p (a b)")
        uT = sqv[:, 0:512].rearrange("p (a b) -> p a b", a=2)
        vg = sqv[:, 512:1024].rearrange("p (a b) -> p a b", a=2)
        vn = sqv[:, 1024:1536].rearrange("p (a b) -> p a b", a=2)
        yv = Y[:, :, :].rearrange("p a b -> p (a b)")
        pT = yv[:, 0:544].rearrange("p (a b) -> p a b", a=2)
        wA = yv[:, 544:1088].rearrange("p (a b) -> p a b", a=2)
        wB = yv[:, 1088:1632].rearrange("p (a b) -> p a b", a=2)
        pd = yv[:, 1632:2144].rearrange("p (a b) -> p a b", a=2)
        mem_raw = yv[:, 0:2048].rearrange("p (a b) -> p a b", a=KT)
        qM = ar(4608, KT, S)
        Em = ar(2048, 2, 2, S)
        PTm = ar(3072, 2, 2, S)
        Gt = ar(0, 2, S)
        Vt = ar(512, 2, S)
        Ft = ar(1024, 2, S)
        Ut = ar(1536, 2, S)
        cT = ar(0, T)
        CX = ar(512, T + 2)
        SZ = ar(1024, T)
        ZZ = ar(1536, T)
        Yc = ar(2048, T)
        Fc = ar(2560, T)
        rstd2 = ar(3072, T)
        lk = yv.rearrange("p (a b) -> p a b", a=KT)
        lq = sqv[:, 0:2048].rearrange("p (a b) -> p a b", a=KT)
        lv = ar(0, 3, 2048)
        so = ar(6144, 4, S)
        hn = ar(7168, 4, S)
        sqh = ar(8192, 4, S)
        Pl = ar(9216, 640)
        Dl = ar(9856, 640)
        em = ar(10496, S)
        rden = ar(10752, S)
        rhead = ar(11008, S)
        lroot = ar(11264, S)
        lvT = ar(11520, 2, T)
        tz = ar(11520, 2, S)
        gx = ar(6144, T)
        ge = ar(6416, T)
        gl = ar(6688, T)
        gF = ar(6960, T)
        gA = ar(7232, T)
        gM = ar(7504, T)
        gone = ar(7776, T)
        lf = ar(8048, T)
        negM = root_m[0:LHEADS, :]
        negFM = rstd_m[0:LHEADS, :]
        acol = small[:, 0:12].rearrange("p (a b) -> p a b", a=3)

        ACC = [psum("acc0", 512), psum("acc1", 512)]
        SC = psum("scores", 1024)
        PTB = psum("turned", 1024)
        OB = [psum("outs0", 512), psum("outs1", 512)]

        x_loaded = [sem("x_loaded0"), sem("x_loaded1")]
        meta_loaded, mem_loaded, params_loaded, gains_loaded = sem("meta_loaded"), sem("mem_loaded"), sem("params_loaded"), sem("gains_loaded")
        rf_zero, sum_ready, cmp_hidden, cmp_copied, rest_pool, x_updated_pool = (
            sem("rf_zero"), sem("sum_ready"), sem("cmp_hidden"), sem("cmp_copied"), sem("rest_pool"), sem("x_updated_pool"))
        rel_loaded = sem("rel_loaded")
        bias_stored, bias_loaded, out_stored = sem("bias_stored"), sem("bias_loaded"), sem("out_stored")
        weights_loaded = [sem(f"weights_loaded{s}") for s in range(SLOTS)]
        hi_ready, lo_ready, chunk_done = sem("hi_ready"), sem("lo_ready"), sem("chunk_done")
        evacuated = [sem("evacuated0"), sem("evacuated1")]
        consts_ready = sem("consts_ready")
        sgu_masked = sem("sgu_masked")
        sq_ready, stat_ready, root_ready = sem("sq_ready"), sem("stat_ready"), sem("root_ready")
        mem_sq = sem("mem_sq")
        raw_hi, raw_lo, squared_rstd, u_tapped = sem("raw_hi"), sem("raw_lo"), sem("squared_rstd"), sem("u_tapped")
        c_conv, c_scaled = sem("c_conv"), sem("c_scaled")
        normed, normed_hi, normed_lo = sem("normed"), sem("normed_hi"), sem("normed_lo")
        mem_normed, mem_hi, mem_lo = sem("mem_normed"), sem("mem_hi"), sem("mem_lo")
        rstd_ready = sem("rstd_ready")
        y_ready, x_updated = sem("y_ready"), sem("x_updated")
        act_ready, act_hi, act_lo = sem("act_ready"), sem("act_hi"), sem("act_lo")
        bias_vec, bias_copied = sem("bias_vec"), sem("bias_copied")
        cmp_bias = sem("cmp_bias")
        cmp_in = sem("cmp_in")
        cmp_out, cmp_kv = sem("cmp_out"), sem("cmp_kv")
        cb_copied, pc_zero, hc_zero, vx_zero = sem("cb_copied"), sem("pc_zero"), sem("hc_zero"), sem("vx_zero")
        sgu_var, sgu_root, sgu_normed, sgu_mixed = sem("sgu_var"), sem("sgu_root"), sem("sgu_normed"), sem("sgu_mixed")
        pool_padded, pool_diff, pool_mixed, pool_scaled = sem("pool_padded"), sem("pool_diff"), sem("pool_mixed"), sem("pool_scaled")
        sgu_gated = sem("sgu_gated")
        gate_turned, gate_ready = sem("gate_turned"), sem("gate_ready")
        cs_ready, cs_shifted, cs_exp, cp_ready, cp_turned, cp_copied = (
            sem("cs_ready"), sem("cs_shifted"), sem("cs_exp"), sem("cp_ready"), sem("cp_turned"), sem("cp_copied"))
        scores, max_ready, exped, probs, turned, copied, outs = (
            sem("scores"), sem("max_ready"), sem("exped"), sem("probs"), sem("turned"), sem("copied"), sem("outs"))
        m_scores, m_max, m_exped, m_probs, m_turned, m_copied, m_outs = (
            sem("m_scores"), sem("m_max"), sem("m_exped"), sem("m_probs"), sem("m_turned"), sem("m_copied"), sem("m_outs"))
        f_init, f_gelu = sem("f_init"), sem("f_gelu")
        c_sig, cx_zero = sem("c_sig"), sem("cx_zero")
        g_raw, g_abs, g_ln, g_rows, g_turned, g_cols = (
            sem("g_raw"), sem("g_abs"), sem("g_ln"), sem("g_rows"), sem("g_turned"), sem("g_cols"))
        l_vturned, l_vcopied = sem("l_vturned"), sem("l_vcopied")
        l_scores, l_rows, l_decay, l_masked, l_probs, l_num, l_hn, l_sq, l_stat, l_root, l_rhead = (
            sem("l_scores"), sem("l_rows"), sem("l_decay"), sem("l_masked"), sem("l_probs"), sem("l_num"),
            sem("l_hn"), sem("l_sq"), sem("l_stat"), sem("l_root"), sem("l_rhead"))
        o_sig, z_sig = sem("o_sig"), sem("z_sig")
        vec_steps, act_steps, pool_steps = sem("vec_steps"), sem("act_steps"), sem("pool_steps")

        def acc(t):
            return ACC[t % 2]

        def wait_evacuated(eng, t, i=0):
            eng.wait_ge(evacuated[t % 2], t // 2 + 1 + 2 * i)

        def wait_chunk(eng, n, i=0):
            eng.wait_ge(chunk_done, n + 1 + 4 * i)

        def freed(ins, t):
            ins.then_inc(evacuated[t % 2], 1)

        def a_hi(k, w=S):
            return AH[:, k * w:(k + 1) * w]

        def a_lo(k, w=S):
            return AL[:, k * w:(k + 1) * w]

        def wait_rstd(eng, e):
            eng.wait_ge(rstd_ready, max(e, 1))

        def raw_parts(lo):
            return (lambda k: XH[:, k, lo:T]), (lambda k: XL[:, k, lo:T])

        def l_in(part, lo):
            return lambda k: part[:, (8 + k) * T + lo:(9 + k) * T]

        def l_out(part, k):
            if k < 8:
                return (XH if part is AH else XL)[:, k, 0:S]
            return (MH if part is AH else ML)[:, k - 8, :]

        def ffn_hi(k):
            return a_hi(k) if k < 16 else MH[:, k - 16, :]

        def ffn_lo(k):
            return a_lo(k) if k < 16 else ML[:, k - 16, :]

        block = ctx.enter_context(nc.Block())

        @block.sync
        def _(sp):
            sp.dma_start(rb[0:32, :], rel_bias).then_inc(rel_loaded, 16)
            sp.dma_start(hot[0:33, :], onehot).then_inc(rel_loaded, 16)
            for c in range(2):
                sp.dma_start(XR[:, 4 * c:4 * c + 4, META:T], x_in[:, 4 * c:4 * c + 4, :]).then_inc(x_loaded[c], 16)
            sp.dma_start(cst[:, 0:GAINS], params[:, 0:GAINS]).then_inc(gains_loaded, 16)

            def load(n, i=0):
                if n >= SLOTS:
                    sp.wait_ge(lo_ready, n - SLOTS + 1 + 4 * i)
                sp.dma_start(raw[:, n % SLOTS, :], weights[n + 4 * i]).then_inc(weights_loaded[n % SLOTS], 16)

            load(0)
            sp.dma_start(mem_raw, mem_in).then_inc(mem_loaded, 16)
            load(1)
            load(2)
            sp.dma_start(cst[:, GAINS:NCOLS], params[:, GAINS:NCOLS]).then_inc(params_loaded, 16)
            load(3)
            sp.dma_start(XR[:, :, 0:META], meta_in).then_inc(meta_loaded, 16)
            rounds = (NCHUNKS - SLOTS) // SLOTS
            with sp.Fori(0, rounds) as i:
                for s in range(SLOTS):
                    load(SLOTS + s, i)
            for n in range(SLOTS * (rounds + 1), NCHUNKS):
                load(n)
            for k in range(KT):
                sp.wait_ge(normed, 8 * 2 + k + 1)
                sp.dma_start(out[k * P:(k + 1) * P, :], SQ[:, k, META:T]).then_inc(out_stored, 16)
            sp.wait_ge(out_stored, 16 * KT)

        @block.gpsimd
        def _(pool):
            chain = Chain(pool, pool_steps)

            def sum_squares(ready, lo):
                ready(0)
                for m in range(1, KT - 1):
                    ready(m)
                    ins = nc.gpsimd.tensor_tensor(SS[:, lo:T], SQ[:, 0, lo:T] if m == 1 else SS[:, lo:T], SQ[:, m, lo:T], ALU.add)
                    if m < KT - 2:
                        chain.link(ins)
                ins.then_inc(sum_ready, 1)

            def rest(pre, lo, h, l):
                for k in range(1, KT, 2):
                    pool.wait_ge(normed_hi, 8 * pre + k + 1)
                    nc.gpsimd.tensor_tensor(l(k), SQ[:, k, lo:T], h(k).bitcast(F32), ALU.subtract).then_inc(rest_pool, 1)

            nc.gpsimd.memset(ones_d[:, :], 1.0 / D).then_inc(consts_ready, 1)
            nc.gpsimd.memset(ones_h[:, :], 1.0 / 512).then_inc(consts_ready, 1)
            nc.gpsimd.memset(ones_1[:, :], 1.0).then_inc(consts_ready, 1)
            chain.link(nc.gpsimd.memset(ident[:, :], 0.0))
            chain.link(nc.gpsimd.memset(sel[:, :, :], 0.0))
            nc.gpsimd.affine_select(out=ident[:, :], in_=ident[:, :], compare_op=ALU.not_equal, fill=1.0, base=0,
                                    pattern=[[-1, P]], channel_multiplier=1).then_inc(consts_ready, 1)
            nc.gpsimd.affine_select(out=sel[:, :, :], in_=sel[:, :, :], compare_op=ALU.not_equal, fill=1.0, base=0,
                                    pattern=[[-1, LHEADS], [0, P]], channel_multiplier=1).then_inc(consts_ready, 1)
            pool.wait_ge(consts_ready, 7)
            pool.wait_ge(mem_loaded, 16)
            nc.gpsimd.tensor_tensor(KTm[:, :, :], mem_raw, mem_raw, ALU.mult).then_inc(mem_sq, 1)
            nc.gpsimd.memset(AR[:, 2048:3072], 0.0).then_inc(rf_zero, 1)
            rest(PRE_X, META, *raw_parts(META))
            nc.gpsimd.memset(hc[:, :, :, :], 0.0).then_inc(hc_zero, 1)
            nc.gpsimd.memset(VX[:, :, :, :], 0.0).then_inc(vx_zero, 1)
            pool.wait_ge(params_loaded, 16)
            sw = col("sgu_w", 0, 512).rearrange("p (h t) -> p h t", h=4)
            nc.gpsimd.affine_select(out=sw, in_=sw, compare_op=ALU.is_ge, fill=0.0, base=0,
                                    pattern=[[0, 4], [1, P]], channel_multiplier=-1).then_inc(sgu_masked, 1)
            pool.wait_ge(cmp_in, 1)
            nc.gpsimd.memset(AR[:, 3584:4096], 0.0).then_inc(pc_zero, 1)
            pool.wait_ge(bias_copied, 1)
            pool.dma_start(bias_rows, vec[0:HEADS, :]).then_inc(bias_stored, 16)
            pool.wait_ge(bias_stored, 16)
            pool.dma_start(bias, bass.AP(tensor=bias_rows.tensor, offset=bias_rows.offset + S - 127,
                                         ap=[[1, P], [512, HEADS], [1, S]])).then_inc(bias_loaded, 16)
            pool.wait_ge(mem_lo, 1)
            nc.gpsimd.memset(pT[:, :, 0:META], 0.0).then_inc(pool_padded, 1)
            pool.wait_ge(pool_padded, 1)
            for t in (TILE["pool"], TILE["pool"] + 1):
                wait_evacuated(pool, t)
            chain.link(nc.gpsimd.tensor_tensor(wA[:, :, 1:T], pT[:, :, 1:T], pT[:, :, 0:T - 1], ALU.add))
            chain.link(nc.gpsimd.tensor_tensor(wB[:, :, 3:T], wA[:, :, 3:T], wA[:, :, 1:T - 2], ALU.add))
            inv = col("pool_inv", 0, 512).rearrange("p (a b) -> p a b", a=2)
            chain.link(nc.gpsimd.tensor_tensor(pd[0:64, 0, :], wA[0:64, 0, META:T], inv[0:64, 0, :], ALU.mult))
            chain.link(nc.gpsimd.tensor_tensor(pd[64:128, 0, :], wB[64:128, 0, META:T], inv[64:128, 0, :], ALU.mult))
            chain.link(nc.gpsimd.tensor_tensor(wA[:, 1, 7:T], wB[:, 1, 7:T], wB[:, 1, 3:T - 4], ALU.add))
            chain.link(nc.gpsimd.tensor_tensor(pd[0:64, 1, :], wA[0:64, 1, META:T], inv[0:64, 1, :], ALU.mult))
            chain.link(nc.gpsimd.tensor_tensor(wB[64:128, 1, 15:T], wA[64:128, 1, 15:T], wA[64:128, 1, 7:T - 8], ALU.add))
            chain.link(nc.gpsimd.tensor_tensor(pd[64:128, 1, :], wB[64:128, 1, META:T], inv[64:128, 1, :], ALU.mult))
            nc.gpsimd.tensor_tensor(pd, pd, pT[:, :, META:T], ALU.subtract).then_inc(pool_diff, 1)
            for update, name in enumerate(("w_out", "mo", "down")):
                if name == "down":
                    for p in range(FFN_TILES):
                        pool.wait_ge(f_gelu, p + 1)
                        pool.wait_ge(u_tapped, 2 * p + 2)
                        nc.gpsimd.tensor_tensor(Ft[:, p % 2, :], Gt[:, p % 2, :], Vt[:, p % 2, :], ALU.mult).then_inc(act_ready, 1)
                        pool.wait_ge(act_hi, 12 + p + 1)
                        nc.gpsimd.tensor_tensor(ffn_lo(p), Ft[:, p % 2, :], ffn_hi(p).bitcast(F32), ALU.subtract).then_inc(act_lo, 1)
                sum_squares(lambda m: wait_evacuated(pool, TILE[name] + m), META)
                wait_rstd(pool, (NORM_MIX, NORM_MEMOUT, NORM_FFN)[update])
                pool.wait_ge(y_ready, 8 * update + 8)
                for k in (POOL_FROM, POOL_FROM + 1):
                    chain.link(nc.gpsimd.tensor_tensor(Y[:, k, META:T], Y[:, k, META:T], rstd[:, META:T], ALU.mult))
                    nc.gpsimd.tensor_tensor(XR[:, k, META:T], XR[:, k, META:T], Y[:, k, META:T], ALU.add).then_inc(x_updated_pool, 1)
            for i in range(E_TILES):
                pool.wait_ge(c_conv, i + 1)
                nc.gpsimd.tensor_tensor(Yc, Yc, rstd[:, :], ALU.mult).then_inc(c_scaled, 1)
            sum_squares(lambda m: pool.wait_ge(sq_ready, SQ_H1 + m + 1), 0)
            rest(PRE_H1, 0, l_in(AH, 0), l_in(AL, 0))
            for h in range(LHEADS):
                pool.wait_ge(l_decay, 2 * h + 1)
                nc.gpsimd.affine_select(out=Dl[:, 0:S], in_=Dl[:, 0:S], compare_op=ALU.is_ge, fill=0.0, base=0,
                                        pattern=[[1, S]], channel_multiplier=-1).then_inc(l_masked, 1)
                nc.gpsimd.affine_select(out=Dl[:, S:S + P], in_=Dl[:, S:S + P], compare_op=ALU.is_ge, fill=0.0,
                                        base=0, pattern=[[1, P]], channel_multiplier=-1).then_inc(l_masked, 1)
            sum_squares(lambda m: pool.wait_ge(sq_ready, SQ_FINAL + m + 1), META)

        @block.scalar
        def _(act):
            chain = Chain(act, act_steps)

            def hi(n, i=0):
                act.wait_ge(weights_loaded[n % SLOTS], 16 * (n // SLOTS + 1) + 16 * i)
                if n >= SLOTS:
                    act.wait_ge(chunk_done, n - SLOTS + 1 + 4 * i)
                nc.scalar.activation(w_hi[:, n % SLOTS, :], raw[:, n % SLOTS, :], ACT.Copy).then_inc(hi_ready, 1)

            def ahead(n, i=0):
                if n + AHEAD < NCHUNKS:
                    hi(n + AHEAD, i)

            def take_root(e, w, lo, dst=root):
                nc.scalar.activation(small[:, 157:158], eps_col, ACT.Sqrt)
                act.wait_ge(stat_ready, e + 1)
                nc.scalar.activation(dst[:, lo:T], OB[1][:, 0:w], ACT.Sqrt, bias=eps_col).then_inc(root_ready, 1)

            def to_hi(pre, lo, dst, k):
                act.wait_ge(normed, 8 * pre + k + 1)
                nc.scalar.activation(dst(k), SQ[:, k, lo:T], ACT.Copy).then_inc(normed_hi, 1)

            def wait_x(update, k):
                if k < POOL_FROM:
                    act.wait_ge(x_updated, POOL_FROM // 2 * update + k // 2 + 1)
                else:
                    act.wait_ge(x_updated_pool, (KT - POOL_FROM) * update + k - POOL_FROM + 1)

            def raw_to_hi(lo, u, gain):
                dst = raw_parts(lo)[0]
                for k in range(KT):
                    wait_x(u, k)
                    nc.scalar.activation(dst(k), XR[:, k, lo:T], ACT.Copy, scale=col(gain, k)).then_inc(raw_hi, 1)

            def square_x(lo, update):
                for k in range(0, KT, 2):
                    wait_x(update, k + 1)
                    nc.scalar.activation(SQ[:, k:k + 2, lo:T], XR[:, k:k + 2, lo:T], ACT.Square).then_inc(sq_ready, 2)

            def to_y(t, m, gain):
                nc.scalar.activation(Y[:, m, META:T], acc(t)[:, 0:S], ACT.Copy, scale=col(gain, m)).then_inc(y_ready, 1)
                freed(nc.scalar.activation(SQ[:, m, META:T], acc(t)[:, 0:S], ACT.Square), t)

            eps_col = small[:, 158:159]
            act.wait_ge(consts_ready, 7)
            for k in range(0, KT, 2):
                if k % 4 == 0:
                    act.wait_ge(x_loaded[k // 4], 16)
                nc.scalar.activation(SQ[:, k:k + 2, META:T], XR[:, k:k + 2, META:T], ACT.Square).then_inc(sq_ready, 2)
            hi(0)
            take_root(NORM_X, S, META)
            for k in range(KT):
                to_hi(PRE_X, META, raw_parts(META)[0], k)
            hi(1)
            hi(2)
            act.wait_ge(bias_vec, 1)
            nc.scalar.activation(vec[0:HEADS, :], OB[0][0:HEADS, :], ACT.Copy).then_inc(bias_copied, 1)
            n, t = CHUNK["kc"], TILE["kc"]
            ahead(n)
            wait_chunk(act, n)
            for g in range(GROUPS):
                src = acc(t)[g * HD:(g + 1) * HD, 0:S]
                chain.note(nc.scalar.activation(KC2[0:HD, 0, g, :], src, ACT.Copy))
                last = nc.scalar.activation(KC2[HD:P, 0, g, 0:S - 1], src[:, 1:S], ACT.Copy)
                if g == 0:
                    chain.note(last)
            chain.wait()
            freed(last, t)
            ahead(CHUNK["vc"])
            act.wait_ge(stat_ready, NORM_MEM + 1)
            nc.scalar.activation(root_m[:, 0:S], PTB[:, 0:S], ACT.Sqrt, bias=eps_col).then_inc(root_ready, 1)
            n, t = CHUNK["sgu_v"], TILE["sgu_v"]
            ahead(n)
            ahead(n + 1)
            wait_chunk(act, n + 1)
            freed(nc.scalar.activation(vg[:, :, :], acc(t)[:, :].rearrange("p (a b) -> p a b", a=2), ACT.Gelu_apprx_tanh), t)
            for j in range(2):
                n, t = CHUNK["sgu_u"] + j, TILE["sgu_u"] + j
                ahead(n)
                wait_chunk(act, n)
                freed(nc.scalar.activation(uT[:, j, :], acc(t)[:, 0:S], ACT.Gelu_apprx_tanh), t)
            for c in range(CHUNK["cmp"], CHUNK["cmp"] + 4):
                ahead(c)
            act.wait_ge(mem_normed, 1)
            nc.scalar.activation(MH[:, :, :], mem_raw, ACT.Copy).then_inc(mem_hi, 1)
            for c in range(2):
                ahead(CHUNK["vsw"] + c)
            act.wait_ge(cmp_hidden, 1)
            nc.scalar.activation(hk, OB[1][:, 0:32], ACT.Gelu_apprx_tanh, bias=col("cmp_b1", 0)).then_inc(cmp_copied, 1)
            act.wait_ge(hc_zero, 1)
            for r in range(4):
                nc.scalar.activation(hc[:, :, r, 0:NCMP], OB[0][:, 0:32].rearrange("p (g c) -> p g c", g=2)[:, :, 0:NCMP],
                                     ACT.Gelu_apprx_tanh, bias=col("cmp_b1", 1)).then_inc(cmp_copied, 1)
            act.wait_ge(sgu_var, 1)
            nc.scalar.activation(rs2, mv[:, :, 1], ACT.Sqrt, bias=eps_col).then_inc(sgu_root, 1)
            act.wait_ge(mem_lo, 1)
            for j in range(2):
                n, t = CHUNK["pool"] + j, TILE["pool"] + j
                ahead(n)
                wait_chunk(act, n)
                freed(nc.scalar.activation(pT[:, j, META:T], acc(t)[:, 0:S], ACT.Copy), t)
            for name in ("ks", "kw"):
                ahead(CHUNK[name])
            for j in range(4):
                n, t = CHUNK["q"] + j, TILE["q"] + j
                ahead(n)
                wait_chunk(act, n)
                freed(nc.scalar.mul(qT[:, j, :], acc(t)[:, 0:S], HD ** -0.5), t)
            n, t = CHUNK["gates"], TILE["gates"]
            ahead(n)
            wait_chunk(act, n)
            freed(nc.scalar.activation(gT[0:24, :], acc(t)[0:24, 0:S], ACT.Exp, scale=-1.0), t)
            act.wait_ge(cs_shifted, 1)
            nc.scalar.activation(Sc[:, :, :, :], Sc[:, :, :, :], ACT.Exp).then_inc(cs_exp, 1)

            def out_hi(j):
                act.wait_ge(outs, j + 1)
                nc.scalar.activation(a_hi(j), OB[j % 2][:, 0:S], ACT.Copy).then_inc(act_hi, 1)

            for h in range(HEADS):
                n = CHUNK["mk"] + 2 * h
                ahead(n)
                act.wait_ge(max_ready, h + 1)
                for b in range(4):
                    lo, w = (P * b, P) if b < 2 else (S * (b - 1), S)
                    last = nc.scalar.activation(Sx[:, lo:lo + w], Sx[:, lo:lo + w], ACT.Exp, bias=mx4[:, b:b + 1],
                                                accum_out=sm4[:, b:b + 1])
                    if b < 3:
                        chain.note(last)
                chain.wait()
                last.then_inc(exped, 1)
                ahead(n + 1)
                if h >= 2 and h % 2 == 0:
                    out_hi(h // 2 - 1)
                if h == 0:
                    act.wait_ge(cp_turned, 1)
                    nc.scalar.activation(PcT[:, :, :], OB[0][:, 0:512].rearrange("p (g t) -> p g t", g=2),
                                         ACT.Copy).then_inc(cp_copied, 1)
                act.wait_ge(turned, h + 1)
                nc.scalar.activation(PTx[:, :, :], PTB[:, :].rearrange("p (b t) -> p b t", b=2)[:, :, 0:384],
                                     ACT.Copy).then_inc(copied, 1)
            out_hi(3)
            for j in range(2):
                act.wait_ge(pool_scaled, 4)
                nc.scalar.activation(a_hi(4 + j), t512[:, j * S:(j + 1) * S], ACT.Copy).then_inc(act_hi, 1)
            for j in range(2):
                act.wait_ge(sgu_gated, 1)
                nc.scalar.activation(a_hi(6 + j), vg[:, j, :], ACT.Copy).then_inc(act_hi, 1)
            for m in range(KT):
                n, t = CHUNK["w_out"] + m, TILE["w_out"] + m
                ahead(n)
                wait_chunk(act, n)
                to_y(t, m, "g_mix_post")
            take_root(NORM_MIX, S, META)
            raw_to_hi(META, RAW_X1, "g_mem_pre")
            square_x(META, 0)
            take_root(NORM_X1, S, META)
            def m_exp(h):
                act.wait_ge(m_max, h + 1)
                if h >= 2:
                    act.wait_ge(m_turned, h - 1)
                for b in range(2):
                    last = nc.scalar.activation(Em[:, h % 2, b, :], SC[:, (h % 2) * 512 + b * S:(h % 2) * 512 + (b + 1) * S],
                                                ACT.Exp, bias=small[:, 16 + 2 * h + b:17 + 2 * h + b],
                                                accum_out=small[:, 24 + 2 * h + b:25 + 2 * h + b])
                    if b < 1:
                        chain.link(last)
                last.then_inc(m_exped, 1)

            def m_copy(h):
                act.wait_ge(m_turned, h + 1)
                if h >= 2:
                    act.wait_ge(m_outs, h - 1)
                nc.scalar.activation(PTm[:, h % 2, :, :], PTB[:, (h % 2) * 512:(h % 2) * 512 + 512].rearrange("p (m t) -> p m t", m=2),
                                     ACT.Copy).then_inc(m_copied, 1)

            def m_hi(h):
                act.wait_ge(m_outs, h + 1)
                nc.scalar.activation(AH[:, 2 * h * S:(2 * h + 2) * S], OB[h % 2][:, :], ACT.Copy).then_inc(act_hi, 1)

            for m in range(KT):
                n, t = CHUNK["mq"] + m, TILE["mq"] + m
                ahead(n)
                if m >= 3 and m % 2 == 1:
                    m_exp((m - 3) // 2)
                if m >= 5 and m % 2 == 1:
                    m_copy((m - 5) // 2)
                if m == 7:
                    m_hi(0)
            m_exp(3)
            m_copy(2)
            m_hi(1)
            m_copy(3)
            m_hi(2)
            m_hi(3)
            for m in range(KT):
                n, t = CHUNK["mo"] + m, TILE["mo"] + m
                ahead(n)
                wait_chunk(act, n)
                to_y(t, m, "g_mem_post")
            take_root(NORM_MEMOUT, S, META)
            raw_to_hi(META, RAW_X2, "g_ffn_pre")
            square_x(META, 1)
            take_root(NORM_X2, S, META)
            taps = col("ffn_conv", 0, 176).rearrange("p (a b) -> p a b", b=8)

            def ffn_act(p, i, hidden):
                for v in range(2):
                    n, t = CHUNK["up"] + 2 * p + v, TILE["up"] + 2 * p + v
                    ahead(n, i)
                    wait_evacuated(act, t, i)
                    nc.scalar.activation((Gt, Vt)[v][:, p % 2, :], Ut[:, v, :], ACT.Identity, bias=taps[:, p + 2 * i, 4 * v + 3:4 * v + 4],
                                         scale=taps[:, p + 2 * i, 4 * v + 2:4 * v + 3]).then_inc(f_init, 1)
                    if hidden is not None:
                        (ffn_gelu, ffn_hidden)[v](p - 1, i, hidden)

            def ffn_gelu(p, i, _):
                act.wait_ge(u_tapped, 2 * p + 1 + 4 * i)
                nc.scalar.activation(Gt[:, p % 2, :], Gt[:, p % 2, :], ACT.Gelu_apprx_tanh).then_inc(f_gelu, 1)

            def ffn_hidden(p, i, dst):
                act.wait_ge(act_ready, p + 1 + 2 * i)
                nc.scalar.activation(dst, Ft[:, p % 2, :], ACT.Copy).then_inc(act_hi, 1)

            ffn_act(0, 0, None)
            for i in range(8):
                for p in (1, 2):
                    ffn_act(p, i, a_hi(p - 1 + 2 * i))
            for p in range(17, FFN_TILES):
                ffn_act(p, 0, ffn_hi(p - 1))
            ffn_gelu(FFN_TILES - 1, 0, None)
            ffn_hidden(FFN_TILES - 1, 0, ffn_hi(FFN_TILES - 1))
            for m in range(KT):
                n, t = CHUNK["down"] + 3 * m, TILE["down"] + m
                for c in range(3):
                    ahead(n + c)
                wait_chunk(act, n + 2)
                to_y(t, m, "g_ffn_post")
            take_root(NORM_FFN, S, META)
            act.wait_ge(meta_loaded, 16)
            raw_to_hi(0, RAW_H0, "g_conv")
            square_x(0, 2)
            take_root(NORM_H0, T, 0)
            def conv_act(i):
                n, t = CHUNK["conv_in"], TILE["conv_in"]
                for c in range(3):
                    ahead(n + c, i)
                wait_evacuated(act, t + 2, i)
                nc.scalar.activation(SZ, ZZ, ACT.Sigmoid).then_inc(c_sig, 1)
                ahead(n + 3, i)
                wait_evacuated(act, t + 3, i)
                nc.scalar.activation(a_hi(i, T), Fc, ACT.Copy).then_inc(act_hi, 1)

            for i in range(E_TILES):
                conv_act(i)
            for m in range(KT):
                n, t = CHUNK["conv_out"] + 2 * m, TILE["conv_out"] + m
                ahead(n)
                ahead(n + 1)
                wait_evacuated(act, t)
                nc.scalar.activation(XH[:, m, :], XR[:, m, :], ACT.Copy, scale=col("g_mlstm", m)).then_inc(raw_hi, 1)
                nc.scalar.activation(SQ[:, m, :], XR[:, m, :], ACT.Square).then_inc(sq_ready, 1)
            take_root(NORM_H1, T, 0)
            n, t = CHUNK["lgates"], TILE["lgates"]
            ahead(n)
            for m in range(KT):
                ahead(CHUNK["lk"] + m)
                to_hi(PRE_H1, 0, l_in(AH, 0), m)
                if m == 2:
                    wait_evacuated(act, TILE["lgates"])
                    nc.scalar.activation(gx[0:36, :], gx[0:36, :], ACT.Identity, bias=col("gate_b")[0:36]).then_inc(g_raw, 1)
                    act.wait_ge(g_raw, 1)
                    chain.link(nc.scalar.activation(ge[32:36, :], gx[32:36, :], ACT.Abs))
                    chain.link(nc.scalar.activation(ge[32:36, :], ge[32:36, :], ACT.Exp, scale=-1.0))
                    nc.scalar.activation(gl[32:36, :], ge[32:36, :], ACT.Ln, bias=ones_1[32:36, 0:1]).then_inc(g_ln, 1)
            for m in range(KT):
                n, t = CHUNK["lq"] + m, TILE["lq"] + m
                ahead(n)
                wait_chunk(act, n)
                freed(nc.scalar.mul(lq[:, m, :], acc(t)[:, 0:S], S ** -0.5), t)

            def decay(h):
                act.wait_ge(l_rows, h + 1)
                if h == 0:
                    act.wait_ge(g_cols, 1)
                else:
                    act.wait_ge(l_probs, 3 * h)
                chain.note(nc.scalar.activation(Dl[:, 0:S], PTB[:, 0:S], ACT.Exp, bias=acol[:, 1, h:h + 1]))
                chain.note(nc.scalar.activation(Dl[:, S:S + P], PTB[:, P:S], ACT.Exp, bias=acol[:, 2, h:h + 1]))
                chain.wait()
                nc.scalar.activation(Dl[0:META, 384:640], PTB[0:META, 0:S], ACT.Exp,
                                     bias=acol[0:META, 0, h:h + 1]).then_inc(l_decay, 1)
                if h:
                    act.wait_ge(l_hn, h)
                nc.scalar.activation(em, PTB[:, S:2 * S], ACT.Exp).then_inc(l_decay, 1)

            for m in range(E_TILES):
                n, t = CHUNK["lv"] + m, TILE["lv"] + m
                ahead(n)
                wait_chunk(act, n)
                if m >= 2:
                    act.wait_ge(l_vturned, m - 1)
                freed(nc.scalar.activation(lvT[:, m % 2, :], acc(t)[:, 0:T], ACT.Copy), t)
                if m == 4:
                    decay(0)
            def l_hi(e):
                wait_evacuated(act, TILE["oz"] + 8 * (e // 4) + 4 + e % 4)
                nc.scalar.activation(l_out(AH, e), hn[:, e % 4, :], ACT.Copy).then_inc(act_hi, 1)

            for h in range(LHEADS):
                n0, t0 = CHUNK["oz"] + 8 * h, TILE["oz"] + 8 * h
                if h + 1 < LHEADS:
                    decay(h + 1)
                act.wait_ge(l_hn, h + 1)
                nc.scalar.activation(sqh[:, :, :], hn[:, :, :], ACT.Square).then_inc(l_sq, 1)
                for m in range(4):
                    ahead(n0 + m)
                    wait_chunk(act, n0 + m)
                    if h:
                        wait_evacuated(act, t0 - 4 + m)
                    freed(nc.scalar.activation(so[:, m, :], acc(t0 + m)[:, 0:S], ACT.Sigmoid), t0 + m)
                act.wait_ge(l_stat, h + 1)
                nc.scalar.activation(lroot, PTB[:, 512:512 + S], ACT.Sqrt, bias=eps_col).then_inc(l_root, 1)
                for m in range(4):
                    n, t = n0 + 4 + m, t0 + 4 + m
                    ahead(n)
                    wait_chunk(act, n)
                    nc.scalar.activation(tz[:, m % 2, :], acc(t)[:, 0:S], ACT.Sigmoid).then_inc(z_sig, 1)
                    if m:
                        l_hi(4 * h + m - 1)
                l_hi(4 * h + 3)
            for m in range(KT):
                n, t = CHUNK["lout"] + 2 * m, TILE["lout"] + m
                ahead(n)
                ahead(n + 1)
                wait_evacuated(act, t)
                nc.scalar.activation(SQ[:, m, META:T], XR[:, m, META:T], ACT.Square).then_inc(sq_ready, 1)
            take_root(NORM_FINAL, S, META)

        @block.tensor
        def _(pe):
            def stat(e, src, w, dst):
                for k in range(KT):
                    src(k)
                    last = nc.tensor.matmul(dst, ones_d[:, :], (SQ[:, k, T - w:T] if e != NORM_MEM else KTm[:, k, :]),
                                            start=(k == 0), stop=(k == KT - 1))
                last.then_inc(stat_ready, 1)

            def stat_x(e, count, w):
                stat(e, lambda k: pe.wait_ge(sq_ready, 8 * count + k + 1), w, OB[1][:, 0:w])

            def stat_sum(e, count, last_ready, w):
                pe.wait_ge(sum_ready, count)
                nc.tensor.matmul(OB[1][:, 0:w], ones_d[:, :], SS[:, T - w:T], start=True, stop=False)
                last_ready()
                nc.tensor.matmul(OB[1][:, 0:w], ones_d[:, :], SQ[:, KT - 1, T - w:T], start=False, stop=True).then_inc(stat_ready, 1)

            def stat_y(e, count, name):
                stat_sum(e, count, lambda: wait_evacuated(pe, TILE[name] + KT - 1), S)

            def keep_warm(products):
                for _ in range(products):
                    nc.tensor.matmul(OB[0][:, 0:P], ones_d[:, :], ident[:, :], start=True, stop=True)

            def begin(n, t, first, i=0):
                pe.wait_ge(lo_ready, n + 1 + 4 * i)
                if first and t >= 2:
                    pe.wait_ge(evacuated[t % 2], t // 2 + 2 * i)

            def chunk(n, t, xh, xl, w, i=0, k0=0, nk=KT, total=KT, ready=None):
                begin(n, t, k0 == 0, i)
                s = n % SLOTS
                for j in range(nk):
                    k = k0 + j
                    if ready:
                        ready(k)
                    wh, wl = w_hi[:, s, j * P:(j + 1) * P], w_lo[:, s, j * P:(j + 1) * P]
                    nc.tensor.matmul(acc(t)[:, 0:w], wh, xh(k), start=(k == 0), stop=False)
                    nc.tensor.matmul(acc(t)[:, 0:w], wh, xl(k), start=False, stop=False)
                    last = nc.tensor.matmul(acc(t)[:, 0:w], wl, xh(k), start=False, stop=(k == total - 1))
                last.then_inc(chunk_done, 1)

            def slots(part, n, cols):
                a, b = sorted((n % SLOTS, (n + 1) % SLOTS))
                return part[:, a:b + 1:b - a, cols]

            def pair_tokens(n, t, xh, xl, between=None):
                begin(n + 1, t, True)
                for b in range(2):
                    o = acc(t)[:, b * S:(b + 1) * S].rearrange("p (r c) -> p r c", r=2)
                    for k in range(KT):
                        cols = slice(k * P, (k + 1) * P)
                        wh, wl = slots(w_hi, n, cols), slots(w_lo, n, cols)
                        nc.tensor.matmul(o, xh(k)[:, b * P:(b + 1) * P], wh, start=(k == 0), stop=False)
                        nc.tensor.matmul(o, xl(k)[:, b * P:(b + 1) * P], wh, start=False, stop=False)
                        last = nc.tensor.matmul(o, xh(k)[:, b * P:(b + 1) * P], wl, start=False, stop=(k == KT - 1))
                    if b == 0 and between:
                        between()
                last.then_inc(chunk_done, 2)

            def xh(k):
                return XH[:, k, META:T]

            def xl(k):
                return XL[:, k, META:T]

            def xha(k):
                return XH[:, k, :]

            def xla(k):
                return XL[:, k, :]

            def pre_ready(pre):
                return lambda k: pe.wait_ge((normed_lo, rest_pool)[k % 2], 4 * pre + k // 2 + 1)

            pe.wait_ge(consts_ready, 7)
            stat_x(NORM_X, 0, S)
            pe.wait_ge(rel_loaded, 32)
            nc.tensor.matmul(OB[0][0:HEADS, :], rb[:, :], hot[0:33, :], start=True, stop=True).then_inc(bias_vec, 1)
            for i in range(CMP_BIASES):
                lo = S - 31 - CSTRIDE * (NCMP - 1) + CSTRIDE * i
                last = nc.tensor.matmul(SC[:, i * HEADS:(i + 1) * HEADS], hot[0:33, lo:lo + P], rb[:, :], start=True, stop=True)
            last.then_inc(cmp_bias, 1)
            chunk(CHUNK["kc"], TILE["kc"], xh, xl, S, ready=pre_ready(PRE_X))
            chunk(CHUNK["vc"], TILE["vc"], xh, xl, S)
            stat(NORM_MEM, lambda k: pe.wait_ge(mem_sq, 1), S, PTB[:, 0:S])
            pair_tokens(CHUNK["sgu_v"], TILE["sgu_v"], xh, xl)
            for j in range(2):
                chunk(CHUNK["sgu_u"] + j, TILE["sgu_u"] + j, xh, xl, S)
            pe.wait_ge(cmp_in, 2)
            for c in range(2):
                n, t = CHUNK["cmp"] + 2 * c, TILE["cmp"]
                begin(n + 1, t, c == 0)
                o = acc(t)[0:64, 0:S].rearrange("p (r c) -> p r c", r=2)
                for k in range(KT):
                    j, cols = KT * c + k, slice(k * P, (k + 1) * P)
                    rows = slice(2048 + 64 * j, 2048 + 64 * (j + 1))
                    nc.tensor.matmul(o, AH[:, rows], slots(w_hi, n, cols), start=(j == 0), stop=False)
                    nc.tensor.matmul(o, AL[:, rows], slots(w_hi, n, cols), start=False, stop=False)
                    last = nc.tensor.matmul(o, AH[:, rows], slots(w_lo, n, cols), start=False, stop=(j == 15))
                last.then_inc(chunk_done, 2)
            pair_tokens(CHUNK["vsw"], TILE["vsw"], xh, xl)
            wait_evacuated(pe, TILE["cmp"])
            pe.wait_ge(root_ready, 1)
            pe.wait_ge(bias_copied, 1)
            nc.tensor.transpose(OB[1][:, 0:32], ch[0:32, 0:P], ident[0:32, 0:32])
            nc.tensor.transpose(OB[0][:, 0:32], ch[32:64, P:S], ident[32:64, 32:64]).then_inc(cmp_hidden, 1)
            for j in range(2):
                chunk(CHUNK["pool"] + j, TILE["pool"] + j, xh, xl, S)
            w2 = col("cmp_w2", 0, 128)
            pe.wait_ge(cmp_copied, 5)
            for g in range(GROUPS):
                nc.tensor.matmul(OB[0][g * HD:(g + 1) * HD, 0:NCMP], w2[:, 0:HD], hk[:, g * 16:g * 16 + NCMP],
                                 start=True, stop=True)
            for g in range(GROUPS):
                last = nc.tensor.matmul(OB[0][:, 64 + g * HD:64 + (g + 1) * HD], hc[:, g, :, :].rearrange("p a b -> p (a b)"),
                                        w2[:, HD:2 * HD], start=True, stop=True)
            last.then_inc(cmp_out, 1)
            chunk(CHUNK["ks"], TILE["ks"], xh, xl, S)
            chunk(CHUNK["kw"], TILE["kw"], xh, xl, S)
            pe.wait_ge(sgu_normed, 1)
            pe.wait_ge(sgu_masked, 1)
            sw = col("sgu_w", 0, 512).rearrange("p (h t) -> p h t", h=4)
            for h in range(4):
                for b in range(2):
                    o = OB[1][(h % 2) * HD:(h % 2 + 1) * HD, (h // 2) * S + b * P:(h // 2) * S + (b + 1) * P]
                    last = nc.tensor.matmul(o, vn[:, b, h * HD:(h + 1) * HD], sw[:, h, :], start=True, stop=True)
            last.then_inc(sgu_mixed, 1)
            for j in range(4):
                chunk(CHUNK["q"] + j, TILE["q"] + j, xh, xl, S)
            chunk(CHUNK["gates"], TILE["gates"], xh, xl, S)
            pe.wait_ge(pool_diff, 1)
            pe.wait_ge(root_ready, 2)
            pw = col("pool_w", 0, 128).rearrange("p (a b) -> p a b", a=2)
            for j in range(2):
                for r in range(2):
                    o = PTB[r * HD:(r + 1) * HD, r * 512 + j * S:r * 512 + (j + 1) * S]
                    last = nc.tensor.matmul(o, pw[r * HD:(r + 1) * HD, j, :], pd[r * HD:(r + 1) * HD, j, :],
                                            start=True, stop=True)
            last.then_inc(pool_mixed, 1)
            wait_evacuated(pe, TILE["gates"])
            pe.wait_ge(sgu_mixed, 2)
            for b in range(2):
                last = nc.tensor.transpose(OB[1][:, b * 24:(b + 1) * 24], gT[0:24, b * P:(b + 1) * P], ident[0:24, 0:24])
            last.then_inc(gate_turned, 1)
            pe.wait_ge(cmp_kv, 2)
            pe.wait_ge(cb_copied, 1)
            for g in range(GROUPS):
                for j in range(4):
                    for b in range(2):
                        o = g * 512 + (b * 4 + j) * NCMP
                        last = nc.tensor.matmul(SC[:, o:o + NCMP], qT[g * HD:(g + 1) * HD, j, b * P:(b + 1) * P],
                                                kcmp[g * HD:(g + 1) * HD, 0:NCMP], start=True, stop=True)
            last.then_inc(cs_ready, 1)

            def qk(h):
                j, g = h // 2, h % 2
                if h == 0:
                    pe.wait_ge(cs_shifted, 1)
                    wait_evacuated(pe, TILE["kw"])
                    wait_evacuated(pe, TILE["q"] + 3)
                else:
                    pe.wait_ge(max_ready, h)
                q = qT[g * HD:(g + 1) * HD, j, :]
                for r in range(2):
                    k = kT[g * HD:(g + 1) * HD, r, :]
                    nc.tensor.matmul(SC[:, r * P:(r + 1) * P], q[:, 0:P], k[:, 0:P], start=True, stop=True)
                for r in range(2):
                    k = kT[g * HD:(g + 1) * HD, r, :]
                    last = nc.tensor.matmul(SC[:, 512 + r * S:512 + (r + 1) * S], q[:, P:S], k, start=True, stop=True)
                last.then_inc(scores, 1)

            def turn(h):
                pe.wait_ge(probs, h + 1)
                if h == 0:
                    pe.wait_ge(pool_scaled, 4)
                else:
                    pe.wait_ge(copied, h)
                for r in range(2):
                    o = r * 512
                    nc.tensor.transpose(PTB[:, o:o + P], Sx[:, r * P:(r + 1) * P], ident[:, :])
                    nc.tensor.transpose(PTB[:, o + P:o + S], Sx[:, S + r * S:S + r * S + P], ident[:, :])
                    last = nc.tensor.transpose(PTB[:, o + S:o + S + P], Sx[:, S + r * S + P:S + (r + 1) * S], ident[:, :])
                last.then_inc(turned, 1)

            def pv(h):
                j, g = h // 2, h % 2
                pe.wait_ge(copied, h + 1)
                if h == 0:
                    pe.wait_ge(cp_copied, 1)
                if g == 0 and j >= 2:
                    pe.wait_ge(act_lo, j - 1)
                o = OB[j % 2][g * HD:(g + 1) * HD, 0:S]
                for r in range(2):
                    nc.tensor.matmul(o, Vtok[:, r, 0, g * HD:(g + 1) * HD], PTx[:, r, 0:S], start=(r == 0), stop=False)
                    nc.tensor.matmul(o[:, P:S], Vtok[:, r, 1, g * HD:(g + 1) * HD], PTx[:, r, S:384], start=False, stop=False)
                last = nc.tensor.matmul(o, VX[:, g, j, :], PcT[:, g, :], start=False, stop=True)
                if g:
                    last.then_inc(outs, 1)

            for h in range(HEADS):
                qk(h)
                n, t = CHUNK["mk"] + 2 * h, TILE["mk"] + 2 * h
                if h == 0:
                    pe.wait_ge(mem_lo, 1)
                if h < HEADS // 2:
                    for c in range(2):
                        if c == 1 and h:
                            pv(h - 1)
                        chunk(n + c, t + c, lambda k: MH[:, k, :], lambda k: ML[:, k, :], S)
                else:
                    pair_tokens(n, TILE["mv"] + h - HEADS // 2, lambda k: MH[:, k, :], lambda k: ML[:, k, :], lambda: pv(h - 1))
                if h == 0:
                    pe.wait_ge(cp_ready, 1)
                    pe.wait_ge(cmp_kv, 2)
                    for g in range(GROUPS):
                        for b in range(2):
                            last = nc.tensor.transpose(OB[0][:, g * S + b * P:g * S + (b + 1) * P],
                                                       Pc[:, b, g, :, :].rearrange("p a b -> p (a b)"), ident[:, :])
                    last.then_inc(cp_turned, 1)
                turn(h)
            pv(HEADS - 1)
            pe.wait_ge(act_lo, 8)
            for m in range(KT):
                chunk(CHUNK["w_out"] + m, TILE["w_out"] + m, a_hi, a_lo, S)
            stat_y(NORM_MIX, 1, "w_out")
            keep_warm(WARM)

            def raw_ready(u):
                return lambda k: pe.wait_ge(raw_lo, 8 * u + k + 1)

            def m_qk(h):
                for j in (2 * h, 2 * h + 1):
                    wait_evacuated(pe, TILE["mq"] + j)
                if h >= 2:
                    pe.wait_ge(m_exped, h - 1)
                for b in range(2):
                    for j in range(2):
                        last = nc.tensor.matmul(SC[:, (h % 2) * 512 + b * S:(h % 2) * 512 + (b + 1) * S],
                                                qM[:, 2 * h + j, b * P:(b + 1) * P], KTm[:, 2 * h + j, :],
                                                start=(j == 0), stop=(j == 1))
                last.then_inc(m_scores, 1)

            def m_turn(h):
                pe.wait_ge(m_probs, h + 1)
                if h >= 2:
                    pe.wait_ge(m_copied, h - 1)
                for m in range(2):
                    for b in range(2):
                        last = nc.tensor.transpose(PTB[:, (h % 2) * 512 + m * S + b * P:(h % 2) * 512 + m * S + (b + 1) * P],
                                                   Em[:, h % 2, b, m * P:(m + 1) * P], ident[:, :])
                last.then_inc(m_turned, 1)

            def m_pv(h):
                pe.wait_ge(m_copied, h + 1)
                if h >= 2:
                    pe.wait_ge(act_lo, ACT_MEM + h - 1)
                for v in range(2):
                    for m in range(2):
                        last = nc.tensor.matmul(OB[h % 2][:, v * S:(v + 1) * S], VM[:, 2 * h + v, m, :], PTm[:, h % 2, m, :],
                                                start=(m == 0), stop=(m == 1))
                last.then_inc(m_outs, 1)

            for m in range(KT):
                chunk(CHUNK["mq"] + m, TILE["mq"] + m, xh, xl, S, ready=raw_ready(RAW_X1) if m == 0 else None)
                if m == 0:
                    stat_x(NORM_X1, 1, S)
                if m == 2:
                    m_qk(0)
                if m == 4:
                    m_turn(0)
                    m_qk(1)
                if m == 5:
                    m_pv(0)
                if m == 6:
                    m_turn(1)
                    m_qk(2)
                if m == 7:
                    m_pv(1)
            m_qk(3)
            m_turn(2)
            m_pv(2)
            m_turn(3)
            m_pv(3)
            pe.wait_ge(act_lo, 12)
            for m in range(KT):
                chunk(CHUNK["mo"] + m, TILE["mo"] + m, a_hi, a_lo, S)
            stat_y(NORM_MEMOUT, 2, "mo")
            keep_warm(WARM)
            def ffn_pe(i, first=False):
                for r in range(4):
                    chunk(CHUNK["up"] + r, TILE["up"] + r, xh, xl, S, i=i, ready=raw_ready(RAW_X2) if first and r == 0 else None)
                    if first and r == 0:
                        stat_x(NORM_X2, 2, S)

            for i in range(FFN_TILES // 2):
                ffn_pe(i, i == 0)
            for m in range(KT):
                for c in range(3):
                    chunk(CHUNK["down"] + 3 * m + c, TILE["down"] + m, ffn_hi, ffn_lo, S, k0=8 * c,
                          nk=min(8, FFN_TILES - 8 * c), total=FFN_TILES,
                          ready=(lambda k: pe.wait_ge(act_lo, 12 + k + 1)) if m == 0 else None)
            stat_y(NORM_FFN, 3, "down")
            keep_warm(WARM)
            def conv_pe(i, first=False):
                for r in range(4):
                    chunk(CHUNK["conv_in"] + r, TILE["conv_in"] + r, xha, xla, T, i=i, ready=raw_ready(RAW_H0) if first and r == 0 else None)
                    if first and r == 0:
                        stat_x(NORM_H0, 3, T)

            for i in range(E_TILES):
                conv_pe(i, i == 0)
            for m in range(KT):
                for c in range(2):
                    chunk(CHUNK["conv_out"] + 2 * m + c, TILE["conv_out"] + m, lambda k: a_hi(k, T), lambda k: a_lo(k, T), T,
                          k0=8 * c, total=E_TILES, ready=(lambda k: pe.wait_ge(act_lo, 12 + FFN_TILES + k + 1)) if m == 0 else None)
            chunk(CHUNK["lgates"], TILE["lgates"], xha, xla, T, ready=raw_ready(RAW_H1))
            stat_sum(NORM_H1, 4, lambda: pe.wait_ge(sq_ready, SQ_H1 + KT), T)
            for m in range(KT):
                chunk(CHUNK["lk"] + m, TILE["lk"] + m, xha, xla, T)
            pe.wait_ge(g_rows, 3)
            for s, (lo, w) in enumerate(((0, META), (META, P), (META + P, P))):
                last = nc.tensor.transpose(OB[0][0:w, 4 * s:4 * s + 4], gA[0:LHEADS, lo:lo + w], ident[0:LHEADS, 0:LHEADS])
            last.then_inc(g_turned, 1)
            for m in range(KT):
                chunk(CHUNK["lq"] + m, TILE["lq"] + m, l_in(AH, META), l_in(AL, META), S, ready=pre_ready(PRE_H1) if m == 0 else None)

            def l_qk(h):
                if h == 0:
                    wait_evacuated(pe, TILE["lk"] + 7)
                    wait_evacuated(pe, TILE["lq"] + 7)
                else:
                    pe.wait_ge(l_probs, 3 * h)
                for j in range(2):
                    nc.tensor.matmul(SC[:, 0:S], lk[:, 2 * h + j, META:META + P], lq[:, 2 * h + j, :],
                                     start=(j == 0), stop=(j == 1))
                for j in range(2):
                    nc.tensor.matmul(SC[:, S:S + P], lk[:, 2 * h + j, META + P:T], lq[:, 2 * h + j, P:S],
                                     start=(j == 0), stop=(j == 1))
                for j in range(2):
                    last = nc.tensor.matmul(SC[0:META, 512:512 + S], lk[:, 2 * h + j, 0:META], lq[:, 2 * h + j, :],
                                            start=(j == 0), stop=(j == 1))
                last.then_inc(l_scores, 1)

            def l_bcast(h):
                if h:
                    pe.wait_ge(l_decay, 2 * h)
                nc.tensor.matmul(PTB[:, 0:S], sel[:, h, :], negM[:, META:T], start=True, stop=True)
                nc.tensor.matmul(PTB[:, S:2 * S], sel[:, h, :], negFM[:, META:T], start=True, stop=True).then_inc(l_rows, 1)

            def l_pv(h):
                pe.wait_ge(l_probs, 3 * h + 3)
                if h:
                    pe.wait_ge(l_root, h)
                parts = ((0, P, Pl[:, 0:S], 0), (1, P, Pl[:, S:S + P], P), (2, META, Pl[0:META, 384:640], 0))
                for s, w, p, lo in parts:
                    nc.tensor.matmul(PTB[:, 512 + lo:512 + S], ones_1[0:w, :], p, start=(s == 0), stop=(s == 2))
                for v in range(4):
                    o = OB[v // 2][:, (v % 2) * S:(v % 2 + 1) * S]
                    for s, w, p, lo in parts:
                        c = 512 * h + v * P
                        last = nc.tensor.matmul(o[:, lo:S], lv[0:w, s, c:c + P], p, start=(s == 0), stop=(s == 2))
                last.then_inc(l_num, 1)

            def v_turn(m):
                wait_evacuated(pe, TILE["lv"] + m)
                if m >= 2:
                    pe.wait_ge(l_vcopied, m - 1)
                if m == 0:
                    pe.wait_ge(g_cols, 1)
                o = OB[m % 2]
                nc.tensor.transpose(o[:, 0:P], lvT[:, m % 2, META:META + P], ident[:, :])
                nc.tensor.transpose(o[:, P:2 * P], lvT[:, m % 2, META + P:T], ident[:, :])
                nc.tensor.transpose(o[0:META, 2 * P:3 * P], lvT[:, m % 2, 0:META], ident[:, :]).then_inc(l_vturned, 1)

            for m in range(E_TILES):
                chunk(CHUNK["lv"] + m, TILE["lv"] + m, l_in(AH, 0), l_in(AL, 0), T)
                if m >= 1:
                    v_turn(m - 1)
                if m == 2:
                    pe.wait_ge(g_rows, 3)
                    l_bcast(0)
                if m == 4:
                    l_qk(0)
            v_turn(E_TILES - 1)
            pe.wait_ge(l_vcopied, E_TILES)
            for h in range(LHEADS):
                l_pv(h)
                if h + 1 < LHEADS:
                    l_bcast(h + 1)
                    l_qk(h + 1)
                n, t = CHUNK["oz"] + 8 * h, TILE["oz"] + 8 * h
                for m in range(4):
                    chunk(n + m, t + m, l_in(AH, META), l_in(AL, META), S)
                pe.wait_ge(l_sq, h + 1)
                for v in range(4):
                    last = nc.tensor.matmul(PTB[:, 512:512 + S], ones_h[:, :], sqh[:, v, :], start=(v == 0), stop=(v == 3))
                last.then_inc(l_stat, 1)
                for m in range(4, 8):
                    chunk(n + m, t + m, l_in(AH, META), l_in(AL, META), S)
            for m in range(KT):
                for c in range(2):
                    chunk(CHUNK["lout"] + 2 * m + c, TILE["lout"] + m, lambda k: l_out(AH, k), lambda k: l_out(AL, k), S, k0=8 * c, total=E_TILES,
                          ready=(lambda k: pe.wait_ge(act_lo, 12 + FFN_TILES + E_TILES + k + 1)) if m == 0 else None)
            stat_sum(NORM_FINAL, 5, lambda: pe.wait_ge(sq_ready, SQ_FINAL + KT), S)

        @block.vector
        def _(dve):
            chain = Chain(dve, vec_steps)
            V = nc.vector

            def lo(n, i=0):
                dve.wait_ge(hi_ready, n + 1 + 4 * i)
                s = n % SLOTS
                V.tensor_tensor(w_lo[:, s, :], raw[:, s, :], w_hi[:, s, :].bitcast(F32), ALU.subtract).then_inc(lo_ready, 1)

            def ahead(n, i=0):
                if n + AHEAD < NCHUNKS:
                    lo(n + AHEAD, i)

            def reciprocal_root(e, a):
                dve.wait_ge(root_ready, e + 1)
                V.reciprocal(rstd[:, a:T], root[:, a:T]).then_inc(rstd_ready, 1)
                wait_rstd(dve, e)

            def apply_norm(pre, gain, a, h, l, k):
                if k < KT:
                    V.scalar_tensor_tensor(out=SQ[:, k, a:T], in0=XR[:, k, a:T], scalar=col(gain, k), in1=rstd[:, a:T],
                                           op0=ALU.mult, op1=ALU.mult).then_inc(normed, 1)
                k -= 2
                if k >= 0 and k % 2 == 0:
                    dve.wait_ge(normed_hi, 8 * pre + k + 1)
                    V.tensor_tensor(l(k), SQ[:, k, a:T], h(k).bitcast(F32), ALU.subtract).then_inc(normed_lo, 1)

            def raw_rest(u, gain, a, k):
                dve.wait_ge(raw_hi, 8 * u + k + 1)
                V.scalar_tensor_tensor(out=XL[:, k, a:T], in0=XR[:, k, a:T], scalar=col(gain, k),
                                       in1=XH[:, k, a:T].bitcast(F32), op0=ALU.mult, op1=ALU.subtract).then_inc(raw_lo, 1)

            def post_norm(e, update, gain, a):
                reciprocal_root(e, META)
                dve.wait_ge(y_ready, 8 * update + 8)
                scaled = chain.count
                for k in range(0, POOL_FROM, 2):
                    chain.note(V.tensor_tensor(Y[:, k:k + 2, META:T], Y[:, k:k + 2, META:T],
                                               rstd[:, META:T].unsqueeze(1).to_broadcast([P, 2, S]), ALU.mult))
                    if k:
                        add(k - 2, update, scaled)
                add(POOL_FROM - 2, update, scaled)
                for k in range(KT):
                    raw_rest(update, gain, a, k)

            def add(k, update, scaled):
                dve.wait_ge(vec_steps, scaled + k // 2 + 1)
                V.tensor_tensor(XR[:, k:k + 2, META:T], XR[:, k:k + 2, META:T], Y[:, k:k + 2, META:T], ALU.add).then_inc(x_updated, 1)

            V.memset(rb[32:33, :], MASKED).then_inc(consts_ready, 1)
            V.memset(small[:, 158:159], EPS).then_inc(consts_ready, 1)
            lo(0)
            dve.wait_ge(gains_loaded, 16)
            reciprocal_root(NORM_X, META)
            for k in range(KT + 1):
                apply_norm(PRE_X, "g_mix_pre", META, *raw_parts(META), k)
            lo(1)
            lo(2)
            ahead(CHUNK["kc"])
            n, t = CHUNK["vc"], TILE["vc"]
            wait_chunk(dve, n)
            for g in range(GROUPS):
                src = acc(t)[g * HD:(g + 1) * HD, 0:S]
                chain.note(V.tensor_copy(KC2[0:HD, 1, g, :], src))
                last = V.tensor_copy(KC2[HD:P, 1, g, 0:S - 1], src[:, 1:S])
                if g == 0:
                    chain.note(last)
            freed(last, t)
            ahead(n)
            dve.wait_ge(cmp_bias, 1)
            V.tensor_copy(cb[:, :, :].rearrange("p a b -> p (a b)"), SC[:, 0:CMP_BIASES * HEADS]).then_inc(cb_copied, 1)
            dve.wait_ge(rf_zero, 1)
            dve.wait_ge(params_loaded, 16)
            wait_evacuated(dve, TILE["kc"])
            wait_evacuated(dve, TILE["vc"])
            chain.wait()
            pos = col("cmp_pos", 0, 32).rearrange("p (a b) -> p a b", a=2)
            for v in range(2):
                for g in range(GROUPS):
                    src = KC2[:, v, g, :].rearrange("p (c l) -> p l c", l=CSTRIDE)
                    for half in range(2):
                        ks = slice(8 * half, 8 * half + 8)
                        chain.note(V.tensor_tensor(RF[:, ks, v, g, 0:NCMP], src[:, 0:CSTRIDE:2, half:half + NCMP],
                                                   pos[:, v, ks].unsqueeze(2).to_broadcast([P, 8, NCMP]), ALU.add))
            chain.wait()
            rf = RF[:, :, :, :, :].rearrange("p a b c d -> p (a b c d)")
            V.tensor_copy(AH[:, 2048:3072], rf).then_inc(cmp_in, 1)
            dve.wait_ge(cmp_in, 1)
            V.tensor_tensor(AL[:, 2048:3072], rf, AH[:, 2048:3072].bitcast(F32), ALU.subtract).then_inc(cmp_in, 1)
            ahead(CHUNK["sgu_v"])
            dve.wait_ge(root_ready, 2)
            chain.link(V.reciprocal(rstd_m[:, 0:S], root_m[:, 0:S]))
            for k in range(KT):
                last = V.scalar_tensor_tensor(out=mem_raw[:, k, :], in0=mem_raw[:, k, :], scalar=col("g_mem_kv", k),
                                              in1=rstd_m[:, 0:S], op0=ALU.mult, op1=ALU.mult)
                if k < KT - 1:
                    chain.note(last)
            chain.wait()
            last.then_inc(mem_normed, 1)
            ahead(CHUNK["sgu_v"] + 1)
            wait_evacuated(dve, TILE["sgu_v"])
            for b in range(2):
                chain.note(V.bn_stats(stats[:, b, :], vg[:, b, :]))
            chain.wait()
            for b in range(2):
                last = V.bn_aggr(mv[:, b, :], stats[:, b, :])
                if b == 0:
                    chain.link(last)
            last.then_inc(sgu_var, 1)
            ahead(CHUNK["sgu_u"])
            ahead(CHUNK["sgu_u"] + 1)
            n, t = CHUNK["cmp"], TILE["cmp"]
            for c in range(3):
                ahead(n + c)
            wait_chunk(dve, n + 3)
            freed(V.tensor_copy(ch[0:64, :], acc(t)[0:64, 0:S]), t)
            ahead(n + 3)
            n, t = CHUNK["vsw"], TILE["vsw"]
            ahead(n)
            dve.wait_ge(mem_hi, 1)
            V.tensor_tensor(ML[:, :, :], mem_raw, MH[:, :, :].bitcast(F32), ALU.subtract).then_inc(mem_lo, 1)
            ahead(n + 1)
            wait_chunk(dve, n + 1)
            freed(V.tensor_copy(Vtok[:, :, :, :].rearrange("p r b c -> p b r c"),
                                acc(t)[:, :].rearrange("p (b r c) -> p b r c", b=2, r=2)), t)
            dve.wait_ge(sgu_root, 1)
            chain.link(V.reciprocal(rs2, rs2))
            for b in range(2):
                chain.note(V.tensor_scalar(vn[:, b, :], vg[:, b, :], mv[:, b, 0:1], rs2[:, b:b + 1], ALU.subtract, ALU.mult))
            chain.wait()
            for gain, op in (("sgu_g", ALU.mult), ("sgu_b", ALU.add)):
                last = V.tensor_tensor(vn[:, :, :], vn[:, :, :], col(gain, 0, 256).unsqueeze(1).to_broadcast([P, 2, 256]), op)
                if op == ALU.mult:
                    chain.link(last)
            last.then_inc(sgu_normed, 1)
            for j in range(2):
                ahead(CHUNK["pool"] + j)
            dve.wait_ge(cmp_out, 1)
            V.tensor_scalar(kcmp[:, 0:NCMP], OB[0][:, 0:NCMP], col("cmp_b2k"), None, ALU.add).then_inc(cmp_kv, 1)
            for g in range(GROUPS):
                chain.note(V.tensor_tensor(vcmp[:, g, :], OB[0][:, 64 + g * HD:64 + (g + 1) * HD], col("cmp_b2v", 0, 64), ALU.add))
            chain.wait()
            dve.wait_ge(vx_zero, 1)
            for j in range(4):
                last = V.tensor_copy(VX[32 * j:32 * j + 32, :, j, :], vcmp[32 * j:32 * j + 32, :, :])
                if j < 3:
                    chain.note(last)
            chain.wait()
            last.then_inc(cmp_kv, 1)
            for j, name in enumerate(("ks", "kw")):
                n, t = CHUNK[name], TILE[name]
                ahead(n)
                wait_chunk(dve, n)
                freed(V.tensor_copy(kT[:, j, :], acc(t)[:, 0:S]), t)
            ahead(CHUNK["q"])
            ahead(CHUNK["q"] + 1)
            dve.wait_ge(sgu_mixed, 1)
            dve.wait_ge(sgu_normed, 1)
            sbias = col("sgu_bias", 0, 256).rearrange("p (a b) -> p a b", a=2)
            for j in range(2):
                last = V.tensor_tensor(vg[:, j, :].rearrange("p (n t) -> p n t", n=2), OB[1][:, j * S:(j + 1) * S].rearrange("p (n t) -> p n t", n=2),
                                       sbias[:, j, :].unsqueeze(1).to_broadcast([P, 2, P]), ALU.add)
                if j == 0:
                    chain.note(last)
            last.then_inc(sgu_mixed, 1)
            chain.wait()
            dve.wait_ge(sgu_mixed, 2)
            ahead(CHUNK["q"] + 2)
            ahead(CHUNK["q"] + 3)
            for j in range(2):
                wait_evacuated(dve, TILE["sgu_u"] + j)
            V.tensor_tensor(vg[:, :, :], vg[:, :, :], uT[:, :, :], ALU.mult).then_inc(sgu_gated, 1)
            ahead(CHUNK["gates"])
            dve.wait_ge(gate_turned, 1)
            chain.link(V.tensor_scalar(gtok[:, :, :], OB[1][:, 0:48].rearrange("p (a b) -> p a b", a=2), 1.0, None, ALU.add))
            chain.link(V.reciprocal(gtok[:, :, :], gtok[:, :, :]))
            dve.wait_ge(pool_mixed, 1)
            for j in range(2):
                for r in range(2):
                    V.tensor_scalar(t512[r * HD:(r + 1) * HD, j * S:(j + 1) * S],
                                    PTB[r * HD:(r + 1) * HD, r * 512 + j * S:r * 512 + (j + 1) * S],
                                    col("pool_scale", j)[r * HD:(r + 1) * HD], None, ALU.mult).then_inc(pool_scaled, 1)
            dve.wait_ge(cs_ready, 1)
            for b in range(2):
                first = NCMP - 1 + b * P // CSTRIDE
                for g in range(GROUPS):
                    chain.note(V.tensor_tensor(Sc[:, b, 4 * g:4 * g + 4, :],
                                               SC[:, g * 512 + b * 60:g * 512 + (b + 1) * 60].rearrange("p (j c) -> p j c", j=4),
                                               cb[:, first::-1, g:HEADS:2][:, 0:NCMP, :].rearrange("p c h -> p h c"), ALU.add))
            chain.wait()
            sc = Sc[:, :, :, :].rearrange("p b h c -> p (b h) c")
            chain.link(V.tensor_reduce(m16, sc, AX.X, ALU.max))
            chain.link(V.tensor_scalar(m16, m16, MASKED * 1e-10, None, ALU.max))
            V.tensor_tensor(sc, sc, m16.unsqueeze(2).to_broadcast([P, 16, NCMP]), ALU.subtract).then_inc(cs_shifted, 1)
            dve.wait_ge(cs_exp, 1)
            chain.link(V.tensor_reduce(s16, sc, AX.X, ALU.add))
            chain.link(V.tensor_scalar(s16, s16, 1.0, None, ALU.max))
            chain.link(V.reciprocal(s16, s16))
            gate = gtok[:, :, :].rearrange("p b (h r) -> p b h r", r=3)
            chain.link(V.tensor_tensor(s16.rearrange("p (b h) -> p b h", b=2), s16.rearrange("p (b h) -> p b h", b=2),
                                       gate[:, :, :, 0], ALU.mult))
            dve.wait_ge(pc_zero, 1)
            for b in range(2):
                last = V.tensor_tensor(Pc[:, b, :, :, 0:NCMP].rearrange("p g j c -> p (g j) c"), Sc[:, b, :, :],
                                       s16[:, 8 * b:8 * b + 8].unsqueeze(2).to_broadcast([P, 8, NCMP]), ALU.mult)
                if b == 0:
                    chain.link(last)
            last.then_inc(cp_ready, 1)

            def out_lo(j):
                dve.wait_ge(act_hi, j + 1)
                V.tensor_tensor(a_lo(j), OB[j % 2][:, 0:S], a_hi(j).bitcast(F32), ALU.subtract).then_inc(act_lo, 1)

            dve.wait_ge(bias_loaded, 16)
            for h in range(HEADS):
                n, t = CHUNK["mk"] + 2 * h, TILE["mk"] + 2 * h
                ahead(n)
                dve.wait_ge(scores, h + 1)
                if h:
                    dve.wait_ge(turned, h)
                chain.note(V.tensor_tensor(Sx[:, 0:S].rearrange("p (r s) -> p r s", r=2), SC[:, 0:S].rearrange("p (r s) -> p r s", r=2),
                                           bias[:, h, 127::-1].unsqueeze(1).to_broadcast([P, 2, P]), ALU.add))
                chain.link(V.tensor_tensor(Sx[:, S:768].rearrange("p (r s) -> p r s", r=2), SC[:, 512:1024].rearrange("p (r s) -> p r s", r=2),
                                           bias[:, h, 255::-1].unsqueeze(1).to_broadcast([P, 2, S]), ALU.add))
                chain.note(V.tensor_reduce(mx4[:, 0:2], Sx[:, 0:S].rearrange("p (r s) -> p r s", r=2), AX.X, ALU.max, negate=True))
                last = V.tensor_reduce(mx4[:, 2:4], Sx[:, S:768].rearrange("p (r s) -> p r s", r=2), AX.X, ALU.max, negate=True)
                chain.wait()
                last.then_inc(max_ready, 1)

                def evac(c):
                    wait_chunk(dve, n + c)
                    freed(V.tensor_copy(KTm[:, 2 * h + c, :], acc(t + c)[:, 0:S]), t + c)

                if h < HEADS // 2:
                    evac(0)
                dve.wait_ge(exped, h + 1)
                chain.link(V.reciprocal(rc4, sm4))
                hh = 4 * (h % 2) + h // 2
                chain.link(V.tensor_tensor(rc4.rearrange("p (b r) -> p b r", b=2), rc4.rearrange("p (b r) -> p b r", b=2),
                                           gtok[:, :, 3 * hh + 1:3 * hh + 3], ALU.mult))
                for b in range(4):
                    a, w = (P * b, P) if b < 2 else (S * (b - 1), S)
                    last = V.tensor_scalar(Sx[:, a:a + w], Sx[:, a:a + w], rc4[:, b:b + 1], None, ALU.mult)
                    if b < 3:
                        chain.note(last)
                chain.wait()
                last.then_inc(probs, 1)
                ahead(n + 1)
                if h < HEADS // 2:
                    evac(1)
                else:
                    q = h - HEADS // 2
                    t = TILE["mv"] + q
                    wait_chunk(dve, n + 1)
                    freed(V.tensor_copy(VM[:, 2 * q:2 * q + 2, :, :].rearrange("p r b c -> p b r c"),
                                        acc(t)[:, :].rearrange("p (b r c) -> p b r c", b=2, r=2)), t)
                if h >= 2 and h % 2 == 0:
                    out_lo(h // 2 - 1)
            out_lo(3)
            for j in range(2):
                dve.wait_ge(act_hi, 5 + j)
                V.tensor_tensor(a_lo(4 + j), t512[:, j * S:(j + 1) * S], a_hi(4 + j).bitcast(F32), ALU.subtract).then_inc(act_lo, 1)
            for j in range(2):
                dve.wait_ge(act_hi, 7 + j)
                V.tensor_tensor(a_lo(6 + j), vg[:, j, :], a_hi(6 + j).bitcast(F32), ALU.subtract).then_inc(act_lo, 1)
            for m in range(KT):
                ahead(CHUNK["w_out"] + m)
            post_norm(NORM_MIX, 0, "g_mem_pre", META)
            reciprocal_root(NORM_X1, META)

            def m_maximum(h):
                dve.wait_ge(m_scores, h + 1)
                V.tensor_reduce(small[:, 16 + 2 * h:18 + 2 * h], SC[:, (h % 2) * 512:(h % 2) * 512 + 512].rearrange("p (b m) -> p b m", b=2),
                                AX.X, ALU.max, negate=True).then_inc(m_max, 1)

            def m_normalise(h):
                dve.wait_ge(m_exped, h + 1)
                chain.link(V.reciprocal(small[:, 32 + 2 * h:34 + 2 * h], small[:, 24 + 2 * h:26 + 2 * h]))
                for b in range(2):
                    last = V.tensor_scalar(Em[:, h % 2, b, :], Em[:, h % 2, b, :], small[:, 32 + 2 * h + b:33 + 2 * h + b], None, ALU.mult)
                    if b == 0:
                        chain.link(last)
                last.then_inc(m_probs, 1)

            def m_lo(h):
                dve.wait_ge(act_hi, 8 + h + 1)
                V.tensor_tensor(AL[:, 2 * h * S:(2 * h + 2) * S], OB[h % 2][:, :], AH[:, 2 * h * S:(2 * h + 2) * S].bitcast(F32),
                                ALU.subtract).then_inc(act_lo, 1)

            for m in range(KT):
                n, t = CHUNK["mq"] + m, TILE["mq"] + m
                wait_chunk(dve, n)
                freed(V.scalar_tensor_tensor(out=qM[:, m, :], in0=acc(t)[:, 0:S], scalar=(D // MEM_HEADS) ** -0.5, in1=rstd[:, META:T],
                                             op0=ALU.mult, op1=ALU.mult), t)
                ahead(n)
                if m >= 3 and m % 2 == 1:
                    m_maximum((m - 3) // 2)
                    m_normalise((m - 3) // 2)
                if m == 7:
                    m_lo(0)
            m_maximum(3)
            m_normalise(3)
            for h in range(1, 4):
                m_lo(h)
            for m in range(KT):
                ahead(CHUNK["mo"] + m)
            post_norm(NORM_MEMOUT, 1, "g_ffn_pre", META)
            reciprocal_root(NORM_X2, META)
            taps = col("ffn_conv", 0, 176).rearrange("p (a b) -> p a b", b=8)

            def ffn_dve(p, i, first=False):
                for v in range(2):
                    n, t = CHUNK["up"] + 2 * p + v, TILE["up"] + 2 * p + v
                    wait_chunk(dve, n, i)
                    if not first:
                        dve.wait_ge(u_tapped, 2 * p + v - 1 + 4 * i)
                    freed(V.tensor_tensor(Ut[:, v, :], acc(t)[:, 0:S], rstd[:, META:T], ALU.mult), t)
                    if v:
                        ffn_taps(p, 0, i)
                    elif not first:
                        ffn_taps(p - 1, 1, i)
                    ahead(n, i)

            def ffn_taps(p, v, i):
                dst = (Gt, Vt)[v][:, p % 2, :]
                dve.wait_ge(f_init, 2 * p + v + 1 + 4 * i)
                chain.link(V.scalar_tensor_tensor(out=dst[:, 1:S], in0=Ut[:, v, 0:S - 1], scalar=taps[:, p + 2 * i, 4 * v + 1:4 * v + 2],
                                                  in1=dst[:, 1:S], op0=ALU.mult, op1=ALU.add))
                V.scalar_tensor_tensor(out=dst[:, 2:S], in0=Ut[:, v, 0:S - 2], scalar=taps[:, p + 2 * i, 4 * v:4 * v + 1],
                                       in1=dst[:, 2:S], op0=ALU.mult, op1=ALU.add).then_inc(u_tapped, 1)

            ffn_dve(0, 0, first=True)
            for i in range(8):
                for p in (1, 2):
                    ffn_dve(p, i)
            for p in range(17, FFN_TILES):
                ffn_dve(p, 0)
            ffn_taps(FFN_TILES - 1, 1, 0)
            for c in range(24):
                ahead(CHUNK["down"] + c)
            post_norm(NORM_FFN, 2, "g_conv", 0)
            reciprocal_root(NORM_H0, 0)
            V.tensor_tensor(rstd2, rstd[:, :], rstd[:, :], ALU.mult).then_inc(squared_rstd, 1)
            ctaps = col("conv_taps", 0, 48).rearrange("p (a b) -> p a b", b=3)
            chain.link(V.memset(CX[:, 0:2], 0.0))
            base_hi = 12 + FFN_TILES

            def conv_dve(i):
                n, t = CHUNK["conv_in"], TILE["conv_in"]
                wait_chunk(dve, n, i)
                freed(V.tensor_tensor(cT, acc(t)[:, 0:T], rstd2, ALU.mult), t)
                ahead(n, i)
                wait_chunk(dve, n + 1, i)
                wait_evacuated(dve, t, i)
                freed(V.tensor_tensor(CX[:, 2:T + 2], acc(t + 1)[:, 0:T], cT, ALU.mult), t + 1)
                wait_evacuated(dve, t + 1, i)
                chain.link(V.tensor_scalar(Yc, CX[:, 2:T + 2], ctaps[:, i, 2:3], None, ALU.mult))
                chain.link(V.scalar_tensor_tensor(out=Yc, in0=CX[:, 1:T + 1], scalar=ctaps[:, i, 1:2], in1=Yc, op0=ALU.mult, op1=ALU.add))
                V.scalar_tensor_tensor(out=Yc, in0=CX[:, 0:T], scalar=ctaps[:, i, 0:1], in1=Yc, op0=ALU.mult, op1=ALU.add).then_inc(c_conv, 1)
                ahead(n + 1, i)
                wait_chunk(dve, n + 2, i)
                freed(V.tensor_tensor(ZZ, acc(t + 2)[:, 0:T], rstd[:, :], ALU.mult), t + 2)
                ahead(n + 2, i)
                dve.wait_ge(c_sig, 1 + i)
                chain.link(V.tensor_tensor(ZZ, ZZ, SZ, ALU.mult))
                dve.wait_ge(c_scaled, 1 + i)
                chain.link(V.tensor_tensor(Yc, Yc, ZZ, ALU.mult))
                wait_chunk(dve, n + 3, i)
                freed(V.tensor_tensor(Fc, acc(t + 3)[:, 0:T], Yc, ALU.mult), t + 3)
                ahead(n + 3, i)
                dve.wait_ge(act_hi, base_hi + 1 + i)
                V.tensor_tensor(a_lo(i, T), Fc, a_hi(i, T).bitcast(F32), ALU.subtract).then_inc(act_lo, 1)

            dve.wait_ge(squared_rstd, 1)
            for i in range(E_TILES):
                conv_dve(i)
            for m in range(KT):
                n, t = CHUNK["conv_out"] + 2 * m, TILE["conv_out"] + m
                ahead(n)
                ahead(n + 1)
                wait_chunk(dve, n + 1)
                freed(V.tensor_tensor(XR[:, m, :], acc(t)[:, 0:T], XR[:, m, :], ALU.add), t)
                raw_rest(RAW_H1, "g_mlstm", 0, m)
            reciprocal_root(NORM_H1, 0)

            def lk_tiles(first, end):
                for m in range(first, end):
                    n, t = CHUNK["lk"] + m, TILE["lk"] + m
                    wait_chunk(dve, n)
                    freed(V.tensor_tensor(lk[:, m, :], acc(t)[:, 0:T], rstd[:, :], ALU.mult), t)
                    ahead(n)
                    apply_norm(PRE_H1, "g_mlstm", 0, l_in(AH, 0), l_in(AL, 0), m)

            n, t = CHUNK["lgates"], TILE["lgates"]
            wait_chunk(dve, n)
            freed(V.tensor_tensor(gx[0:36, :], acc(t)[0:36, 0:T], rstd[0:36, :], ALU.mult), t)
            ahead(n)
            lk_tiles(0, 5)
            chain.note(V.memset(gone[0:LHEADS, :], 1.0))
            dve.wait_ge(g_raw, 1)
            chain.note(V.tensor_scalar(lf[32:36, :], gx[32:36, :], 0.0, None, ALU.min))
            chain.wait()
            dve.wait_ge(g_ln, 1)
            chain.link(V.tensor_tensor(lf[0:LHEADS, :], lf[32:36, :], gl[32:36, :], ALU.subtract))
            chain.link(V.tensor_tensor_scan(gF[0:LHEADS, :], gone[0:LHEADS, :], lf[0:LHEADS, :], 0.0, ALU.mult, ALU.add))
            V.tensor_tensor(gA[0:LHEADS, :], gx[0:LHEADS, :], gF[0:LHEADS, :], ALU.subtract).then_inc(g_rows, 1)
            dve.wait_ge(g_rows, 1)
            chain.link(V.tensor_tensor_scan(gM[0:LHEADS, :], gone[0:LHEADS, :], gA[0:LHEADS, :], 0.0, ALU.mult, ALU.max))
            V.tensor_scalar(negM, gM[0:LHEADS, :], -1.0, None, ALU.mult).then_inc(g_rows, 1)
            dve.wait_ge(g_rows, 2)
            V.tensor_tensor(negFM, negM, gF[0:LHEADS, :], ALU.subtract).then_inc(g_rows, 1)
            lk_tiles(5, KT)
            apply_norm(PRE_H1, "g_mlstm", 0, l_in(AH, 0), l_in(AL, 0), KT)
            dve.wait_ge(g_turned, 1)
            chain.note(V.tensor_copy(acol[0:META, 0, :], OB[0][0:META, 0:4]))
            last = V.tensor_copy(acol[:, 1:3, :], OB[0][:, 4:12].rearrange("p (a b) -> p a b", a=2))
            chain.wait()
            last.then_inc(g_cols, 1)
            for m in range(KT):
                ahead(CHUNK["lq"] + m)

            def l_weights(h):
                dve.wait_ge(l_scores, h + 1)
                dve.wait_ge(l_masked, 2 * h + 2)
                V.tensor_tensor(Pl[:, 0:S], SC[:, 0:S], Dl[:, 0:S], ALU.mult).then_inc(l_probs, 1)
                V.tensor_tensor(Pl[:, S:S + P], SC[:, S:S + P], Dl[:, S:S + P], ALU.mult).then_inc(l_probs, 1)
                V.tensor_tensor(Pl[0:META, 384:640], SC[0:META, 512:512 + S], Dl[0:META, 384:640], ALU.mult).then_inc(l_probs, 1)

            def v_copy(m):
                dve.wait_ge(l_vturned, m + 1)
                o = OB[m % 2]
                c = slice(m * P, (m + 1) * P)
                chain.note(V.tensor_copy(lv[0:META, 2, c], o[0:META, 2 * P:3 * P]))
                last = V.tensor_copy(lv[:, 0:2, c], o[:, 0:2 * P].rearrange("p (a b) -> p a b", a=2))
                chain.wait()
                last.then_inc(l_vcopied, 1)

            for m in range(E_TILES):
                ahead(CHUNK["lv"] + m)
                if m >= 2:
                    v_copy(m - 2)
                if m == 6:
                    l_weights(0)
            v_copy(E_TILES - 2)
            v_copy(E_TILES - 1)
            base_hi = 12 + FFN_TILES + E_TILES

            def l_lo(e):
                dve.wait_ge(act_hi, base_hi + e + 1)
                V.tensor_tensor(l_out(AL, e), hn[:, e % 4, :], l_out(AH, e).bitcast(F32), ALU.subtract).then_inc(act_lo, 1)

            for h in range(LHEADS):
                n, t = CHUNK["oz"] + 8 * h, TILE["oz"] + 8 * h
                dve.wait_ge(l_num, h + 1)
                dve.wait_ge(l_decay, 2 * h + 2)
                if h:
                    dve.wait_ge(act_hi, base_hi + 4 * h)
                chain.link(V.scalar_tensor_tensor(out=rden, in0=PTB[:, 512:512 + S], scalar=-1.0, in1=em, op0=ALU.mult, op1=ALU.max))
                chain.link(V.tensor_tensor(rden, PTB[:, 512:512 + S], rden, ALU.max))
                chain.link(V.reciprocal(rden, rden))
                for v in range(2):
                    last = V.tensor_tensor(hn[:, 2 * v:2 * v + 2, :], OB[v][:, :].rearrange("p (a b) -> p a b", a=2),
                                           rden.unsqueeze(1).to_broadcast([P, 2, S]), ALU.mult)
                    if v == 0:
                        chain.link(last)
                last.then_inc(l_hn, 1)
                for m in range(3):
                    ahead(n + m)
                if h + 1 < LHEADS:
                    l_weights(h + 1)
                ahead(n + 3)
                dve.wait_ge(l_root, h + 1)
                chain.link(V.reciprocal(rhead, lroot))
                chain.link(V.tensor_tensor(hn[:, :, :], hn[:, :, :], rhead.unsqueeze(1).to_broadcast([P, 4, S]), ALU.mult))
                for m in range(4):
                    e = 4 * h + m
                    ahead(n + 4 + m)
                    wait_evacuated(dve, t + m)
                    chain.link(V.scalar_tensor_tensor(out=hn[:, m, :], in0=hn[:, m, :], scalar=col("head_norm", e), in1=so[:, m, :],
                                                      op0=ALU.mult, op1=ALU.mult))
                    dve.wait_ge(z_sig, e + 1)
                    chain.link(V.tensor_tensor(hn[:, m, :], hn[:, m, :], tz[:, m % 2, :], ALU.mult))
                    freed(V.tensor_tensor(hn[:, m, :], acc(t + 4 + m)[:, 0:S], hn[:, m, :], ALU.mult), t + 4 + m)
                    if m:
                        l_lo(e - 1)
                l_lo(4 * h + 3)
            for m in range(KT):
                n, t = CHUNK["lout"] + 2 * m, TILE["lout"] + m
                ahead(n)
                ahead(n + 1)
                wait_chunk(dve, n + 1)
                freed(V.tensor_tensor(XR[:, m, META:T], acc(t)[:, 0:S], XR[:, m, META:T], ALU.add), t)
            reciprocal_root(NORM_FINAL, META)
            for k in range(KT):
                V.scalar_tensor_tensor(out=SQ[:, k, META:T], in0=XR[:, k, META:T], scalar=col("g_final", k), in1=rstd[:, META:T],
                                       op0=ALU.mult, op1=ALU.mult).then_inc(normed, 1)


def _tiles(np, w, cols):
    k = w.shape[0] // P
    return w[:, cols].reshape(k, P, len(cols)).transpose(1, 0, 2).reshape(P, -1)


def _pack_weights(np, a):
    ar = np.arange

    def lin(w):
        return [_tiles(np, w, ar(m * P, (m + 1) * P)) for m in range(w.shape[1] // P)]

    def pad(c):
        return np.concatenate([c, np.zeros((P, D - c.shape[1]), c.dtype)], axis=1)

    def narrow(w, at):
        out = np.zeros((D, P), w.dtype)
        out[:, at] = w
        return _tiles(np, out, ar(P))

    def deep(w):
        rows = [w[r:r + D] for r in range(0, w.shape[0], D)]
        return [pad(_tiles(np, r, ar(m * P, (m + 1) * P))) for m in range(KT) for r in rows]

    w = a["w_in"][0]
    q, kc, vc, ks, vs, kw, vw, gt, pin, u, v = np.split(w, np.cumsum([512] + [128] * 6 + [24, 256, 256]), axis=1)
    pairs = [np.concatenate([ar(j * HD, (j + 1) * HD), ar((j + 4) * HD, (j + 5) * HD)]) for j in range(4)]
    parts = lin(kc) + lin(vc) + lin(v) + lin(u)
    for r in (0, D):
        parts += [_tiles(np, a["cmp_w1"][0, kv].reshape(2048, P)[r:r + D], ar(P)) for kv in range(2)]
    parts += lin(vs) + lin(vw) + lin(pin) + lin(ks) + lin(kw) + [_tiles(np, q, p) for p in pairs] + [narrow(gt, ar(24))]
    mv = lin(a["w_mv"][0])
    parts += lin(a["w_mk"][0]) + [mv[m ^ 1 if (CHUNK["mv"] + m - m % 2) % SLOTS == SLOTS - 1 else m] for m in range(KT)]
    rows = np.concatenate(pairs + [ar(512, 1024)])
    parts += lin(a["w_out"][0][rows]) + lin(a["w_mq"][0]) + lin(a["w_mo"][0])
    up = a["w_up"][0]
    for j in range(FFN_TILES):
        parts += [_tiles(np, up, ar(c, c + P)) for c in (j * P, (FFN_TILES + j) * P)]
    parts += deep(a["w_down"][0])
    cin = a["conv_in_w_2"][0]
    for e in range(E_TILES):
        for part in (1, 2, 3, 0):
            parts.append(_tiles(np, cin, ar(part * 2048 + e * P, part * 2048 + (e + 1) * P)))
    parts += deep(a["conv_out_w_2"][0])
    lq, lk, lv, lo, lz, lg = np.split(a["mlstm_in_w_2"][0], [1024, 2048, 4096, 6144, 8192], axis=1)
    parts += [narrow(lg, np.concatenate([ar(4), ar(32, 36)]))] + lin(lk) + lin(lq) + lin(lv)
    o, z = lin(lo), lin(lz)
    for h in range(LHEADS):
        parts += o[4 * h:4 * h + 4] + z[4 * h:4 * h + 4]
    parts += deep(a["mlstm_out_w_2"][0])
    out = np.stack(parts)
    assert out.shape == (NCHUNKS, P, D)
    return out


def _pack_params(np, a):
    def cols(v):
        return v.reshape(-1, P).T

    def rows(v):
        return np.broadcast_to(v[None, :], (P, v.shape[0]))

    f = {}
    for name, key in (("g_mix_pre", "mix_norm_pre"), ("g_mix_post", "mix_norm_post"), ("g_mem_pre", "mem_norm_pre"),
                      ("g_mem_kv", "mem_norm_kv"), ("g_mem_post", "mem_norm_post"), ("g_ffn_pre", "ffn_norm_pre"),
                      ("g_ffn_post", "ffn_norm_post"), ("pool_scale", "pool_scale"), ("cmp_b1", "cmp_b1")):
        f[name] = cols(a[key][0])
    f["g_conv"], f["g_mlstm"] = cols(a["norm_w_2"][0]), cols(a["norm_w_2"][1])
    f["g_final"] = cols(a["final_norm_w_2"])
    f["cmp_b2k"] = np.concatenate([a["cmp_b2"][0, 0]] * 2)[:, None]
    f["cmp_b2v"] = rows(a["cmp_b2"][0, 1])
    f["cmp_pos"] = a["cmp_pos"][0].reshape(2, 16, P).transpose(2, 0, 1).reshape(P, 32)
    f["cmp_w2"] = a["cmp_w2"][0].transpose(1, 0, 2).reshape(P, 128)
    f["sgu_g"], f["sgu_b"] = rows(a["sgu_norm_g"][0]), rows(a["sgu_norm_b"][0])
    sb = a["sgu_b"][0]
    f["sgu_bias"] = np.concatenate([np.repeat(sb[2 * j:2 * j + 2], HD, axis=0) for j in range(2)], axis=1)
    f["sgu_w"] = a["sgu_w"][0].transpose(2, 0, 1).reshape(P, 512)
    pw = a["pool_w"][0]
    f["pool_w"] = np.concatenate([pw[0:2].reshape(P, HD), pw[2:4].reshape(P, HD)], axis=1)
    tokens = np.arange(S)
    inv = [1.0 / np.minimum(tokens + 1, w) for w in (2, 4, 8, 16)]
    f["pool_inv"] = np.concatenate([np.repeat(np.stack(inv[2 * j:2 * j + 2]), HD, axis=0) for j in range(2)], axis=1).astype(np.float32)
    cw, cbias = a["conv_w"][0], a["conv_b"][0]
    four = np.concatenate([cw, cbias[None]], axis=0).reshape(4, 2, FFN_TILES, P)
    f["ffn_conv"] = four.transpose(3, 2, 1, 0).reshape(P, 176)
    f["conv_taps"] = a["conv_w_2"][0].reshape(3, E_TILES, P).transpose(2, 1, 0).reshape(P, 48)
    f["head_norm"] = cols(a["mlstm_head_norm_w_2"][0])
    gb = np.zeros((P, 1), np.float32)
    gb[0:4, 0], gb[32:36, 0] = a["mlstm_gate_b_2"][0][0:4], a["mlstm_gate_b_2"][0][4:8]
    f["gate_b"] = gb
    return np.concatenate([f[name] for name, _ in _COLS], axis=1)


def _onehot(np):
    import math
    d = np.arange(512) - 256
    n = np.maximum(d, 1).astype(np.float32)
    large = 16 + (np.log(n / np.float32(16)) / np.float32(math.log(64.0)) * np.float32(16)).astype(np.int32)
    bucket = np.where(d < 16, d, np.minimum(large, 31))
    bucket = np.where(d < 0, 32, bucket)
    return (np.arange(33)[:, None] == bucket[None, :]).astype(np.float32)


def kernel(**inputs):
    import numpy as np
    import concourse.bacc as bacc
    from concourse.bass_utils import run_bass_kernel_spmd as run

    a = {k: np.asarray(v) for k, v in inputs.items()}
    order = [j + 4 * g for j in range(4) for g in range(2)]

    def feature_major(v):
        return v.T.reshape(KT, P, -1).transpose(1, 0, 2)

    arrays = {
        "weights": _pack_weights(np, a),
        "x_t": feature_major(a["x"][0]),
        "mem_t": feature_major(a["mem"][0]),
        "meta_t": feature_major(a["meta_tokens_2"]),
        "params": _pack_params(np, a),
        "rel_bias": a["rel_bias"][:, order],
        "onehot": _onehot(np),
    }
    arrays = {k: np.ascontiguousarray(v) for k, v in arrays.items()}
    nc = bacc.Bacc("TRN2", target_bir_lowering=False, num_devices=1)
    args = [nc.dram_tensor(k, v.shape, F32, kind="ExternalInput").ap() for k, v in arrays.items()]
    out = nc.dram_tensor("out_t", (D, S), F32, kind="ExternalOutput").ap()
    bias_rows = nc.dram_tensor("bias_rows", (HEADS, 512), F32, kind="Internal").ap()
    build(nc, *args, out, bias_rows)
    r = run(nc, [arrays], core_ids=[0])
    return np.ascontiguousarray(r.results[0]["out_t"].T)[None]
```

```python
from contextlib import ExitStack

import concourse.bass as bass
from concourse import mybir

F32 = mybir.dt.float32
F32R = mybir.dt.float32r
ALU = mybir.AluOpType
ACT = mybir.ActivationFunctionType
AX = mybir.AxisListType

P = 128
S = 256
META = 16
T = META + S
D = 1024
KT = D // P
HEADS, GROUPS, HD = 8, 2, 64
NCMP = 15
CSTRIDE = 16
CMP_FIRST = P // CSTRIDE - 1
FFN_TILES = 22
E_TILES = 16
GELU_HEAD = 1
MEM_HEADS = 4
LHEADS = 4
EPS = 1e-6
MASKED = -1.0e30

SLOTS = 4
AHEAD = SLOTS - 1
_LAYOUT = [("kc", 1), ("vc", 1), ("vsw", 2), ("ks", 1), ("kw", 1), ("cmp", 4), ("q", 4), ("gates", 1), ("sgu_v", 2), ("sgu_u", 2),
           ("pool", 2), ("mk", 8), ("sgu_mix", 0), ("pool_mix", 0), ("w_out", 8), ("mv", 4), ("mq", 8), ("mv2", 4),
           ("mo", 8), ("up", 44), ("down", 24), ("conv_in", 64), ("conv_out", 16), ("lgates", 1), ("lk", 8),
           ("lq", 8), ("lv", 16), ("oz", 32), ("lout", 16)]
CHUNK = {}
NCHUNKS = 0
for _name, _n in _LAYOUT:
    CHUNK[_name] = NCHUNKS
    NCHUNKS += _n
_TILES = dict(sgu_v=1, cmp=1, vsw=1, sgu_mix=1, pool_mix=2, mv=2, mv2=2, down=8, conv_out=8, lout=8)
TILE = {}
_t = 0
for _name, _n in _LAYOUT:
    TILE[_name] = _t
    _t += _TILES.get(_name, _n)

_COLS = [("g_mix_pre", 8), ("g_mix_post", 8), ("g_mem_pre", 8), ("g_mem_kv", 8), ("g_mem_post", 8),
         ("g_ffn_pre", 8), ("g_ffn_post", 8), ("g_conv", 8), ("g_mlstm", 8), ("g_final", 8),
         ("pool_scale", 2), ("cmp_b1", 2), ("cmp_b2k", 1), ("cmp_b2v", 64), ("cmp_pos", 32), ("cmp_w2", 128),
         ("sgu_g", 256), ("sgu_b", 256), ("sgu_bias", 256), ("sgu_w", 512), ("pool_w", 128), ("pool_inv", 512),
         ("ffn_conv", 176), ("conv_taps", 48), ("head_norm", 16), ("gate_b", 1)]
COL = {}
NCOLS = 0
for _name, _n in _COLS:
    COL[_name] = NCOLS
    NCOLS += _n
GAINS = COL["pool_scale"]

NORM_X, NORM_MEM, NORM_MIX, NORM_X1, NORM_MEMOUT, NORM_X2, NORM_FFN, NORM_H0, NORM_H1, NORM_FINAL = range(10)
PRE_X, PRE_H1 = range(2)
RAW_X1, RAW_X2, RAW_H0, RAW_H1 = range(4)
ACT_MEM = 4
ACT_FFN = ACT_MEM + MEM_HEADS
ACT_CONV = ACT_FFN + FFN_TILES
ACT_LSTM = ACT_CONV + E_TILES
SQ_H1, SQ_FINAL = 32, 40
WARM = 28
WARM_START, WARM_X = 10, 12
POOL_FROM = 6


def span(k, w):
    return slice(k * w, (k + 1) * w) if isinstance(k, int) else bass.ds(k * w, w)


class Chain:

    def __init__(self, eng, sem):
        self.eng, self.sem, self.count = eng, sem, 0
        self.earlier = 0

    def begin_round(self, i, notes):
        self.earlier, self.body_end = notes * i, self.count + notes

    def end_rounds(self, rounds, notes):
        assert self.count == self.body_end
        self.earlier, self.count = 0, self.count + notes * (rounds - 1)

    def note(self, ins):
        ins.then_inc(self.sem, 1)
        self.count += 1
        return ins

    def wait(self):
        self.eng.wait_ge(self.sem, self.count + self.earlier)

    def link(self, ins):
        self.note(ins)
        self.wait()


def build(nc, weights, x_in, mem_in, meta_in, params, rel_bias, onehot, out, bias_rows):
    with ExitStack() as ctx:
        def sb(name, shape, dt=F32):
            return ctx.enter_context(nc.sbuf_tensor(name, shape, dt))

        def sem(name):
            return ctx.enter_context(nc.semaphore(name))

        def psum(name, cols):
            return ctx.enter_context(nc.psum_tensor(name, [P, cols], F32))

        raw = sb("raw", [P, SLOTS, D])
        w_hi = sb("w_hi", [P, SLOTS, D], F32R)
        w_lo = sb("w_lo", [P, SLOTS, D], F32R)
        XR = sb("XR", [P, KT, T])
        XH = sb("XH", [P, KT, T], F32R)
        XL = sb("XL", [P, KT, T], F32R)
        MH = sb("MH", [P, KT, S], F32R)
        ML = sb("ML", [P, KT, S], F32R)
        AH = sb("AH", [P, E_TILES * T], F32R)
        AL = sb("AL", [P, E_TILES * T], F32R)
        cst = sb("cst", [P, NCOLS])
        ident = sb("ident", [P, P])
        ones_d = sb("ones_d", [P, P])
        ones_h = sb("ones_h", [P, P])
        ones_1 = sb("ones_1", [P, P])
        Y = sb("Y", [P, KT, T])
        SQ = sb("SQ", [P, KT, T])
        root = sb("root", [P, T])
        rstd = sb("rstd", [P, T])
        root_m = sb("root_m", [P, T])
        rstd_m = sb("rstd_m", [P, T])
        rb = sb("rb", [33, HEADS])
        sel = sb("sel", [LHEADS, LHEADS, P])
        small = sb("small", [P, 160])
        AR = sb("AR", [P, 12200])

        def col(name, i=0, w=1):
            return cst[:, COL[name] + i:COL[name] + i + w]

        def ar(off, *dims):
            n = 1
            for d in dims:
                n *= d
            v = AR[:, off:off + n]
            if len(dims) == 1:
                return v
            if len(dims) == 2:
                return v.rearrange("p (a b) -> p a b", a=dims[0])
            if len(dims) == 3:
                return v.rearrange("p (a b c) -> p a b c", a=dims[0], b=dims[1])
            return v.rearrange("p (a b c d) -> p a b c d", a=dims[0], b=dims[1], c=dims[2])

        bias = ar(0, HEADS, S)
        Sx = ar(2048, 768)
        PTx = ar(2816, 2, 384)
        RF = ar(2048, 16, 2, 2, 16)
        KC2 = ar(3584, 2, GROUPS, S)
        Pc = ar(3584, 2, 2, 4, 32)
        PcT = ar(4096, GROUPS, S)
        qT = ar(4608, 4, S)
        kT = ar(5632, 2, S)
        Vtok = ar(6144, 2, 2, P)
        VX = ar(6656, GROUPS, 4, HD)
        hc = ar(7168, GROUPS, 4, 32)
        hk = ar(7424, 32)
        kcmp = ar(12064, GROUPS, 16)
        vcmp = ar(7472, GROUPS, HD)
        Sc = ar(7840, 2, HEADS, NCMP)
        gT = ar(8080, S)
        gtok = ar(8336, 2, 24)
        m16 = ar(8384, 16)
        s16 = ar(8400, 16)
        KTm = ar(8448, KT, S)
        VM = ar(0, KT, 2, P)
        hot = ar(10496, 512)
        vec = ar(11008, 512)
        stats = ar(11520, 2, 6)
        mv = ar(11532, 2, 2)
        rs2 = ar(11536, 2)
        mx4 = ar(11540, 4)
        sm4 = ar(11544, 4)
        rc4 = ar(11548, 4)
        t512 = ar(11552, 512)
        ch = ar(4096, S)
        SS = sb("SS", [P, T])
        sqv = SQ[:, :, :].rearrange("p a b -> p (a b)")
        uT = sqv[:, 0:512].rearrange("p (a b) -> p a b", a=2)
        vg = sqv[:, 512:1024].rearrange("p (a b) -> p a b", a=2)
        vn = sqv[:, 1024:1536].rearrange("p (a b) -> p a b", a=2)
        yv = Y[:, :, :].rearrange("p a b -> p (a b)")
        pT = yv[:, 0:544].rearrange("p (a b) -> p a b", a=2)
        wA = yv[:, 544:1088].rearrange("p (a b) -> p a b", a=2)
        wB = yv[:, 1088:1632].rearrange("p (a b) -> p a b", a=2)
        pd = yv[:, 1632:2144].rearrange("p (a b) -> p a b", a=2)
        mem_raw = yv[:, 0:2048].rearrange("p (a b) -> p a b", a=KT)
        qM = ar(4608, KT, S)
        Em = ar(2048, 2, 2, S)
        PTm = ar(3072, 2, 2, S)
        Gt = ar(0, 2, S)
        Vt = ar(512, 2, S)
        Ft = ar(1024, 2, S)
        Ut = ar(1536, 2, S)
        cT = ar(0, T)
        CX = ar(512, T + 2)
        SZ = ar(1024, T)
        ZZ = ar(1536, T)
        Yc = ar(2048, T)
        Fc = ar(2560, T)
        rstd2 = ar(3072, T)
        lk = yv.rearrange("p (a b) -> p a b", a=KT)
        lq = sqv[:, 0:2048].rearrange("p (a b) -> p a b", a=KT)
        lv = ar(0, 3, 2048)
        so = ar(6144, 4, S)
        hn = ar(7168, 4, S)
        sqh = ar(8192, 4, S)
        Pl = ar(9216, 640)
        Dl = ar(9856, 640)
        em = ar(10496, S)
        rden = ar(10752, S)
        rhead = ar(11008, S)
        lroot = ar(11264, S)
        lvT = ar(11520, 2, T)
        tz = ar(11520, 2, S)
        gx = ar(6144, T)
        ge = ar(6416, T)
        gl = ar(6688, T)
        gF = ar(6960, T)
        gA = ar(7232, T)
        gM = ar(7504, T)
        gone = ar(7776, T)
        lf = ar(8048, T)
        negM = root_m[0:LHEADS, :]
        negFM = rstd_m[0:LHEADS, :]
        acol = small[:, 0:12].rearrange("p (a b) -> p a b", a=3)

        ACC = [psum("acc0", 512), psum("acc1", 512)]
        SC = psum("scores", 1024)
        PTB = psum("turned", 1024)
        OB = [psum("outs0", 512), psum("outs1", 512)]

        x_loaded = [sem("x_loaded0"), sem("x_loaded1")]
        meta_loaded, mem_loaded, params_loaded, gains_loaded = sem("meta_loaded"), sem("mem_loaded"), sem("params_loaded"), sem("gains_loaded")
        rf_zero, sum_ready, cmp_hidden, cmp_copied, rest_pool, x_updated_pool = (
            sem("rf_zero"), sem("sum_ready"), sem("cmp_hidden"), sem("cmp_copied"), sem("rest_pool"), sem("x_updated_pool"))
        rel_loaded = sem("rel_loaded")
        bias_stored, bias_loaded, out_stored = sem("bias_stored"), sem("bias_loaded"), sem("out_stored")
        weights_loaded = [sem(f"weights_loaded{s}") for s in range(SLOTS)]
        hi_ready, lo_ready, chunk_done = sem("hi_ready"), sem("lo_ready"), sem("chunk_done")
        evacuated = [sem("evacuated0"), sem("evacuated1")]
        consts_ready = sem("consts_ready")
        sgu_masked = sem("sgu_masked")
        sq_ready, stat_ready, root_ready = sem("sq_ready"), sem("stat_ready"), sem("root_ready")
        mem_sq, last_sq, mem_summed, pair_summed, l_summed = sem("mem_sq"), sem("last_sq"), sem("mem_summed"), sem("pair_summed"), sem("l_summed")
        raw_hi, raw_lo, squared_rstd, u_tapped = sem("raw_hi"), sem("raw_lo"), sem("squared_rstd"), sem("u_tapped")
        c_conv, c_scaled = sem("c_conv"), sem("c_scaled")
        normed, normed_hi, normed_lo = sem("normed"), sem("normed_hi"), sem("normed_lo")
        mem_normed, mem_hi, mem_lo = sem("mem_normed"), sem("mem_hi"), sem("mem_lo")
        rstd_ready = sem("rstd_ready")
        y_ready, x_updated = sem("y_ready"), sem("x_updated")
        act_ready, act_hi, act_lo = sem("act_ready"), sem("act_hi"), sem("act_lo")
        bias_vec, bias_copied = sem("bias_vec"), sem("bias_copied")
        cmp_in = sem("cmp_in")
        cmp_out, cmp_kv = sem("cmp_out"), sem("cmp_kv")
        pc_zero, hc_zero, vx_zero, sc_masked = sem("pc_zero"), sem("hc_zero"), sem("vx_zero"), sem("sc_masked")
        sgu_gelu, sgu_var, sgu_root, sgu_normed, sgu_mixed = (
            sem("sgu_gelu"), sem("sgu_var"), sem("sgu_root"), sem("sgu_normed"), sem("sgu_mixed"))
        pool_padded, pool_diff, pool_mixed = sem("pool_padded"), sem("pool_diff"), sem("pool_mixed")
        sgu_gated, mix_hi, mix_lo, kc_zero = sem("sgu_gated"), sem("mix_hi"), sem("mix_lo"), sem("kc_zero")
        gate_turned = sem("gate_turned")
        cs_ready, cs_shifted, cs_exp, cp_ready, cp_turned, cp_copied = (
            sem("cs_ready"), sem("cs_shifted"), sem("cs_exp"), sem("cp_ready"), sem("cp_turned"), sem("cp_copied"))
        scores, max_ready, exped, probs, turned, copied, outs = (
            sem("scores"), sem("max_ready"), sem("exped"), sem("probs"), sem("turned"), sem("copied"), sem("outs"))
        m_scores, m_max, m_exped, m_probs, m_turned, m_copied, m_outs = (
            sem("m_scores"), sem("m_max"), sem("m_exped"), sem("m_probs"), sem("m_turned"), sem("m_copied"), sem("m_outs"))
        f_init, f_gelu = sem("f_init"), sem("f_gelu")
        c_sig = sem("c_sig")
        g_raw, g_ln, g_rows, g_turned, g_cols = (
            sem("g_raw"), sem("g_ln"), sem("g_rows"), sem("g_turned"), sem("g_cols"))
        l_vturned, l_vcopied = sem("l_vturned"), sem("l_vcopied")
        l_scores, l_rows, l_decay, l_masked, l_probs, l_num, l_hn, l_sq, l_stat, l_root = (
            sem("l_scores"), sem("l_rows"), sem("l_decay"), sem("l_masked"), sem("l_probs"), sem("l_num"),
            sem("l_hn"), sem("l_sq"), sem("l_stat"), sem("l_root"))
        z_sig = sem("z_sig")
        vec_steps, act_steps, pool_steps = sem("vec_steps"), sem("act_steps"), sem("pool_steps")

        def acc(t):
            return ACC[t % 2]

        def wait_evacuated(eng, t, i=0):
            eng.wait_ge(evacuated[t % 2], t // 2 + 1 + 2 * i)

        def wait_chunk(eng, n, i=0):
            eng.wait_ge(chunk_done, n + 1 + 4 * i)

        def freed(ins, t):
            ins.then_inc(evacuated[t % 2], 1)

        def wait_y(eng, update):
            eng.wait_ge(y_ready, 7 * update + 7)
            wait_evacuated(eng, TILE[("w_out", "mo", "down")[update]] + KT - 1)

        def a_hi(k, w=S):
            return AH[:, span(k, w)]

        def a_lo(k, w=S):
            return AL[:, span(k, w)]

        def wait_rstd(eng, e):
            eng.wait_ge(rstd_ready, max(e, 1))

        def raw_parts(lo):
            return (lambda k: XH[:, k, lo:T]), (lambda k: XL[:, k, lo:T])

        def l_in(part, lo):
            return lambda k: part[:, (8 + k) * T + lo:(9 + k) * T]

        def l_out(part, k):
            if k < 8:
                return (XH if part is AH else XL)[:, k, 0:S]
            return (MH if part is AH else ML)[:, k - 8, :]

        def ffn_hi(k):
            return a_hi(k) if k < 16 else MH[:, k - 16, :]

        def ffn_lo(k):
            return a_lo(k) if k < 16 else ML[:, k - 16, :]

        block = ctx.enter_context(nc.Block())

        @block.sync
        def _(sp):
            sp.dma_start(rb[0:32, :], rel_bias).then_inc(rel_loaded, 16)
            sp.dma_start(hot[0:33, :], onehot).then_inc(rel_loaded, 16)
            for c in range(2):
                sp.dma_start(XR[:, 4 * c:4 * c + 4, META:T], x_in[:, 4 * c:4 * c + 4, :]).then_inc(x_loaded[c], 16)
            sp.dma_start(cst[:, 0:GAINS], params[:, 0:GAINS]).then_inc(gains_loaded, 16)

            def load(n, i=0):
                if n >= SLOTS:
                    sp.wait_ge(lo_ready, n - SLOTS + 1 + 4 * i)
                sp.dma_start(raw[:, n % SLOTS, :], weights[n + 4 * i]).then_inc(weights_loaded[n % SLOTS], 16)

            load(0)
            load(1)
            load(2)
            sp.dma_start(mem_raw, mem_in).then_inc(mem_loaded, 16)
            sp.dma_start(cst[:, GAINS:NCOLS], params[:, GAINS:NCOLS]).then_inc(params_loaded, 16)
            load(3)
            sp.dma_start(XR[:, :, 0:META], meta_in).then_inc(meta_loaded, 16)
            rounds = (NCHUNKS - SLOTS) // SLOTS
            with sp.Fori(0, rounds) as i:
                for s in range(SLOTS):
                    load(SLOTS + s, i)
            for n in range(SLOTS * (rounds + 1), NCHUNKS):
                load(n)
            for k in range(KT):
                sp.wait_ge(normed, 8 * 2 + k + 1)
                sp.dma_start(out[k * P:(k + 1) * P, :], SQ[:, k, META:T]).then_inc(out_stored, 16)
            sp.wait_ge(out_stored, 16 * KT)

        @block.gpsimd
        def _(pool):
            chain = Chain(pool, pool_steps)

            def sum_squares(ready, lo):
                ready(0)
                for m in range(1, KT - 1):
                    ready(m)
                    ins = nc.gpsimd.tensor_tensor(SS[:, lo:T], SQ[:, 0, lo:T] if m == 1 else SS[:, lo:T], SQ[:, m, lo:T], ALU.add)
                    if m < KT - 2:
                        chain.link(ins)
                ins.then_inc(sum_ready, 1)

            def sum_pairs(count, lo):
                for k in range(0, KT, 2):
                    pool.wait_ge(sq_ready, 8 * count + k + 2)
                    nc.gpsimd.tensor_tensor(SQ[:, k, lo:T], SQ[:, k, lo:T], SQ[:, k + 1, lo:T], ALU.add).then_inc(pair_summed, 1)

            def rest(pre, lo, h, l):
                for k in range(1, KT, 2):
                    pool.wait_ge(normed_hi, 8 * pre + k + 1)
                    nc.gpsimd.tensor_tensor(l(k), SQ[:, k, lo:T], h(k).bitcast(F32), ALU.subtract).then_inc(rest_pool, 1)

            nc.gpsimd.memset(ones_d[:, :], 1.0 / D).then_inc(consts_ready, 1)
            nc.gpsimd.memset(ones_h[:, :], 1.0 / 512).then_inc(consts_ready, 1)
            nc.gpsimd.memset(ones_1[:, :], 1.0).then_inc(consts_ready, 1)
            chain.link(nc.gpsimd.memset(ident[:, :], 0.0))
            chain.link(nc.gpsimd.memset(sel[:, :, :], 0.0))
            nc.gpsimd.affine_select(out=ident[:, :], in_=ident[:, :], compare_op=ALU.not_equal, fill=1.0, base=0,
                                    pattern=[[-1, P]], channel_multiplier=1).then_inc(consts_ready, 1)
            nc.gpsimd.affine_select(out=sel[:, :, :], in_=sel[:, :, :], compare_op=ALU.not_equal, fill=1.0, base=0,
                                    pattern=[[-1, LHEADS], [0, P]], channel_multiplier=1).then_inc(consts_ready, 1)
            pool.wait_ge(consts_ready, 7)
            nc.gpsimd.memset(AR[:, 2048:3072], 0.0).then_inc(rf_zero, 1)
            sum_pairs(0, META)
            rest(PRE_X, META, *raw_parts(META))
            pool.wait_ge(mem_sq, 1)
            for half in (4, 2, 1):
                ins = nc.gpsimd.tensor_tensor(KTm[:, 0:half, :], KTm[:, 0:half, :], KTm[:, half:2 * half, :], ALU.add)
                if half > 1:
                    chain.link(ins)
            ins.then_inc(mem_summed, 1)
            nc.gpsimd.memset(hc[:, :, :, :], 0.0).then_inc(hc_zero, 1)
            nc.gpsimd.memset(VX[:, :, :, :], 0.0).then_inc(vx_zero, 1)
            nc.gpsimd.memset(kcmp[:, :, :], 0.0).then_inc(kc_zero, 1)
            nc.gpsimd.memset(Sc[:, 0, :, CMP_FIRST:NCMP], MASKED).then_inc(sc_masked, 1)
            pool.wait_ge(params_loaded, 16)
            sw = col("sgu_w", 0, 512).rearrange("p (h t) -> p h t", h=4)
            nc.gpsimd.affine_select(out=sw, in_=sw, compare_op=ALU.is_ge, fill=0.0, base=0,
                                    pattern=[[0, 4], [1, P]], channel_multiplier=-1).then_inc(sgu_masked, 1)
            pool.wait_ge(cmp_in, 1)
            nc.gpsimd.memset(AR[:, 3584:4096], 0.0).then_inc(pc_zero, 1)
            pool.wait_ge(bias_copied, 1)
            pool.dma_start(bias_rows, vec[0:HEADS, :]).then_inc(bias_stored, 16)
            pool.wait_ge(bias_stored, 16)
            pool.dma_start(bias, bass.AP(tensor=bias_rows.tensor, offset=bias_rows.offset + S - 127,
                                         ap=[[1, P], [512, HEADS], [1, S]])).then_inc(bias_loaded, 16)
            pool.wait_ge(mem_lo, 1)
            nc.gpsimd.memset(pT[:, :, 0:META], 0.0).then_inc(pool_padded, 1)
            pool.wait_ge(pool_padded, 1)
            for t in (TILE["pool"], TILE["pool"] + 1):
                wait_evacuated(pool, t)
            chain.link(nc.gpsimd.tensor_tensor(wA[:, :, 1:T], pT[:, :, 1:T], pT[:, :, 0:T - 1], ALU.add))
            chain.link(nc.gpsimd.tensor_tensor(wB[:, :, 3:T], wA[:, :, 3:T], wA[:, :, 1:T - 2], ALU.add))
            inv = col("pool_inv", 0, 512).rearrange("p (a b) -> p a b", a=2)
            chain.link(nc.gpsimd.tensor_tensor(pd[0:64, 0, :], wA[0:64, 0, META:T], inv[0:64, 0, :], ALU.mult))
            chain.link(nc.gpsimd.tensor_tensor(pd[64:128, 0, :], wB[64:128, 0, META:T], inv[64:128, 0, :], ALU.mult))
            chain.link(nc.gpsimd.tensor_tensor(wA[:, 1, 7:T], wB[:, 1, 7:T], wB[:, 1, 3:T - 4], ALU.add))
            chain.link(nc.gpsimd.tensor_tensor(pd[0:64, 1, :], wA[0:64, 1, META:T], inv[0:64, 1, :], ALU.mult))
            chain.link(nc.gpsimd.tensor_tensor(wB[64:128, 1, 15:T], wA[64:128, 1, 15:T], wA[64:128, 1, 7:T - 8], ALU.add))
            chain.link(nc.gpsimd.tensor_tensor(pd[64:128, 1, :], wB[64:128, 1, META:T], inv[64:128, 1, :], ALU.mult))
            nc.gpsimd.tensor_tensor(pd, pd, pT[:, :, META:T], ALU.subtract).then_inc(pool_diff, 1)
            for update, name in enumerate(("w_out", "mo", "down")):
                if name == "down":
                    def ffn_pool(p, i, hidden, rest):
                        pool.wait_ge(f_gelu, p + 1 + 2 * i)
                        pool.wait_ge(u_tapped, 2 * p + 2 + 4 * i)
                        nc.gpsimd.tensor_tensor(Ft[:, p % 2, :], Gt[:, p % 2, :], Vt[:, p % 2, :], ALU.mult).then_inc(act_ready, 1)
                        pool.wait_ge(act_hi, ACT_FFN + p + 1 + 2 * i)
                        nc.gpsimd.tensor_tensor(rest, Ft[:, p % 2, :], hidden.bitcast(F32), ALU.subtract).then_inc(act_lo, 1)

                    with pool.Fori(0, 8) as i:
                        for p in (0, 1):
                            ffn_pool(p, i, a_hi(p + 2 * i), a_lo(p + 2 * i))
                    for p in range(16, FFN_TILES):
                        ffn_pool(p, 0, ffn_hi(p), ffn_lo(p))
                sum_squares(lambda m: wait_evacuated(pool, TILE[name] + m), META)
                wait_rstd(pool, (NORM_MIX, NORM_MEMOUT, NORM_FFN)[update])
                wait_y(pool, update)
                for k in (POOL_FROM, POOL_FROM + 1):
                    chain.link(nc.gpsimd.tensor_tensor(Y[:, k, META:T], Y[:, k, META:T], rstd[:, META:T], ALU.mult))
                    nc.gpsimd.tensor_tensor(XR[:, k, META:T], XR[:, k, META:T], Y[:, k, META:T], ALU.add).then_inc(x_updated_pool, 1)
                sum_pairs(update + 1, 0 if name == "down" else META)
            with pool.Fori(0, E_TILES) as i:
                pool.wait_ge(c_conv, i + 1)
                nc.gpsimd.tensor_tensor(Yc, Yc, rstd[:, :], ALU.mult).then_inc(c_scaled, 1)
            sum_squares(lambda m: pool.wait_ge(sq_ready, SQ_H1 + m + 1), 0)
            rest(PRE_H1, 0, l_in(AH, 0), l_in(AL, 0))
            def l_mask(h):
                pool.wait_ge(l_decay, 2 * h + 1)
                nc.gpsimd.affine_select(out=Dl[:, 0:S], in_=Dl[:, 0:S], compare_op=ALU.is_ge, fill=0.0, base=0,
                                        pattern=[[1, S]], channel_multiplier=-1).then_inc(l_masked, 1)
                nc.gpsimd.affine_select(out=Dl[:, S:S + P], in_=Dl[:, S:S + P], compare_op=ALU.is_ge, fill=0.0,
                                        base=0, pattern=[[1, P]], channel_multiplier=-1).then_inc(l_masked, 1)

            l_mask(0)
            for h in range(LHEADS):
                if h + 1 < LHEADS:
                    l_mask(h + 1)
                pool.wait_ge(l_sq, h + 1)
                nc.gpsimd.tensor_tensor(sqh[:, 0:2, :], sqh[:, 0:2, :], sqh[:, 2:4, :], ALU.add).then_inc(l_summed, 1)
            sum_squares(lambda m: pool.wait_ge(sq_ready, SQ_FINAL + m + 1), META)

        @block.scalar
        def _(act):
            chain = Chain(act, act_steps)

            def hi(n, i=0):
                act.wait_ge(weights_loaded[n % SLOTS], 16 * (n // SLOTS + 1) + 16 * i)
                if n >= SLOTS:
                    act.wait_ge(chunk_done, n - SLOTS + 1 + 4 * i)
                nc.scalar.activation(w_hi[:, n % SLOTS, :], raw[:, n % SLOTS, :], ACT.Copy).then_inc(hi_ready, 1)

            def ahead(n, i=0):
                if n + AHEAD < NCHUNKS:
                    hi(n + AHEAD, i)

            def load_root():
                nc.scalar.activation(small[:, 157:158], eps_col, ACT.Sqrt)

            def take_root(e, w, lo, dst=root, loaded=False):
                if not loaded:
                    load_root()
                act.wait_ge(stat_ready, e + 1)
                nc.scalar.activation(dst[:, lo:T], OB[1][:, 0:w], ACT.Sqrt, bias=eps_col).then_inc(root_ready, 1)

            def to_hi(pre, lo, dst, k):
                act.wait_ge(normed, 8 * pre + k + 1)
                nc.scalar.activation(dst(k), SQ[:, k, lo:T], ACT.Copy).then_inc(normed_hi, 1)

            def wait_x(update, k):
                if k < POOL_FROM:
                    act.wait_ge(x_updated, POOL_FROM // 2 * update + k // 2 + 1)
                else:
                    act.wait_ge(x_updated_pool, (KT - POOL_FROM) * update + k - POOL_FROM + 1)

            def raw_to_hi(lo, u, gain):
                dst = raw_parts(lo)[0]
                for k in range(KT):
                    wait_x(u, k)
                    nc.scalar.activation(dst(k), XR[:, k, lo:T], ACT.Copy, scale=col(gain, k)).then_inc(raw_hi, 1)

            def square_x(lo, update):
                for k in range(0, KT, 2):
                    wait_x(update, k + 1)
                    nc.scalar.activation(SQ[:, k:k + 2, lo:T], XR[:, k:k + 2, lo:T], ACT.Square).then_inc(sq_ready, 2)

            def to_y(t, m, gain, n):
                if m == KT // 2:
                    load_root()
                if m == KT - 1:
                    wait_chunk(act, n)
                    nc.scalar.activation(SQ[:, m, META:T], acc(t)[:, 0:S], ACT.Square).then_inc(last_sq, 1)
                    freed(nc.scalar.activation(Y[:, m, META:T], acc(t)[:, 0:S], ACT.Copy, scale=col(gain, m)), t)
                else:
                    wait_chunk(act, n)
                    nc.scalar.activation(Y[:, m, META:T], acc(t)[:, 0:S], ACT.Copy, scale=col(gain, m)).then_inc(y_ready, 1)
                    freed(nc.scalar.activation(SQ[:, m, META:T], acc(t)[:, 0:S], ACT.Square), t)

            eps_col = small[:, 158:159]
            act.wait_ge(consts_ready, 7)
            nc.scalar.activation(small[:, 156:157], eps_col, ACT.Square)
            for k in range(0, KT, 2):
                if k % 4 == 0:
                    act.wait_ge(x_loaded[k // 4], 16)
                nc.scalar.activation(SQ[:, k:k + 2, META:T], XR[:, k:k + 2, META:T], ACT.Square).then_inc(sq_ready, 2)
            hi(0)
            take_root(NORM_X, S, META)
            hi(1)
            hi(2)
            for k in range(KT):
                to_hi(PRE_X, META, raw_parts(META)[0], k)
            hi(3)
            act.wait_ge(bias_vec, 1)
            nc.scalar.activation(vec[0:HEADS, :], OB[0][0:HEADS, :], ACT.Copy).then_inc(bias_copied, 1)
            n, t = CHUNK["kc"], TILE["kc"]
            wait_chunk(act, n)
            for g in range(GROUPS):
                src = acc(t)[g * HD:(g + 1) * HD, 0:S]
                chain.note(nc.scalar.activation(KC2[0:HD, 0, g, :], src, ACT.Copy))
                last = nc.scalar.activation(KC2[HD:P, 0, g, 0:S - 1], src[:, 1:S], ACT.Copy)
                if g == 0:
                    chain.note(last)
            chain.wait()
            freed(last, t)
            ahead(CHUNK["vc"])
            act.wait_ge(mem_loaded, 16)
            nc.scalar.activation(KTm[:, :, :], mem_raw, ACT.Square).then_inc(mem_sq, 1)
            ahead(CHUNK["vsw"])
            ahead(CHUNK["vsw"] + 1)
            ahead(CHUNK["ks"])
            ahead(CHUNK["kw"])
            act.wait_ge(stat_ready, NORM_MEM + 1)
            nc.scalar.activation(root_m[:, 0:S], PTB[:, 0:S], ACT.Sqrt, bias=eps_col).then_inc(root_ready, 1)
            for c in range(4):
                ahead(CHUNK["cmp"] + c)

            for j in range(4):
                n, t = CHUNK["q"] + j, TILE["q"] + j
                ahead(n)
                wait_chunk(act, n)
                freed(nc.scalar.mul(qT[:, j, :], acc(t)[:, 0:S], HD ** -0.5), t)
                if j == 0:
                    act.wait_ge(cmp_hidden, 1)
                    nc.scalar.activation(hk, OB[1][:, 0:32], ACT.Gelu_apprx_tanh, bias=col("cmp_b1", 0)).then_inc(cmp_copied, 1)
                    act.wait_ge(hc_zero, 1)
                    for r in range(4):
                        nc.scalar.activation(hc[:, :, r, 0:NCMP], OB[0][:, 0:32].rearrange("p (g c) -> p g c", g=2)[:, :, 0:NCMP],
                                             ACT.Gelu_apprx_tanh, bias=col("cmp_b1", 1)).then_inc(cmp_copied, 1)
            n, t = CHUNK["gates"], TILE["gates"]
            nc.scalar.activation(small[:, 156:157], eps_col, ACT.Exp)
            ahead(n)
            wait_chunk(act, n)
            freed(nc.scalar.activation(gT[0:24, :], acc(t)[0:24, 0:S], ACT.Exp, scale=-1.0), t)

            def out_hi(j):
                act.wait_ge(outs, j + 1)
                nc.scalar.activation(a_hi(j), OB[j % 2][:, 0:S], ACT.Copy).then_inc(act_hi, 1)

            def fill_act(h):
                if h == 0:
                    t = TILE["sgu_v"]
                    wait_chunk(act, CHUNK["sgu_v"] + 1)
                    freed(nc.scalar.activation(vg[:, :, :], acc(t)[:, :].rearrange("p (a b) -> p a b", a=2), ACT.Copy), t)
                    act.wait_ge(cp_turned, 1)
                    nc.scalar.activation(PcT[:, :, :], OB[0][:, 0:512].rearrange("p (g t) -> p g t", g=2),
                                         ACT.Copy).then_inc(cp_copied, 1)
                if h == GELU_HEAD:
                    for j in range(2):
                        n, t = CHUNK["sgu_u"] + j, TILE["sgu_u"] + j
                        wait_chunk(act, n)
                        freed(nc.scalar.activation(uT[:, j, :], acc(t)[:, 0:S], ACT.Copy), t)
                    wait_evacuated(act, TILE["sgu_v"])
                    nc.scalar.activation(vg[:, :, :], vg[:, :, :], ACT.Gelu_apprx_tanh).then_inc(sgu_gelu, 1)
                if h == 2:
                    act.wait_ge(mem_lo, 1)
                    for j in range(2):
                        n, t = CHUNK["pool"] + j, TILE["pool"] + j
                        wait_chunk(act, n)
                        freed(nc.scalar.activation(pT[:, j, META:T], acc(t)[:, 0:S], ACT.Copy), t)
                    act.wait_ge(sgu_var, 1)
                    nc.scalar.activation(rs2, mv[:, :, 1], ACT.Sqrt, bias=eps_col).then_inc(sgu_root, 1)

            for h in range(HEADS):
                n = CHUNK["sgu_v"] + 2 * h
                if h < HEADS - 1 and h != GELU_HEAD + 1:
                    ahead(n)
                act.wait_ge(max_ready, h + 1)
                for b in range(4):
                    lo, w = (P * b, P) if b < 2 else (S * (b - 1), S)
                    last = nc.scalar.activation(Sx[:, lo:lo + w], Sx[:, lo:lo + w], ACT.Exp, bias=mx4[:, b:b + 1],
                                                accum_out=sm4[:, b:b + 1])
                    if b < 3:
                        chain.note(last)
                chain.wait()
                last.then_inc(exped, 1)
                if h == HEADS - 1:
                    wait_evacuated(act, TILE["sgu_u"])
                    wait_evacuated(act, TILE["sgu_u"] + 1)
                    nc.scalar.activation(uT[:, :, :], uT[:, :, :], ACT.Gelu_apprx_tanh).then_inc(sgu_gelu, 1)
                if h == 0:
                    act.wait_ge(cs_shifted, 1)
                    nc.scalar.activation(Sc[:, :, :, :], Sc[:, :, :, :], ACT.Exp).then_inc(cs_exp, 1)
                if h == GELU_HEAD + 1:
                    ahead(n)
                if h < HEADS - 1:
                    ahead(n + 1)
                if h >= 2 and h % 2 == 0:
                    out_hi(h // 2 - 1)
                if h == 0:
                    act.wait_ge(mem_normed, 1)
                    nc.scalar.activation(MH[:, :, :], mem_raw, ACT.Copy).then_inc(mem_hi, 1)
                act.wait_ge(turned, h + 1)
                nc.scalar.activation(PTx[:, :, :], PTB[:, :].rearrange("p (b t) -> p b t", b=2)[:, :, 0:384],
                                     ACT.Copy).then_inc(copied, 1)
                fill_act(h)
            for j in range(2):
                wait_evacuated(act, TILE["pool_mix"])
                wait_evacuated(act, TILE["pool_mix"] + 1)
                nc.scalar.activation(a_hi(4 + j), t512[:, j * S:(j + 1) * S], ACT.Copy).then_inc(mix_hi, 1)
            for j in range(2):
                act.wait_ge(sgu_gated, 1)
                nc.scalar.activation(a_hi(6 + j), vg[:, j, :], ACT.Copy).then_inc(mix_hi, 1)
            out_hi(3)
            for m in range(KT):
                n, t = CHUNK["w_out"] + m, TILE["w_out"] + m
                ahead(n)
                to_y(t, m, "g_mix_post", n)
            def v_act(name, q):
                n, t = CHUNK[name] + 2 * q, TILE[name] + q
                wait_chunk(act, n + 1)
                h = q + (2 if name == "mv2" else 0)
                freed(nc.scalar.activation(VM[:, 2 * h:2 * h + 2, :, :].rearrange("p r b c -> p b r c"),
                                           acc(t)[:, :].rearrange("p (b r c) -> p b r c", b=2, r=2), ACT.Copy), t)

            ahead(CHUNK["mv"])
            take_root(NORM_MIX, S, META, loaded=True)
            ahead(CHUNK["mv"] + 1)
            raw_to_hi(META, RAW_X1, "g_mem_pre")
            v_act("mv", 0)
            ahead(CHUNK["mv"] + 2)
            square_x(META, 0)
            v_act("mv", 1)
            ahead(CHUNK["mv"] + 3)
            take_root(NORM_X1, S, META)
            def m_exp(h):
                act.wait_ge(m_max, h + 1)
                if h >= 2:
                    act.wait_ge(m_turned, h - 1)
                for b in range(2):
                    last = nc.scalar.activation(Em[:, h % 2, b, :], SC[:, (h % 2) * 512 + b * S:(h % 2) * 512 + (b + 1) * S],
                                                ACT.Exp, bias=small[:, 16 + 2 * h + b:17 + 2 * h + b],
                                                accum_out=small[:, 24 + 2 * h + b:25 + 2 * h + b])
                    if b < 1:
                        chain.link(last)
                last.then_inc(m_exped, 1)

            def m_copy(h):
                act.wait_ge(m_turned, h + 1)
                if h >= 2:
                    act.wait_ge(m_outs, h - 1)
                nc.scalar.activation(PTm[:, h % 2, :, :], PTB[:, (h % 2) * 512:(h % 2) * 512 + 512].rearrange("p (m t) -> p m t", m=2),
                                     ACT.Copy).then_inc(m_copied, 1)

            def m_hi(h):
                act.wait_ge(m_outs, h + 1)
                nc.scalar.activation(AH[:, 2 * h * S:(2 * h + 2) * S], OB[h % 2][:, :], ACT.Copy).then_inc(act_hi, 1)

            for m in range(KT):
                ahead(CHUNK["mq"] + m)
                if m in (4, 5):
                    m_exp(m - 4)
                if m == 6:
                    m_copy(0)
            m_exp(2)
            m_hi(0)
            m_copy(1)
            ahead(CHUNK["mv2"])
            m_exp(3)
            v_act("mv2", 0)
            m_hi(1)
            ahead(CHUNK["mv2"] + 1)
            ahead(CHUNK["mv2"] + 2)
            m_copy(2)
            v_act("mv2", 1)
            ahead(CHUNK["mv2"] + 3)
            m_copy(3)
            m_hi(2)
            m_hi(3)
            for m in range(KT):
                n, t = CHUNK["mo"] + m, TILE["mo"] + m
                ahead(n)
                to_y(t, m, "g_mem_post", n)
            take_root(NORM_MEMOUT, S, META, loaded=True)
            raw_to_hi(META, RAW_X2, "g_ffn_pre")
            square_x(META, 1)
            take_root(NORM_X2, S, META)
            taps = col("ffn_conv", 0, 176).rearrange("p (a b) -> p a b", b=8)

            def ffn_act(p, i, hidden):
                for v in range(2):
                    n, t = CHUNK["up"] + 2 * p + v, TILE["up"] + 2 * p + v
                    ahead(n, i)
                    wait_evacuated(act, t, i)
                    nc.scalar.activation((Gt, Vt)[v][:, p % 2, :], Ut[:, v, :], ACT.Identity, bias=taps[:, span(p + 2 * i, 1), 4 * v + 3],
                                         scale=taps[:, span(p + 2 * i, 1), 4 * v + 2]).then_inc(f_init, 1)
                    if hidden is not None:
                        (ffn_gelu, ffn_hidden)[v](p - 1, i, hidden)

            def ffn_gelu(p, i, _):
                act.wait_ge(u_tapped, 2 * p + 1 + 4 * i)
                nc.scalar.activation(Gt[:, p % 2, :], Gt[:, p % 2, :], ACT.Gelu_apprx_tanh).then_inc(f_gelu, 1)

            def ffn_hidden(p, i, dst):
                act.wait_ge(act_ready, p + 1 + 2 * i)
                nc.scalar.activation(dst, Ft[:, p % 2, :], ACT.Copy).then_inc(act_hi, 1)

            ffn_act(0, 0, None)
            with act.Fori(0, 8) as i:
                for p in (1, 2):
                    ffn_act(p, i, a_hi(p - 1 + 2 * i))
            for p in range(17, FFN_TILES):
                ffn_act(p, 0, ffn_hi(p - 1))
            ffn_gelu(FFN_TILES - 1, 0, None)
            ffn_hidden(FFN_TILES - 1, 0, ffn_hi(FFN_TILES - 1))
            for m in range(KT):
                n, t = CHUNK["down"] + 3 * m, TILE["down"] + m
                for c in range(3):
                    ahead(n + c)
                to_y(t, m, "g_ffn_post", n + 2)
            take_root(NORM_FFN, S, META, loaded=True)
            act.wait_ge(meta_loaded, 16)
            raw_to_hi(0, RAW_H0, "g_conv")
            square_x(0, 2)
            take_root(NORM_H0, T, 0)
            def conv_act(i):
                n, t = CHUNK["conv_in"], TILE["conv_in"]
                for c in range(3):
                    ahead(n + c, i)
                wait_evacuated(act, t + 2, i)
                nc.scalar.activation(SZ, ZZ, ACT.Sigmoid).then_inc(c_sig, 1)
                ahead(n + 3, i)
                wait_evacuated(act, t + 3, i)
                nc.scalar.activation(a_hi(i, T), Fc, ACT.Copy).then_inc(act_hi, 1)

            with act.Fori(0, E_TILES) as i:
                conv_act(i)
            for m in range(KT):
                n, t = CHUNK["conv_out"] + 2 * m, TILE["conv_out"] + m
                ahead(n)
                ahead(n + 1)
                wait_evacuated(act, t)
                nc.scalar.activation(XH[:, m, :], XR[:, m, :], ACT.Copy, scale=col("g_mlstm", m)).then_inc(raw_hi, 1)
                nc.scalar.activation(SQ[:, m, :], XR[:, m, :], ACT.Square).then_inc(sq_ready, 1)
            take_root(NORM_H1, T, 0)
            n, t = CHUNK["lgates"], TILE["lgates"]
            ahead(n)
            for m in range(KT):
                ahead(CHUNK["lk"] + m)
                to_hi(PRE_H1, 0, l_in(AH, 0), m)
            for m in range(KT):
                ahead(CHUNK["lq"] + m)
                if m == 0:
                    wait_evacuated(act, TILE["lgates"])
                    nc.scalar.activation(gx[0:36, :], gx[0:36, :], ACT.Identity, bias=col("gate_b")[0:36]).then_inc(g_raw, 1)
                    act.wait_ge(g_raw, 1)
                    chain.link(nc.scalar.activation(ge[32:36, :], gx[32:36, :], ACT.Abs))
                    chain.link(nc.scalar.activation(ge[32:36, :], ge[32:36, :], ACT.Exp, scale=-1.0))
                    nc.scalar.activation(gl[32:36, :], ge[32:36, :], ACT.Ln, bias=ones_1[32:36, 0:1]).then_inc(g_ln, 1)

            def decay(h):
                act.wait_ge(l_rows, h + 1)
                if h == 0:
                    act.wait_ge(g_cols, 1)
                else:
                    act.wait_ge(l_probs, 3 * h)
                chain.note(nc.scalar.activation(Dl[:, 0:S], PTB[:, 0:S], ACT.Exp, bias=acol[:, 1, h:h + 1]))
                chain.note(nc.scalar.activation(Dl[:, S:S + P], PTB[:, P:S], ACT.Exp, bias=acol[:, 2, h:h + 1]))
                chain.wait()
                nc.scalar.activation(Dl[0:META, 384:640], PTB[0:META, 0:S], ACT.Exp,
                                     bias=acol[0:META, 0, h:h + 1]).then_inc(l_decay, 1)
                if h:
                    act.wait_ge(l_hn, h)
                nc.scalar.activation(em, PTB[:, S:2 * S], ACT.Exp).then_inc(l_decay, 1)

            for m in range(E_TILES):
                n, t = CHUNK["lv"] + m, TILE["lv"] + m
                ahead(n)
                wait_chunk(act, n)
                if m >= 2:
                    act.wait_ge(l_vturned, m - 1)
                freed(nc.scalar.activation(lvT[:, m % 2, :], acc(t)[:, 0:T], ACT.Copy), t)
                if m == 4:
                    decay(0)
            def l_hi(e):
                wait_evacuated(act, TILE["oz"] + 8 * (e // 4) + 4 + e % 4)
                nc.scalar.activation(l_out(AH, e), hn[:, e % 4, :], ACT.Copy).then_inc(act_hi, 1)

            for h in range(LHEADS):
                n0, t0 = CHUNK["oz"] + 8 * h, TILE["oz"] + 8 * h
                if h + 1 < LHEADS:
                    decay(h + 1)
                act.wait_ge(l_hn, h + 1)
                nc.scalar.activation(sqh[:, :, :], hn[:, :, :], ACT.Square).then_inc(l_sq, 1)
                for m in range(4):
                    ahead(n0 + m)
                    wait_chunk(act, n0 + m)
                    if h:
                        wait_evacuated(act, t0 - 4 + m)
                    freed(nc.scalar.activation(so[:, m, :], acc(t0 + m)[:, 0:S], ACT.Sigmoid), t0 + m)
                    if m == 1:
                        act.wait_ge(l_stat, h + 1)
                        nc.scalar.activation(lroot, PTB[:, 512:512 + S], ACT.Sqrt, bias=eps_col).then_inc(l_root, 1)
                for m in range(4):
                    n, t = n0 + 4 + m, t0 + 4 + m
                    ahead(n)
                    wait_chunk(act, n)
                    nc.scalar.activation(tz[:, m % 2, :], acc(t)[:, 0:S], ACT.Sigmoid).then_inc(z_sig, 1)
                    if m:
                        l_hi(4 * h + m - 1)
                l_hi(4 * h + 3)
            for m in range(KT):
                n, t = CHUNK["lout"] + 2 * m, TILE["lout"] + m
                ahead(n)
                ahead(n + 1)
                wait_evacuated(act, t)
                nc.scalar.activation(SQ[:, m, META:T], XR[:, m, META:T], ACT.Square).then_inc(sq_ready, 1)
            take_root(NORM_FINAL, S, META)

        @block.tensor
        def _(pe):
            def stat_x(e, count, w):
                for k in range(0, KT, 2):
                    pe.wait_ge(pair_summed, 4 * count + k // 2 + 1)
                    last = nc.tensor.matmul(OB[1][:, 0:w], ones_d[:, :], SQ[:, k, T - w:T], start=(k == 0), stop=(k == KT - 2))
                last.then_inc(stat_ready, 1)

            def stat_sum(e, count, last_ready, w):
                pe.wait_ge(sum_ready, count)
                nc.tensor.matmul(OB[1][:, 0:w], ones_d[:, :], SS[:, T - w:T], start=True, stop=False)
                last_ready()
                nc.tensor.matmul(OB[1][:, 0:w], ones_d[:, :], SQ[:, KT - 1, T - w:T], start=False, stop=True).then_inc(stat_ready, 1)

            def stat_y(e, count):
                stat_sum(e, count, lambda: pe.wait_ge(last_sq, count), S)

            def keep_warm(products):
                for _ in range(products):
                    nc.tensor.matmul(SC[:, 0:P], ones_d[:, :], ident[:, :], start=True, stop=True)

            def begin(n, t, first, i=0):
                pe.wait_ge(lo_ready, n + 1 + 4 * i)
                if first and t >= 2:
                    pe.wait_ge(evacuated[t % 2], t // 2 + 2 * i)

            def chunk(n, t, xh, xl, w, i=0, k0=0, nk=KT, total=KT, ready=None, order=None):
                begin(n, t, k0 == 0, i)
                s = n % SLOTS
                order = order or range(k0, k0 + nk)
                for k in order:
                    j = k - k0
                    if ready:
                        ready(k)
                    wh, wl = w_hi[:, s, j * P:(j + 1) * P], w_lo[:, s, j * P:(j + 1) * P]
                    nc.tensor.matmul(acc(t)[:, 0:w], wh, xh(k), start=(k0 == 0 and k == order[0]), stop=False)
                    nc.tensor.matmul(acc(t)[:, 0:w], wh, xl(k), start=False, stop=False)
                    last = nc.tensor.matmul(acc(t)[:, 0:w], wl, xh(k), start=False, stop=(k0 + nk == total and k == order[-1]))
                last.then_inc(chunk_done, 1)

            def slots(part, n, cols):
                a, b = sorted((n % SLOTS, (n + 1) % SLOTS))
                return part[:, a:b + 1:b - a, cols]

            def pair_tokens(n, t, xh, xl, between=None):
                begin(n + 1, t, True)
                for b in range(2):
                    o = acc(t)[:, b * S:(b + 1) * S].rearrange("p (r c) -> p r c", r=2)
                    for k in range(KT):
                        cols = slice(k * P, (k + 1) * P)
                        wh, wl = slots(w_hi, n, cols), slots(w_lo, n, cols)
                        nc.tensor.matmul(o, xh(k)[:, b * P:(b + 1) * P], wh, start=(k == 0), stop=False)
                        nc.tensor.matmul(o, xl(k)[:, b * P:(b + 1) * P], wh, start=False, stop=False)
                        last = nc.tensor.matmul(o, xh(k)[:, b * P:(b + 1) * P], wl, start=False, stop=(k == KT - 1))
                    if b == 0 and between:
                        between()
                last.then_inc(chunk_done, 2)

            def xh(k):
                return XH[:, k, META:T]

            def xl(k):
                return XL[:, k, META:T]

            def xha(k):
                return XH[:, k, :]

            def xla(k):
                return XL[:, k, :]

            def pre_ready(pre):
                return lambda k: pe.wait_ge((normed_lo, rest_pool)[k % 2], 4 * pre + k // 2 + 1)

            pe.wait_ge(consts_ready, 7)
            keep_warm(WARM_START)
            stat_x(NORM_X, 0, S)
            pe.wait_ge(rel_loaded, 32)
            nc.tensor.matmul(OB[0][0:HEADS, :], rb[:, :], hot[0:33, :], start=True, stop=True).then_inc(bias_vec, 1)
            keep_warm(WARM_X)
            chunk(CHUNK["kc"], TILE["kc"], xh, xl, S, ready=pre_ready(PRE_X))
            chunk(CHUNK["vc"], TILE["vc"], xh, xl, S)
            pair_tokens(CHUNK["vsw"], TILE["vsw"], xh, xl)
            chunk(CHUNK["ks"], TILE["ks"], xh, xl, S)
            chunk(CHUNK["kw"], TILE["kw"], xh, xl, S)
            pe.wait_ge(mem_summed, 1)
            nc.tensor.matmul(PTB[:, 0:S], ones_d[:, :], KTm[:, 0, :], start=True, stop=True).then_inc(stat_ready, 1)
            pe.wait_ge(cmp_in, 2)
            for c in range(2):
                n, t = CHUNK["cmp"] + 2 * c, TILE["cmp"]
                begin(n + 1, t, c == 0)
                o = acc(t)[0:64, 0:S].rearrange("p (r c) -> p r c", r=2)
                for k in range(KT):
                    j, cols = KT * c + k, slice(k * P, (k + 1) * P)
                    rows = slice(2048 + 64 * j, 2048 + 64 * (j + 1))
                    nc.tensor.matmul(o, AH[:, rows], slots(w_hi, n, cols), start=(j == 0), stop=False)
                    nc.tensor.matmul(o, AL[:, rows], slots(w_hi, n, cols), start=False, stop=False)
                    last = nc.tensor.matmul(o, AH[:, rows], slots(w_lo, n, cols), start=False, stop=(j == 15))
                last.then_inc(chunk_done, 2)
            chunk(CHUNK["q"], TILE["q"], xh, xl, S)
            wait_evacuated(pe, TILE["cmp"])
            pe.wait_ge(root_ready, 1)
            pe.wait_ge(bias_copied, 1)
            nc.tensor.transpose(OB[1][:, 0:32], ch[0:32, 0:P], ident[0:32, 0:32])
            nc.tensor.transpose(OB[0][:, 0:32], ch[32:64, P:S], ident[32:64, 32:64]).then_inc(cmp_hidden, 1)
            for j in range(1, 3):
                chunk(CHUNK["q"] + j, TILE["q"] + j, xh, xl, S)
            w2 = col("cmp_w2", 0, 128)
            pe.wait_ge(cmp_copied, 5)
            for g in range(GROUPS):
                nc.tensor.matmul(OB[0][g * HD:(g + 1) * HD, 0:NCMP], w2[:, 0:HD], hk[:, g * 16:g * 16 + NCMP],
                                 start=True, stop=True)
            for g in range(GROUPS):
                last = nc.tensor.matmul(OB[0][:, 64 + g * HD:64 + (g + 1) * HD], hc[:, g, :, :].rearrange("p a b -> p (a b)"),
                                        w2[:, HD:2 * HD], start=True, stop=True)
            last.then_inc(cmp_out, 1)
            chunk(CHUNK["q"] + 3, TILE["q"] + 3, xh, xl, S)
            chunk(CHUNK["gates"], TILE["gates"], xh, xl, S)
            pe.wait_ge(cmp_kv, 2)
            pe.wait_ge(root_ready, 2)
            for j in range(4):
                wait_evacuated(pe, TILE["q"] + j)
                for b in range(2):
                    o = (b * 4 + j) * 32
                    last = nc.tensor.matmul(PTB[:, o:o + 32], qT[:, j, b * P:(b + 1) * P], kcmp[:, :, :].rearrange("p g c -> p (g c)"),
                                            start=True, stop=True)
            last.then_inc(cs_ready, 1)
            wait_evacuated(pe, TILE["gates"])
            for b in range(2):
                last = nc.tensor.transpose(OB[1][:, b * 24:(b + 1) * 24], gT[0:24, b * P:(b + 1) * P], ident[0:24, 0:24])
            last.then_inc(gate_turned, 1)

            def sgu_products():
                pe.wait_ge(sgu_normed, 1)
                pe.wait_ge(sgu_masked, 1)
                t = TILE["sgu_mix"]
                pe.wait_ge(evacuated[t % 2], t // 2)
                sw = col("sgu_w", 0, 512).rearrange("p (h t) -> p h t", h=4)
                for h in range(4):
                    for b in range(2):
                        o = acc(t)[(h % 2) * HD:(h % 2 + 1) * HD, (h // 2) * S + b * P:(h // 2) * S + (b + 1) * P]
                        last = nc.tensor.matmul(o, vn[:, b, h * HD:(h + 1) * HD], sw[:, h, :], start=True, stop=True)
                last.then_inc(sgu_mixed, 1)

            def pool_products():
                pe.wait_ge(pool_diff, 1)
                pw = col("pool_w", 0, 128).rearrange("p (a b) -> p a b", a=2)
                for r in range(2):
                    t = TILE["pool_mix"] + r
                    pe.wait_ge(evacuated[t % 2], t // 2)
                    for j in range(2):
                        last = nc.tensor.matmul(acc(t)[r * HD:(r + 1) * HD, j * S:(j + 1) * S], pw[r * HD:(r + 1) * HD, j, :],
                                                pd[r * HD:(r + 1) * HD, j, :], start=True, stop=True)
                last.then_inc(pool_mixed, 1)

            def qk(h):
                j, g = h // 2, h % 2
                if h == 0:
                    wait_evacuated(pe, TILE["kw"])
                    wait_evacuated(pe, TILE["q"] + 3)
                else:
                    pe.wait_ge(max_ready, h)
                q = qT[g * HD:(g + 1) * HD, j, :]
                for r in range(2):
                    k = kT[g * HD:(g + 1) * HD, r, :]
                    nc.tensor.matmul(SC[:, r * P:(r + 1) * P], q[:, 0:P], k[:, 0:P], start=True, stop=True)
                for r in range(2):
                    k = kT[g * HD:(g + 1) * HD, r, :]
                    last = nc.tensor.matmul(SC[:, 512 + r * S:512 + (r + 1) * S], q[:, P:S], k, start=True, stop=True)
                last.then_inc(scores, 1)

            def turn(h):
                pe.wait_ge(probs, h + 1)
                if h == 0:
                    pe.wait_ge(cs_shifted, 1)
                else:
                    pe.wait_ge(copied, h)
                for r in range(2):
                    o = r * 512
                    nc.tensor.transpose(PTB[:, o:o + P], Sx[:, r * P:(r + 1) * P], ident[:, :])
                    nc.tensor.transpose(PTB[:, o + P:o + S], Sx[:, S + r * S:S + r * S + P], ident[:, :])
                    last = nc.tensor.transpose(PTB[:, o + S:o + S + P], Sx[:, S + r * S + P:S + (r + 1) * S], ident[:, :])
                last.then_inc(turned, 1)

            def pv(h):
                j, g = h // 2, h % 2
                pe.wait_ge(copied, h + 1)
                if h == 0:
                    pe.wait_ge(cp_copied, 1)
                if g == 0 and j >= 2:
                    pe.wait_ge(act_lo, j - 1)
                o = OB[j % 2][g * HD:(g + 1) * HD, 0:S]
                for r in range(2):
                    nc.tensor.matmul(o, Vtok[:, r, 0, g * HD:(g + 1) * HD], PTx[:, r, 0:S], start=(r == 0), stop=False)
                    nc.tensor.matmul(o[:, P:S], Vtok[:, r, 1, g * HD:(g + 1) * HD], PTx[:, r, S:384], start=False, stop=False)
                last = nc.tensor.matmul(o, VX[:, g, j, :], PcT[:, g, :], start=False, stop=True)
                if g:
                    last.then_inc(outs, 1)

            def mem_h(k):
                return MH[:, k, :]

            def mem_l(k):
                return ML[:, k, :]

            for h in range(HEADS):
                qk(h)
                if h == 0:
                    pair_tokens(CHUNK["sgu_v"], TILE["sgu_v"], xh, xl)
                elif h < HEADS - 1:
                    name, c = (("sgu_u", 0), ("pool", 0), ("mk", 0), ("mk", 2), ("mk", 4), ("mk", 6))[h - 1]
                    x = (mem_h, mem_l) if name == "mk" else (xh, xl)
                    if h == 1:
                        pe.wait_ge(cp_ready, 1)
                        pe.wait_ge(cmp_kv, 2)
                        for g in range(GROUPS):
                            for b in range(2):
                                last = nc.tensor.transpose(OB[0][:, g * S + b * P:g * S + (b + 1) * P],
                                                           Pc[:, b, g, :, :].rearrange("p a b -> p (a b)"), ident[:, :])
                        last.then_inc(cp_turned, 1)
                    if h == 3:
                        pe.wait_ge(mem_lo, 1)
                    chunk(CHUNK[name] + c, TILE[name] + c, *x, S)
                    pv(h - 1)
                    chunk(CHUNK[name] + c + 1, TILE[name] + c + 1, *x, S)
                else:
                    sgu_products()
                    pv(h - 1)
                turn(h)
            pool_products()
            pv(HEADS - 1)
            def mix_ready(k):
                if k < 4:
                    pe.wait_ge(act_lo, k + 1)
                else:
                    pe.wait_ge(mix_lo, k - 3)

            for m in range(KT):
                chunk(CHUNK["w_out"] + m, TILE["w_out"] + m, a_hi, a_lo, S, ready=mix_ready if m == 0 else None,
                      order=(0, 1, 2, 4, 5, 6, 7, 3) if m == 0 else None)
            stat_y(NORM_MIX, 1)
            for q in range(2):
                pair_tokens(CHUNK["mv"] + 2 * q, TILE["mv"] + q, mem_h, mem_l)

            def raw_ready(u):
                return lambda k: pe.wait_ge(raw_lo, 8 * u + k + 1)

            def m_qk(h):
                for j in (2 * h, 2 * h + 1):
                    wait_evacuated(pe, TILE["mq"] + j)
                if h >= 2:
                    pe.wait_ge(m_exped, h - 1)
                for b in range(2):
                    for j in range(2):
                        last = nc.tensor.matmul(SC[:, (h % 2) * 512 + b * S:(h % 2) * 512 + (b + 1) * S],
                                                qM[:, 2 * h + j, b * P:(b + 1) * P], KTm[:, 2 * h + j, :],
                                                start=(j == 0), stop=(j == 1))
                last.then_inc(m_scores, 1)

            def m_turn(h):
                pe.wait_ge(m_probs, h + 1)
                if h >= 2:
                    pe.wait_ge(m_copied, h - 1)
                for m in range(2):
                    for b in range(2):
                        last = nc.tensor.transpose(PTB[:, (h % 2) * 512 + m * S + b * P:(h % 2) * 512 + m * S + (b + 1) * P],
                                                   Em[:, h % 2, b, m * P:(m + 1) * P], ident[:, :])
                last.then_inc(m_turned, 1)

            def m_pv(h):
                pe.wait_ge(m_copied, h + 1)
                t = TILE[("mv", "mv2")[h // 2]] + h % 2
                wait_evacuated(pe, t)
                if h >= 2:
                    pe.wait_ge(act_lo, ACT_MEM + h - 1)
                for v in range(2):
                    for m in range(2):
                        last = nc.tensor.matmul(OB[h % 2][:, v * S:(v + 1) * S], VM[:, 2 * h + v, m, :], PTm[:, h % 2, m, :],
                                                start=(m == 0), stop=(m == 1))
                last.then_inc(m_outs, 1)

            for m in range(KT):
                chunk(CHUNK["mq"] + m, TILE["mq"] + m, xh, xl, S, ready=raw_ready(RAW_X1) if m == 0 else None)
                if m == 0:
                    stat_x(NORM_X1, 1, S)
                if m == 2:
                    m_qk(0)
                if m == 4:
                    m_qk(1)
                if m == 5:
                    m_turn(0)
                if m == 6:
                    m_qk(2)
                    m_pv(0)
                if m == 7:
                    m_turn(1)
            m_qk(3)
            pair_tokens(CHUNK["mv2"], TILE["mv2"], mem_h, mem_l)
            m_pv(1)
            m_turn(2)
            pair_tokens(CHUNK["mv2"] + 2, TILE["mv2"] + 1, mem_h, mem_l)
            m_turn(3)
            m_pv(2)
            m_pv(3)
            for m in range(KT):
                chunk(CHUNK["mo"] + m, TILE["mo"] + m, a_hi, a_lo, S,
                      ready=(lambda k: pe.wait_ge(act_lo, ACT_MEM + k // 2 + 1)) if m == 0 else None)
            stat_y(NORM_MEMOUT, 2)
            keep_warm(WARM)
            def ffn_pe(i, first=False):
                for r in range(4):
                    chunk(CHUNK["up"] + r, TILE["up"] + r, xh, xl, S, i=i, ready=raw_ready(RAW_X2) if first and r == 0 else None)
                    if first and r == 0:
                        stat_x(NORM_X2, 2, S)

            ffn_pe(0, True)
            with pe.Fori(1, FFN_TILES // 2) as i:
                ffn_pe(i)
            for m in range(KT):
                for c in range(3):
                    chunk(CHUNK["down"] + 3 * m + c, TILE["down"] + m, ffn_hi, ffn_lo, S, k0=8 * c,
                          nk=min(8, FFN_TILES - 8 * c), total=FFN_TILES,
                          ready=(lambda k: pe.wait_ge(act_lo, ACT_FFN + k + 1)) if m == 0 else None)
            stat_y(NORM_FFN, 3)
            keep_warm(WARM)
            def conv_pe(i, first=False):
                for r in range(4):
                    chunk(CHUNK["conv_in"] + r, TILE["conv_in"] + r, xha, xla, T, i=i, ready=raw_ready(RAW_H0) if first and r == 0 else None)
                    if first and r == 0:
                        stat_x(NORM_H0, 3, T)

            conv_pe(0, True)
            with pe.Fori(1, E_TILES) as i:
                conv_pe(i)
            for m in range(KT):
                for c in range(2):
                    chunk(CHUNK["conv_out"] + 2 * m + c, TILE["conv_out"] + m, lambda k: a_hi(k, T), lambda k: a_lo(k, T), T,
                          k0=8 * c, total=E_TILES, ready=(lambda k: pe.wait_ge(act_lo, ACT_CONV + k + 1)) if m == 0 else None)
            chunk(CHUNK["lgates"], TILE["lgates"], xha, xla, T, ready=raw_ready(RAW_H1))
            stat_sum(NORM_H1, 4, lambda: pe.wait_ge(sq_ready, SQ_H1 + KT), T)
            for m in range(KT):
                chunk(CHUNK["lk"] + m, TILE["lk"] + m, xha, xla, T)
            for m in range(KT):
                chunk(CHUNK["lq"] + m, TILE["lq"] + m, l_in(AH, META), l_in(AL, META), S, ready=pre_ready(PRE_H1) if m == 0 else None)
                if m == 5:
                    pe.wait_ge(g_rows, 3)
                    for s, (lo, w) in enumerate(((0, META), (META, P), (META + P, P))):
                        last = nc.tensor.transpose(OB[0][0:w, 4 * s:4 * s + 4], gA[0:LHEADS, lo:lo + w], ident[0:LHEADS, 0:LHEADS])
                    last.then_inc(g_turned, 1)

            def l_qk(h):
                if h == 0:
                    wait_evacuated(pe, TILE["lk"] + 7)
                    wait_evacuated(pe, TILE["lq"] + 7)
                else:
                    pe.wait_ge(l_probs, 3 * h)
                for j in range(2):
                    nc.tensor.matmul(SC[:, 0:S], lk[:, 2 * h + j, META:META + P], lq[:, 2 * h + j, :],
                                     start=(j == 0), stop=(j == 1))
                for j in range(2):
                    nc.tensor.matmul(SC[:, S:S + P], lk[:, 2 * h + j, META + P:T], lq[:, 2 * h + j, P:S],
                                     start=(j == 0), stop=(j == 1))
                for j in range(2):
                    last = nc.tensor.matmul(SC[0:META, 512:512 + S], lk[:, 2 * h + j, 0:META], lq[:, 2 * h + j, :],
                                            start=(j == 0), stop=(j == 1))
                last.then_inc(l_scores, 1)

            def l_bcast(h):
                if h:
                    pe.wait_ge(l_decay, 2 * h)
                nc.tensor.matmul(PTB[:, 0:S], sel[:, h, :], negM[:, META:T], start=True, stop=True)
                nc.tensor.matmul(PTB[:, S:2 * S], sel[:, h, :], negFM[:, META:T], start=True, stop=True).then_inc(l_rows, 1)

            def l_pv(h):
                pe.wait_ge(l_probs, 3 * h + 3)
                if h:
                    pe.wait_ge(l_root, h)
                parts = ((0, P, Pl[:, 0:S], 0), (1, P, Pl[:, S:S + P], P), (2, META, Pl[0:META, 384:640], 0))
                for s, w, p, lo in parts:
                    nc.tensor.matmul(PTB[:, 512 + lo:512 + S], ones_1[0:w, :], p, start=(s == 0), stop=(s == 2))
                for v in range(4):
                    o = OB[v // 2][:, (v % 2) * S:(v % 2 + 1) * S]
                    for s, w, p, lo in parts:
                        c = 512 * h + v * P
                        last = nc.tensor.matmul(o[:, lo:S], lv[0:w, s, c:c + P], p, start=(s == 0), stop=(s == 2))
                last.then_inc(l_num, 1)

            def v_turn(m):
                wait_evacuated(pe, TILE["lv"] + m)
                if m >= 2:
                    pe.wait_ge(l_vcopied, m - 1)
                if m == 0:
                    pe.wait_ge(g_cols, 1)
                o = OB[m % 2]
                nc.tensor.transpose(o[:, 0:P], lvT[:, m % 2, META:META + P], ident[:, :])
                nc.tensor.transpose(o[:, P:2 * P], lvT[:, m % 2, META + P:T], ident[:, :])
                nc.tensor.transpose(o[0:META, 2 * P:3 * P], lvT[:, m % 2, 0:META], ident[:, :]).then_inc(l_vturned, 1)

            for m in range(E_TILES):
                chunk(CHUNK["lv"] + m, TILE["lv"] + m, l_in(AH, 0), l_in(AL, 0), T)
                if m >= 1:
                    v_turn(m - 1)
                if m == 2:
                    pe.wait_ge(g_rows, 3)
                    l_bcast(0)
                if m == 4:
                    l_qk(0)
            v_turn(E_TILES - 1)
            pe.wait_ge(l_vcopied, E_TILES)
            for h in range(LHEADS):
                l_pv(h)
                if h + 1 < LHEADS:
                    l_bcast(h + 1)
                    l_qk(h + 1)
                n, t = CHUNK["oz"] + 8 * h, TILE["oz"] + 8 * h
                for m in range(2):
                    chunk(n + m, t + m, l_in(AH, META), l_in(AL, META), S)
                pe.wait_ge(l_summed, h + 1)
                for v in range(2):
                    last = nc.tensor.matmul(PTB[:, 512:512 + S], ones_h[:, :], sqh[:, v, :], start=(v == 0), stop=(v == 1))
                last.then_inc(l_stat, 1)
                for m in range(2, 8):
                    chunk(n + m, t + m, l_in(AH, META), l_in(AL, META), S)
            for m in range(KT):
                for c in range(2):
                    chunk(CHUNK["lout"] + 2 * m + c, TILE["lout"] + m, lambda k: l_out(AH, k), lambda k: l_out(AL, k), S, k0=8 * c, total=E_TILES,
                          ready=(lambda k: pe.wait_ge(act_lo, ACT_LSTM + k + 1)) if m == 0 else None)
            stat_sum(NORM_FINAL, 5, lambda: pe.wait_ge(sq_ready, SQ_FINAL + KT), S)

        @block.vector
        def _(dve):
            chain = Chain(dve, vec_steps)
            V = nc.vector

            def lo(n, i=0):
                dve.wait_ge(hi_ready, n + 1 + 4 * i)
                s = n % SLOTS
                V.tensor_tensor(w_lo[:, s, :], raw[:, s, :], w_hi[:, s, :].bitcast(F32), ALU.subtract).then_inc(lo_ready, 1)

            def ahead(n, i=0):
                if n + AHEAD < NCHUNKS:
                    lo(n + AHEAD, i)

            def reciprocal_root(e, a):
                dve.wait_ge(root_ready, e + 1)
                V.reciprocal(rstd[:, a:T], root[:, a:T]).then_inc(rstd_ready, 1)
                wait_rstd(dve, e)

            def apply_norm(pre, gain, a, h, l, k):
                if k < KT:
                    V.scalar_tensor_tensor(out=SQ[:, k, a:T], in0=XR[:, k, a:T], scalar=col(gain, k), in1=rstd[:, a:T],
                                           op0=ALU.mult, op1=ALU.mult).then_inc(normed, 1)
                k -= 2
                if k >= 0 and k % 2 == 0:
                    dve.wait_ge(normed_hi, 8 * pre + k + 1)
                    V.tensor_tensor(l(k), SQ[:, k, a:T], h(k).bitcast(F32), ALU.subtract).then_inc(normed_lo, 1)

            def raw_rest(u, gain, a, k):
                dve.wait_ge(raw_hi, 8 * u + k + 1)
                V.scalar_tensor_tensor(out=XL[:, k, a:T], in0=XR[:, k, a:T], scalar=col(gain, k),
                                       in1=XH[:, k, a:T].bitcast(F32), op0=ALU.mult, op1=ALU.subtract).then_inc(raw_lo, 1)

            def post_norm(e, update, gain, a, between=None):
                reciprocal_root(e, META)
                wait_y(dve, update)
                scaled = chain.count
                for k in range(0, POOL_FROM, 2):
                    chain.note(V.tensor_tensor(Y[:, k:k + 2, META:T], Y[:, k:k + 2, META:T],
                                               rstd[:, META:T].unsqueeze(1).to_broadcast([P, 2, S]), ALU.mult))
                    if k:
                        add(k - 2, update, scaled)
                add(POOL_FROM - 2, update, scaled)
                if between:
                    between()
                for k in range(KT):
                    raw_rest(update, gain, a, k)

            def add(k, update, scaled):
                dve.wait_ge(vec_steps, scaled + k // 2 + 1)
                V.tensor_tensor(XR[:, k:k + 2, META:T], XR[:, k:k + 2, META:T], Y[:, k:k + 2, META:T], ALU.add).then_inc(x_updated, 1)

            V.memset(rb[32:33, :], MASKED).then_inc(consts_ready, 1)
            V.memset(small[:, 158:159], EPS).then_inc(consts_ready, 1)
            lo(0)
            dve.wait_ge(gains_loaded, 16)
            reciprocal_root(NORM_X, META)
            for k in range(KT + 1):
                apply_norm(PRE_X, "g_mix_pre", META, *raw_parts(META), k)
            lo(1)
            lo(2)
            ahead(CHUNK["kc"])
            n, t = CHUNK["vc"], TILE["vc"]
            wait_chunk(dve, n)
            for g in range(GROUPS):
                src = acc(t)[g * HD:(g + 1) * HD, 0:S]
                chain.note(V.tensor_copy(KC2[0:HD, 1, g, :], src))
                last = V.tensor_copy(KC2[HD:P, 1, g, 0:S - 1], src[:, 1:S])
                if g == 0:
                    chain.note(last)
            freed(last, t)
            ahead(n)
            dve.wait_ge(rf_zero, 1)
            dve.wait_ge(params_loaded, 16)
            wait_evacuated(dve, TILE["kc"])
            wait_evacuated(dve, TILE["vc"])
            chain.wait()
            pos = col("cmp_pos", 0, 32).rearrange("p (a b) -> p a b", a=2)
            for v in range(2):
                for g in range(GROUPS):
                    src = KC2[:, v, g, :].rearrange("p (c l) -> p l c", l=CSTRIDE)
                    for half in range(2):
                        ks = slice(8 * half, 8 * half + 8)
                        chain.note(V.tensor_tensor(RF[:, ks, v, g, 0:NCMP], src[:, 0:CSTRIDE:2, half:half + NCMP],
                                                   pos[:, v, ks].unsqueeze(2).to_broadcast([P, 8, NCMP]), ALU.add))
            chain.wait()
            rf = RF[:, :, :, :, :].rearrange("p a b c d -> p (a b c d)")
            V.tensor_copy(AH[:, 2048:3072], rf).then_inc(cmp_in, 1)
            dve.wait_ge(cmp_in, 1)
            V.tensor_tensor(AL[:, 2048:3072], rf, AH[:, 2048:3072].bitcast(F32), ALU.subtract).then_inc(cmp_in, 1)
            n, t = CHUNK["vsw"], TILE["vsw"]
            ahead(n)
            wait_chunk(dve, n + 1)
            freed(V.tensor_copy(Vtok[:, :, :, :].rearrange("p r b c -> p b r c"),
                                acc(t)[:, :].rearrange("p (b r c) -> p b r c", b=2, r=2)), t)
            ahead(n + 1)
            for j, name in enumerate(("ks", "kw")):
                n, t = CHUNK[name], TILE[name]
                wait_chunk(dve, n)
                freed(V.tensor_copy(kT[:, j, :], acc(t)[:, 0:S]), t)
                ahead(n)
            n, t = CHUNK["cmp"], TILE["cmp"]
            ahead(n)
            ahead(n + 1)
            ahead(n + 2)
            wait_chunk(dve, n + 3)
            freed(V.tensor_copy(ch[0:64, :], acc(t)[0:64, 0:S]), t)
            ahead(n + 3)
            dve.wait_ge(root_ready, 2)
            chain.link(V.reciprocal(rstd_m[:, 0:S], root_m[:, 0:S]))
            for j in range(2):
                ahead(CHUNK["q"] + j)
            dve.wait_ge(cmp_out, 1)
            dve.wait_ge(kc_zero, 1)
            for g in range(GROUPS):
                rows = slice(g * HD, (g + 1) * HD)
                chain.note(V.tensor_scalar(kcmp[rows, g, 0:NCMP], OB[0][rows, 0:NCMP], col("cmp_b2k")[rows], None, ALU.add))
            for g in range(GROUPS):
                chain.note(V.tensor_tensor(vcmp[:, g, :], OB[0][:, 64 + g * HD:64 + (g + 1) * HD], col("cmp_b2v", 0, 64), ALU.add))
            chain.wait()
            dve.wait_ge(vx_zero, 1)
            for j in range(4):
                last = V.tensor_copy(VX[32 * j:32 * j + 32, :, j, :], vcmp[32 * j:32 * j + 32, :, :])
                if j < 3:
                    chain.note(last)
            chain.wait()
            last.then_inc(cmp_kv, 2)
            ahead(CHUNK["q"] + 2)
            ahead(CHUNK["q"] + 3)
            for k in range(KT):
                last = V.scalar_tensor_tensor(out=mem_raw[:, k, :], in0=mem_raw[:, k, :], scalar=col("g_mem_kv", k),
                                              in1=rstd_m[:, 0:S], op0=ALU.mult, op1=ALU.mult)
                if k < KT - 1:
                    chain.note(last)
            chain.wait()
            last.then_inc(mem_normed, 1)
            ahead(CHUNK["gates"])
            dve.wait_ge(gate_turned, 1)
            chain.link(V.tensor_scalar(gtok[:, :, :], OB[1][:, 0:48].rearrange("p (a b) -> p a b", a=2), 1.0, None, ALU.add))
            chain.link(V.reciprocal(gtok[:, :, :], gtok[:, :, :]))
            sc = Sc[:, :, :, :].rearrange("p b h c -> p (b h) c")

            def compressed_scores():
                dve.wait_ge(cs_ready, 1)
                dve.wait_ge(bias_loaded, 16)
                dve.wait_ge(sc_masked, 1)
                for b in range(2):
                    blocks = CMP_FIRST + b * (P // CSTRIDE)
                    for g in range(GROUPS):
                        chain.note(V.tensor_tensor(Sc[:, b, 4 * g:4 * g + 4, 0:blocks],
                                                   PTB[:, b * P:(b + 1) * P].rearrange("p (j g c) -> p j g c", j=4, g=2)[:, :, g, 0:blocks],
                                                   bias[:, g:HEADS:2, CSTRIDE * (blocks - 1)::-CSTRIDE], ALU.add))
                chain.wait()
                chain.link(V.tensor_reduce(m16, sc, AX.X, ALU.max))
                chain.link(V.tensor_scalar(m16, m16, MASKED * 1e-10, None, ALU.max))
                V.tensor_tensor(sc, sc, m16.unsqueeze(2).to_broadcast([P, 16, NCMP]), ALU.subtract).then_inc(cs_shifted, 1)

            def compressed_probs():
                dve.wait_ge(cs_exp, 1)
                chain.link(V.tensor_reduce(s16, sc, AX.X, ALU.add))
                chain.link(V.tensor_scalar(s16, s16, 1.0, None, ALU.max))
                chain.link(V.reciprocal(s16, s16))
                gate = gtok[:, :, :].rearrange("p b (h r) -> p b h r", r=3)
                chain.link(V.tensor_tensor(s16.rearrange("p (b h) -> p b h", b=2), s16.rearrange("p (b h) -> p b h", b=2),
                                           gate[:, :, :, 0], ALU.mult))
                dve.wait_ge(pc_zero, 1)
                for b in range(2):
                    last = V.tensor_tensor(Pc[:, b, :, :, 0:NCMP].rearrange("p g j c -> p (g j) c"), Sc[:, b, :, :],
                                           s16[:, 8 * b:8 * b + 8].unsqueeze(2).to_broadcast([P, 8, NCMP]), ALU.mult)
                    if b == 0:
                        chain.link(last)
                last.then_inc(cp_ready, 1)

            def out_lo(j):
                dve.wait_ge(act_hi, j + 1)
                V.tensor_tensor(a_lo(j), OB[j % 2][:, 0:S], a_hi(j).bitcast(F32), ALU.subtract).then_inc(act_lo, 1)

            sbias = col("sgu_bias", 0, 256).rearrange("p (a b) -> p a b", a=2)

            def fill_dve(h):
                if h == 1:
                    dve.wait_ge(sgu_gelu, 1)
                    for b in range(2):
                        chain.note(V.bn_stats(stats[:, b, :], vg[:, b, :]))
                    chain.wait()
                    for b in range(2):
                        last = V.bn_aggr(mv[:, b, :], stats[:, b, :])
                        if b == 0:
                            chain.link(last)
                    last.then_inc(sgu_var, 1)
                if h == 2:
                    dve.wait_ge(sgu_root, 1)
                    chain.link(V.reciprocal(rs2, rs2))
                    for b in range(2):
                        chain.note(V.tensor_scalar(vn[:, b, :], vg[:, b, :], mv[:, b, 0:1], rs2[:, b:b + 1], ALU.subtract, ALU.mult))
                    chain.wait()
                    for gain, op in (("sgu_g", ALU.mult), ("sgu_b", ALU.add)):
                        last = V.tensor_tensor(vn[:, :, :], vn[:, :, :], col(gain, 0, 256).unsqueeze(1).to_broadcast([P, 2, 256]), op)
                        if op == ALU.mult:
                            chain.link(last)
                    last.then_inc(sgu_normed, 1)

            def fill_late(h):
                if h == 1:
                    dve.wait_ge(mem_hi, 1)
                    V.tensor_tensor(ML[:, :, :], mem_raw, MH[:, :, :].bitcast(F32), ALU.subtract).then_inc(mem_lo, 1)
                if 3 <= h < HEADS - 1:
                    for c in range(2 * (h - 3), 2 * (h - 3) + 2):
                        n, t = CHUNK["mk"] + c, TILE["mk"] + c
                        wait_chunk(dve, n)
                        freed(V.tensor_copy(KTm[:, c, :], acc(t)[:, 0:S]), t)
                if h == HEADS - 1:
                    t = TILE["sgu_mix"]
                    dve.wait_ge(sgu_mixed, 1)
                    freed(V.tensor_tensor(vg[:, :, :].rearrange("p j (n t) -> p j n t", n=2),
                                          acc(t)[:, :].rearrange("p (j n t) -> p j n t", j=2, n=2),
                                          sbias.unsqueeze(2).to_broadcast([P, 2, 2, P]), ALU.add), t)
                    wait_evacuated(dve, t)
                    dve.wait_ge(sgu_gelu, 2)
                    V.tensor_tensor(vg[:, :, :], vg[:, :, :], uT[:, :, :], ALU.mult).then_inc(sgu_gated, 1)
                    dve.wait_ge(pool_mixed, 1)
                    for r in range(2):
                        t, rows = TILE["pool_mix"] + r, slice(r * HD, (r + 1) * HD)
                        for j in range(2):
                            last = V.tensor_scalar(t512[rows, j * S:(j + 1) * S], acc(t)[rows, j * S:(j + 1) * S],
                                                   col("pool_scale", j)[rows], None, ALU.mult)
                            if j == 0:
                                chain.note(last)
                        chain.wait()
                        freed(last, t)

            dve.wait_ge(bias_loaded, 16)
            for h in range(HEADS):
                n = CHUNK["sgu_v"] + 2 * h
                dve.wait_ge(scores, h + 1)
                if h:
                    dve.wait_ge(turned, h)
                chain.note(V.tensor_tensor(Sx[:, 0:S].rearrange("p (r s) -> p r s", r=2), SC[:, 0:S].rearrange("p (r s) -> p r s", r=2),
                                           bias[:, h, 127::-1].unsqueeze(1).to_broadcast([P, 2, P]), ALU.add))
                chain.link(V.tensor_tensor(Sx[:, S:768].rearrange("p (r s) -> p r s", r=2), SC[:, 512:1024].rearrange("p (r s) -> p r s", r=2),
                                           bias[:, h, 255::-1].unsqueeze(1).to_broadcast([P, 2, S]), ALU.add))
                chain.note(V.tensor_reduce(mx4[:, 0:2], Sx[:, 0:S].rearrange("p (r s) -> p r s", r=2), AX.X, ALU.max, negate=True))
                last = V.tensor_reduce(mx4[:, 2:4], Sx[:, S:768].rearrange("p (r s) -> p r s", r=2), AX.X, ALU.max, negate=True)
                chain.wait()
                last.then_inc(max_ready, 1)
                if h == 0:
                    compressed_scores()
                if h < HEADS - 1 and h != GELU_HEAD + 1:
                    ahead(n)
                if h:
                    fill_dve(h - 1)
                dve.wait_ge(exped, h + 1)
                chain.link(V.reciprocal(rc4, sm4))
                hh = 4 * (h % 2) + h // 2
                chain.link(V.tensor_tensor(rc4.rearrange("p (b r) -> p b r", b=2), rc4.rearrange("p (b r) -> p b r", b=2),
                                           gtok[:, :, 3 * hh + 1:3 * hh + 3], ALU.mult))
                for b in range(4):
                    a, w = (P * b, P) if b < 2 else (S * (b - 1), S)
                    last = V.tensor_scalar(Sx[:, a:a + w], Sx[:, a:a + w], rc4[:, b:b + 1], None, ALU.mult)
                    if b < 3:
                        chain.note(last)
                chain.wait()
                last.then_inc(probs, 1)
                if h == 0:
                    compressed_probs()
                if h == GELU_HEAD + 1:
                    ahead(n)
                if h < HEADS - 1:
                    ahead(n + 1)
                if h >= 2 and h % 2 == 0:
                    out_lo(h // 2 - 1)
                fill_late(h)
            for j in range(2):
                dve.wait_ge(mix_hi, 1 + j)
                V.tensor_tensor(a_lo(4 + j), t512[:, j * S:(j + 1) * S], a_hi(4 + j).bitcast(F32), ALU.subtract).then_inc(mix_lo, 1)
            for j in range(2):
                dve.wait_ge(mix_hi, 3 + j)
                V.tensor_tensor(a_lo(6 + j), vg[:, j, :], a_hi(6 + j).bitcast(F32), ALU.subtract).then_inc(mix_lo, 1)
            out_lo(3)
            for m in range(KT):
                ahead(CHUNK["w_out"] + m)
            ahead(CHUNK["mv"])
            post_norm(NORM_MIX, 0, "g_mem_pre", META, lambda: ahead(CHUNK["mv"] + 1))
            for c in range(2, 4):
                ahead(CHUNK["mv"] + c)
            reciprocal_root(NORM_X1, META)

            def m_maximum(h):
                dve.wait_ge(m_scores, h + 1)
                V.tensor_reduce(small[:, 16 + 2 * h:18 + 2 * h], SC[:, (h % 2) * 512:(h % 2) * 512 + 512].rearrange("p (b m) -> p b m", b=2),
                                AX.X, ALU.max, negate=True).then_inc(m_max, 1)

            def m_normalise(h):
                dve.wait_ge(m_exped, h + 1)
                chain.link(V.reciprocal(small[:, 32 + 2 * h:34 + 2 * h], small[:, 24 + 2 * h:26 + 2 * h]))
                for b in range(2):
                    last = V.tensor_scalar(Em[:, h % 2, b, :], Em[:, h % 2, b, :], small[:, 32 + 2 * h + b:33 + 2 * h + b], None, ALU.mult)
                    if b == 0:
                        chain.link(last)
                last.then_inc(m_probs, 1)

            def m_lo(h):
                dve.wait_ge(act_hi, ACT_MEM + h + 1)
                V.tensor_tensor(AL[:, 2 * h * S:(2 * h + 2) * S], OB[h % 2][:, :], AH[:, 2 * h * S:(2 * h + 2) * S].bitcast(F32),
                                ALU.subtract).then_inc(act_lo, 1)

            for m in range(KT):
                n, t = CHUNK["mq"] + m, TILE["mq"] + m
                wait_chunk(dve, n)
                freed(V.scalar_tensor_tensor(out=qM[:, m, :], in0=acc(t)[:, 0:S], scalar=(D // MEM_HEADS) ** -0.5, in1=rstd[:, META:T],
                                             op0=ALU.mult, op1=ALU.mult), t)
                ahead(n)
                if m in (3, 5):
                    m_maximum((m - 3) // 2)
                if m in (4, 6):
                    m_normalise((m - 4) // 2)
            m_maximum(2)
            m_normalise(2)
            m_lo(0)
            ahead(CHUNK["mv2"])
            m_maximum(3)
            m_normalise(3)
            m_lo(1)
            for c in range(1, 4):
                ahead(CHUNK["mv2"] + c)
            m_lo(2)
            m_lo(3)
            for m in range(KT):
                ahead(CHUNK["mo"] + m)
            post_norm(NORM_MEMOUT, 1, "g_ffn_pre", META)
            reciprocal_root(NORM_X2, META)
            taps = col("ffn_conv", 0, 176).rearrange("p (a b) -> p a b", b=8)

            def ffn_dve(p, i, first=False):
                for v in range(2):
                    n, t = CHUNK["up"] + 2 * p + v, TILE["up"] + 2 * p + v
                    wait_chunk(dve, n, i)
                    if not first:
                        dve.wait_ge(u_tapped, 2 * p + v - 1 + 4 * i)
                    freed(V.tensor_tensor(Ut[:, v, :], acc(t)[:, 0:S], rstd[:, META:T], ALU.mult), t)
                    if v:
                        ffn_taps(p, 0, i)
                    elif not first:
                        ffn_taps(p - 1, 1, i)
                    ahead(n, i)

            def ffn_taps(p, v, i):
                dst = (Gt, Vt)[v][:, p % 2, :]
                dve.wait_ge(f_init, 2 * p + v + 1 + 4 * i)
                chain.link(V.scalar_tensor_tensor(out=dst[:, 1:S], in0=Ut[:, v, 0:S - 1], scalar=taps[:, span(p + 2 * i, 1), 4 * v + 1],
                                                  in1=dst[:, 1:S], op0=ALU.mult, op1=ALU.add))
                V.scalar_tensor_tensor(out=dst[:, 2:S], in0=Ut[:, v, 0:S - 2], scalar=taps[:, span(p + 2 * i, 1), 4 * v],
                                       in1=dst[:, 2:S], op0=ALU.mult, op1=ALU.add).then_inc(u_tapped, 1)

            ffn_dve(0, 0, first=True)
            with dve.Fori(0, 8) as i:
                chain.begin_round(i, 4)
                for p in (1, 2):
                    ffn_dve(p, i)
            chain.end_rounds(8, 4)
            for p in range(17, FFN_TILES):
                ffn_dve(p, 0)
            ffn_taps(FFN_TILES - 1, 1, 0)
            for c in range(24):
                ahead(CHUNK["down"] + c)
            post_norm(NORM_FFN, 2, "g_conv", 0)
            reciprocal_root(NORM_H0, 0)
            V.tensor_tensor(rstd2, rstd[:, :], rstd[:, :], ALU.mult).then_inc(squared_rstd, 1)
            ctaps = col("conv_taps", 0, 48).rearrange("p (a b) -> p a b", b=3)
            chain.link(V.memset(CX[:, 0:2], 0.0))
            base_hi = ACT_CONV

            def conv_dve(i):
                n, t = CHUNK["conv_in"], TILE["conv_in"]
                wait_chunk(dve, n, i)
                freed(V.tensor_tensor(cT, acc(t)[:, 0:T], rstd2, ALU.mult), t)
                ahead(n, i)
                wait_chunk(dve, n + 1, i)
                wait_evacuated(dve, t, i)
                freed(V.tensor_tensor(CX[:, 2:T + 2], acc(t + 1)[:, 0:T], cT, ALU.mult), t + 1)
                wait_evacuated(dve, t + 1, i)
                chain.link(V.tensor_scalar(Yc, CX[:, 2:T + 2], ctaps[:, span(i, 1), 2], None, ALU.mult))
                chain.link(V.scalar_tensor_tensor(out=Yc, in0=CX[:, 1:T + 1], scalar=ctaps[:, span(i, 1), 1], in1=Yc, op0=ALU.mult, op1=ALU.add))
                V.scalar_tensor_tensor(out=Yc, in0=CX[:, 0:T], scalar=ctaps[:, span(i, 1), 0], in1=Yc, op0=ALU.mult, op1=ALU.add).then_inc(c_conv, 1)
                ahead(n + 1, i)
                wait_chunk(dve, n + 2, i)
                freed(V.tensor_tensor(ZZ, acc(t + 2)[:, 0:T], rstd[:, :], ALU.mult), t + 2)
                ahead(n + 2, i)
                dve.wait_ge(c_sig, 1 + i)
                chain.link(V.tensor_tensor(ZZ, ZZ, SZ, ALU.mult))
                dve.wait_ge(c_scaled, 1 + i)
                chain.link(V.tensor_tensor(Yc, Yc, ZZ, ALU.mult))
                wait_chunk(dve, n + 3, i)
                freed(V.tensor_tensor(Fc, acc(t + 3)[:, 0:T], Yc, ALU.mult), t + 3)
                ahead(n + 3, i)
                dve.wait_ge(act_hi, base_hi + 1 + i)
                V.tensor_tensor(a_lo(i, T), Fc, a_hi(i, T).bitcast(F32), ALU.subtract).then_inc(act_lo, 1)

            dve.wait_ge(squared_rstd, 1)
            with dve.Fori(0, E_TILES) as i:
                chain.begin_round(i, 4)
                conv_dve(i)
            chain.end_rounds(E_TILES, 4)
            for m in range(KT):
                n, t = CHUNK["conv_out"] + 2 * m, TILE["conv_out"] + m
                ahead(n)
                wait_chunk(dve, n + 1)
                freed(V.tensor_tensor(XR[:, m, :], acc(t)[:, 0:T], XR[:, m, :], ALU.add), t)
                ahead(n + 1)
                raw_rest(RAW_H1, "g_mlstm", 0, m)
            reciprocal_root(NORM_H1, 0)

            def lk_tiles(first, end):
                for m in range(first, end):
                    n, t = CHUNK["lk"] + m, TILE["lk"] + m
                    wait_chunk(dve, n)
                    freed(V.tensor_tensor(lk[:, m, :], acc(t)[:, 0:T], rstd[:, :], ALU.mult), t)
                    apply_norm(PRE_H1, "g_mlstm", 0, l_in(AH, 0), l_in(AL, 0), m)
                    ahead(n)

            n, t = CHUNK["lgates"], TILE["lgates"]
            wait_chunk(dve, n)
            freed(V.tensor_tensor(gx[0:36, :], acc(t)[0:36, 0:T], rstd[0:36, :], ALU.mult), t)
            ahead(n)
            lk_tiles(0, KT)
            apply_norm(PRE_H1, "g_mlstm", 0, l_in(AH, 0), l_in(AL, 0), KT)
            for m in range(KT):
                n, t = CHUNK["lq"] + m, TILE["lq"] + m
                wait_chunk(dve, n)
                freed(V.tensor_scalar(lq[:, m, :], acc(t)[:, 0:S], S ** -0.5, None, ALU.mult), t)
                ahead(n)
                if m == 2:
                    chain.note(V.memset(gone[0:LHEADS, :], 1.0))
                    dve.wait_ge(g_raw, 1)
                    chain.note(V.tensor_scalar(lf[32:36, :], gx[32:36, :], 0.0, None, ALU.min))
                    chain.wait()
                    dve.wait_ge(g_ln, 1)
                    chain.link(V.tensor_tensor(lf[0:LHEADS, :], lf[32:36, :], gl[32:36, :], ALU.subtract))
                if m == 3:
                    chain.link(V.tensor_tensor_scan(gF[0:LHEADS, :], gone[0:LHEADS, :], lf[0:LHEADS, :], 0.0, ALU.mult, ALU.add))
                    V.tensor_tensor(gA[0:LHEADS, :], gx[0:LHEADS, :], gF[0:LHEADS, :], ALU.subtract).then_inc(g_rows, 1)
                    dve.wait_ge(g_rows, 1)
                    chain.link(V.tensor_tensor_scan(gM[0:LHEADS, :], gone[0:LHEADS, :], gA[0:LHEADS, :], 0.0, ALU.mult, ALU.max))
                if m == 4:
                    V.tensor_scalar(negM, gM[0:LHEADS, :], -1.0, None, ALU.mult).then_inc(g_rows, 1)
                    dve.wait_ge(g_rows, 2)
                    V.tensor_tensor(negFM, negM, gF[0:LHEADS, :], ALU.subtract).then_inc(g_rows, 1)
                if m == 6:
                    dve.wait_ge(g_turned, 1)
                    chain.note(V.tensor_copy(acol[0:META, 0, :], OB[0][0:META, 0:4]))
                    last = V.tensor_copy(acol[:, 1:3, :], OB[0][:, 4:12].rearrange("p (a b) -> p a b", a=2))
                    chain.wait()
                    last.then_inc(g_cols, 1)

            def l_weights(h):
                dve.wait_ge(l_scores, h + 1)
                dve.wait_ge(l_masked, 2 * h + 2)
                V.tensor_tensor(Pl[:, 0:S], SC[:, 0:S], Dl[:, 0:S], ALU.mult).then_inc(l_probs, 1)
                V.tensor_tensor(Pl[:, S:S + P], SC[:, S:S + P], Dl[:, S:S + P], ALU.mult).then_inc(l_probs, 1)
                V.tensor_tensor(Pl[0:META, 384:640], SC[0:META, 512:512 + S], Dl[0:META, 384:640], ALU.mult).then_inc(l_probs, 1)

            def v_copy(m):
                dve.wait_ge(l_vturned, m + 1)
                o = OB[m % 2]
                c = slice(m * P, (m + 1) * P)
                chain.note(V.tensor_copy(lv[0:META, 2, c], o[0:META, 2 * P:3 * P]))
                last = V.tensor_copy(lv[:, 0:2, c], o[:, 0:2 * P].rearrange("p (a b) -> p a b", a=2))
                chain.wait()
                last.then_inc(l_vcopied, 1)

            for m in range(E_TILES):
                ahead(CHUNK["lv"] + m)
                if m >= 2:
                    v_copy(m - 2)
                if m == 6:
                    l_weights(0)
            v_copy(E_TILES - 2)
            v_copy(E_TILES - 1)
            base_hi = ACT_LSTM

            def l_lo(e):
                dve.wait_ge(act_hi, base_hi + e + 1)
                V.tensor_tensor(l_out(AL, e), hn[:, e % 4, :], l_out(AH, e).bitcast(F32), ALU.subtract).then_inc(act_lo, 1)

            for h in range(LHEADS):
                n, t = CHUNK["oz"] + 8 * h, TILE["oz"] + 8 * h
                dve.wait_ge(l_num, h + 1)
                dve.wait_ge(l_decay, 2 * h + 2)
                if h:
                    dve.wait_ge(act_hi, base_hi + 4 * h)
                chain.link(V.scalar_tensor_tensor(out=rden, in0=PTB[:, 512:512 + S], scalar=-1.0, in1=em, op0=ALU.mult, op1=ALU.max))
                chain.link(V.tensor_tensor(rden, PTB[:, 512:512 + S], rden, ALU.max))
                chain.link(V.reciprocal(rden, rden))
                for v in range(2):
                    last = V.tensor_tensor(hn[:, 2 * v:2 * v + 2, :], OB[v][:, :].rearrange("p (a b) -> p a b", a=2),
                                           rden.unsqueeze(1).to_broadcast([P, 2, S]), ALU.mult)
                    if v == 0:
                        chain.link(last)
                last.then_inc(l_hn, 1)
                for m in range(2):
                    ahead(n + m)
                if h + 1 < LHEADS:
                    l_weights(h + 1)
                dve.wait_ge(l_root, h + 1)
                chain.link(V.reciprocal(rhead, lroot))
                chain.link(V.tensor_tensor(hn[:, :, :], hn[:, :, :], rhead.unsqueeze(1).to_broadcast([P, 4, S]), ALU.mult))
                for m in range(2, 4):
                    ahead(n + m)
                for m in range(4):
                    e = 4 * h + m
                    ahead(n + 4 + m)
                    wait_evacuated(dve, t + m)
                    chain.link(V.scalar_tensor_tensor(out=hn[:, m, :], in0=hn[:, m, :], scalar=col("head_norm", e), in1=so[:, m, :],
                                                      op0=ALU.mult, op1=ALU.mult))
                    dve.wait_ge(z_sig, e + 1)
                    chain.link(V.tensor_tensor(hn[:, m, :], hn[:, m, :], tz[:, m % 2, :], ALU.mult))
                    freed(V.tensor_tensor(hn[:, m, :], acc(t + 4 + m)[:, 0:S], hn[:, m, :], ALU.mult), t + 4 + m)
                    if m:
                        l_lo(e - 1)
                l_lo(4 * h + 3)
            for m in range(KT):
                n, t = CHUNK["lout"] + 2 * m, TILE["lout"] + m
                ahead(n)
                ahead(n + 1)
                wait_chunk(dve, n + 1)
                freed(V.tensor_tensor(XR[:, m, META:T], acc(t)[:, 0:S], XR[:, m, META:T], ALU.add), t)
            reciprocal_root(NORM_FINAL, META)
            for k in range(KT):
                V.scalar_tensor_tensor(out=SQ[:, k, META:T], in0=XR[:, k, META:T], scalar=col("g_final", k), in1=rstd[:, META:T],
                                       op0=ALU.mult, op1=ALU.mult).then_inc(normed, 1)


def _tiles(np, w, cols):
    k = w.shape[0] // P
    return w[:, cols].reshape(k, P, len(cols)).transpose(1, 0, 2).reshape(P, -1)


def _pack_weights(np, a):
    ar = np.arange

    def lin(w):
        return [_tiles(np, w, ar(m * P, (m + 1) * P)) for m in range(w.shape[1] // P)]

    def pad(c):
        return np.concatenate([c, np.zeros((P, D - c.shape[1]), c.dtype)], axis=1)

    def narrow(w, at):
        out = np.zeros((D, P), w.dtype)
        out[:, at] = w
        return _tiles(np, out, ar(P))

    def deep(w):
        rows = [w[r:r + D] for r in range(0, w.shape[0], D)]
        return [pad(_tiles(np, r, ar(m * P, (m + 1) * P))) for m in range(KT) for r in rows]

    w = a["w_in"][0]
    q, kc, vc, ks, vs, kw, vw, gt, pin, u, v = np.split(w, np.cumsum([512] + [128] * 6 + [24, 256, 256]), axis=1)
    pairs = [np.concatenate([ar(j * HD, (j + 1) * HD), ar((j + 4) * HD, (j + 5) * HD)]) for j in range(4)]

    def pairs_of(name, tiles):
        return [tiles[m ^ 1 if (CHUNK[name] + m - m % 2) % SLOTS == SLOTS - 1 else m] for m in range(len(tiles))]

    parts = lin(kc) + lin(vc) + lin(vs) + lin(vw) + lin(ks) + lin(kw)
    for r in (0, D):
        parts += [_tiles(np, a["cmp_w1"][0, kv].reshape(2048, P)[r:r + D], ar(P)) for kv in range(2)]
    parts += [_tiles(np, q, p) for p in pairs] + [narrow(gt, ar(24))] + pairs_of("sgu_v", lin(v)) + lin(u) + lin(pin)
    rows = np.concatenate(pairs + [ar(512, 1024)])
    mv = lin(a["w_mv"][0])
    parts += lin(a["w_mk"][0]) + lin(a["w_out"][0][rows]) + pairs_of("mv", mv[0:4]) + lin(a["w_mq"][0]) + pairs_of("mv2", mv[4:8])
    parts += lin(a["w_mo"][0])
    up = a["w_up"][0]
    for j in range(FFN_TILES):
        parts += [_tiles(np, up, ar(c, c + P)) for c in (j * P, (FFN_TILES + j) * P)]
    parts += deep(a["w_down"][0])
    cin = a["conv_in_w_2"][0]
    for e in range(E_TILES):
        for part in (1, 2, 3, 0):
            parts.append(_tiles(np, cin, ar(part * 2048 + e * P, part * 2048 + (e + 1) * P)))
    parts += deep(a["conv_out_w_2"][0])
    lq, lk, lv, lo, lz, lg = np.split(a["mlstm_in_w_2"][0], [1024, 2048, 4096, 6144, 8192], axis=1)
    parts += [narrow(lg, np.concatenate([ar(4), ar(32, 36)]))] + lin(lk) + lin(lq) + lin(lv)
    o, z = lin(lo), lin(lz)
    for h in range(LHEADS):
        parts += o[4 * h:4 * h + 4] + z[4 * h:4 * h + 4]
    parts += deep(a["mlstm_out_w_2"][0])
    out = np.stack(parts)
    assert out.shape == (NCHUNKS, P, D)
    return out


def _pack_params(np, a):
    def cols(v):
        return v.reshape(-1, P).T

    def rows(v):
        return np.broadcast_to(v[None, :], (P, v.shape[0]))

    f = {}
    for name, key in (("g_mix_pre", "mix_norm_pre"), ("g_mix_post", "mix_norm_post"), ("g_mem_pre", "mem_norm_pre"),
                      ("g_mem_kv", "mem_norm_kv"), ("g_mem_post", "mem_norm_post"), ("g_ffn_pre", "ffn_norm_pre"),
                      ("g_ffn_post", "ffn_norm_post"), ("pool_scale", "pool_scale"), ("cmp_b1", "cmp_b1")):
        f[name] = cols(a[key][0])
    f["g_conv"], f["g_mlstm"] = cols(a["norm_w_2"][0]), cols(a["norm_w_2"][1])
    f["g_final"] = cols(a["final_norm_w_2"])
    f["cmp_b2k"] = np.concatenate([a["cmp_b2"][0, 0]] * 2)[:, None]
    f["cmp_b2v"] = rows(a["cmp_b2"][0, 1])
    f["cmp_pos"] = a["cmp_pos"][0].reshape(2, 16, P).transpose(2, 0, 1).reshape(P, 32)
    f["cmp_w2"] = a["cmp_w2"][0].transpose(1, 0, 2).reshape(P, 128)
    f["sgu_g"], f["sgu_b"] = rows(a["sgu_norm_g"][0]), rows(a["sgu_norm_b"][0])
    sb = a["sgu_b"][0]
    f["sgu_bias"] = np.concatenate([np.repeat(sb[2 * j:2 * j + 2], HD, axis=0) for j in range(2)], axis=1)
    f["sgu_w"] = a["sgu_w"][0].transpose(2, 0, 1).reshape(P, 512)
    pw = a["pool_w"][0]
    f["pool_w"] = np.concatenate([pw[0:2].reshape(P, HD), pw[2:4].reshape(P, HD)], axis=1)
    tokens = np.arange(S)
    inv = [1.0 / np.minimum(tokens + 1, w) for w in (2, 4, 8, 16)]
    f["pool_inv"] = np.concatenate([np.repeat(np.stack(inv[2 * j:2 * j + 2]), HD, axis=0) for j in range(2)], axis=1).astype(np.float32)
    cw, cbias = a["conv_w"][0], a["conv_b"][0]
    four = np.concatenate([cw, cbias[None]], axis=0).reshape(4, 2, FFN_TILES, P)
    f["ffn_conv"] = four.transpose(3, 2, 1, 0).reshape(P, 176)
    f["conv_taps"] = a["conv_w_2"][0].reshape(3, E_TILES, P).transpose(2, 1, 0).reshape(P, 48)
    f["head_norm"] = cols(a["mlstm_head_norm_w_2"][0])
    gb = np.zeros((P, 1), np.float32)
    gb[0:4, 0], gb[32:36, 0] = a["mlstm_gate_b_2"][0][0:4], a["mlstm_gate_b_2"][0][4:8]
    f["gate_b"] = gb
    return np.concatenate([f[name] for name, _ in _COLS], axis=1)


def _onehot(np):
    import math
    d = np.arange(512) - 256
    n = np.maximum(d, 1).astype(np.float32)
    large = 16 + (np.log(n / np.float32(16)) / np.float32(math.log(64.0)) * np.float32(16)).astype(np.int32)
    bucket = np.where(d < 16, d, np.minimum(large, 31))
    bucket = np.where(d < 0, 32, bucket)
    return (np.arange(33)[:, None] == bucket[None, :]).astype(np.float32)


def kernel(**inputs):
    import numpy as np
    import concourse.bacc as bacc
    from concourse.bass_utils import run_bass_kernel_spmd as run

    a = {k: np.asarray(v) for k, v in inputs.items()}
    order = [j + 4 * g for j in range(4) for g in range(2)]

    def feature_major(v):
        return v.T.reshape(KT, P, -1).transpose(1, 0, 2)

    arrays = {
        "weights": _pack_weights(np, a),
        "x_t": feature_major(a["x"][0]),
        "mem_t": feature_major(a["mem"][0]),
        "meta_t": feature_major(a["meta_tokens_2"]),
        "params": _pack_params(np, a),
        "rel_bias": a["rel_bias"][:, order],
        "onehot": _onehot(np),
    }
    arrays = {k: np.ascontiguousarray(v) for k, v in arrays.items()}
    nc = bacc.Bacc("TRN2", target_bir_lowering=False, num_devices=1)
    args = [nc.dram_tensor(k, v.shape, F32, kind="ExternalInput").ap() for k, v in arrays.items()]
    out = nc.dram_tensor("out_t", (D, S), F32, kind="ExternalOutput").ap()
    bias_rows = nc.dram_tensor("bias_rows", (HEADS, 512), F32, kind="Internal").ap()
    build(nc, *args, out, bias_rows)
    r = run(nc, [arrays], core_ids=[0])
    return np.ascontiguousarray(r.results[0]["out_t"].T)[None]
```
